# Optimizing a Trainium2 kernel written in Bass

```python
import math
import jax, jax.numpy as jnp
from jax import lax
import numpy as np

'''One layer of a bidirectional hybrid encoder trunk (Hymba-style parallel head groups).

Inputs : x (BATCH, SEQ, D_MODEL) float32 plus learned parameters (leading DEPTH axis on per-layer ones).
Output : (BATCH, SEQ, D_MODEL) float32.

Residual stream = [16 learned meta tokens ; SEQ tokens]  (length SEQ + 16, meta at positions 0..15).
Per layer:
  u = RMSNorm(h); ONE combined projection u @ w_in, columns partitioned into
    group A: windowed GQA with learned per-head sink logit (8 q heads, 2 kv heads, head dim 64)
    group B: differential attention (8 heads, q/k halves of dim 32, value dim 64, learned lambda)
  both groups use per-head QK RMSNorm then rotary (theta 1e4, full head dim)
  outputs concatenated over head groups -> ONE output projection -> residual add
  v = RMSNorm(h); top-4-of-32 gpt-oss style routed clamped-SwiGLU experts -> residual add
Meta tokens are dropped from the returned sequence.
'''

D_MODEL = 1024
BATCH = 1
SEQ = 1024
DEPTH = 1

N_META = 16
BLK = 128
WINDOW = 128
ROPE_THETA = 10000.0
EPS = 1e-6
NEG_INF = -1e30

SWA_HQ = 8
SWA_HKV = 2
SWA_G = SWA_HQ // SWA_HKV
SWA_DH = 64

DIFF_H = 8
DIFF_DQ = 32
DIFF_DV = 2 * DIFF_DQ

IN_WIDTHS = (SWA_HQ * SWA_DH, SWA_HKV * SWA_DH, SWA_HKV * SWA_DH,
             DIFF_H * 2 * DIFF_DQ, DIFF_H * 2 * DIFF_DQ, DIFF_H * DIFF_DV)
IN_WIDTH = 2304
MIX_WIDTH = SWA_HQ * SWA_DH + DIFF_H * DIFF_DV

N_EXPERTS = 32
TOP_K = 4
D_FF = D_MODEL
SWIGLU_LIMIT = 7.0
SWIGLU_ALPHA = 1.702
MOE_BLK = 128

kernel_name = "hymba_swa_sink_diffattn_gptoss_moe"

def _rmsnorm(x, g, eps=EPS):
    xf = x.astype(jnp.float32)
    y = xf * lax.rsqrt(jnp.mean(xf * xf, axis=-1, keepdims=True) + eps)
    return (y * g.astype(jnp.float32)).astype(x.dtype)

def _rope(x, pos):
    d = x.shape[-1]
    inv = ROPE_THETA ** (-jnp.arange(0, d, 2, dtype=jnp.float32) / d)
    ang = pos.astype(jnp.float32)[:, None] * inv[None, :]
    cos = jnp.cos(ang)[None, :, None, :]
    sin = jnp.sin(ang)[None, :, None, :]
    xf = x.astype(jnp.float32)
    x1, x2 = xf[..., : d // 2], xf[..., d // 2:]
    out = jnp.concatenate([x1 * cos - x2 * sin, x2 * cos + x1 * sin], axis=-1)
    return out.astype(x.dtype)

def _band(t):
    pad = [(0, 0)] * t.ndim
    pad[1] = (1, 1)
    tp = jnp.pad(t, pad)
    return jnp.concatenate([tp[:, :-2], tp[:, 1:-1], tp[:, 2:]], axis=2)

def _swa_sink_attention(q, k, v, sink, pos):
    B, L = q.shape[0], q.shape[1]
    P = BLK - N_META
    nb = (L + P) // BLK
    front = ((0, 0), (P, 0), (0, 0), (0, 0))
    qb = jnp.pad(q, front).reshape(B, nb, BLK, SWA_HKV, SWA_G, SWA_DH)
    kb = jnp.pad(k, front).reshape(B, nb, BLK, SWA_HKV, SWA_DH)
    vb = jnp.pad(v, front).reshape(B, nb, BLK, SWA_HKV, SWA_DH)
    k_band, v_band = _band(kb), _band(vb)
    k_meta, v_meta = k[:, :N_META], v[:, :N_META]
    pb = jnp.concatenate([jnp.full((P,), -1, jnp.int32), pos]).reshape(nb, BLK)
    pbp = jnp.pad(pb, ((1, 1), (0, 0)), constant_values=-1)
    p_band = jnp.concatenate([pbp[:-2], pbp[1:-1], pbp[2:]], axis=1)
    band_ok = (p_band[:, None, :] >= N_META) & (jnp.abs(pb[:, :, None] - p_band[:, None, :]) <= WINDOW)
    scale = SWA_DH ** -0.5
    s_meta = jnp.einsum('bnqhgd,bkhd->bnhgqk', qb, k_meta, preferred_element_type=jnp.float32) * scale
    s_band = jnp.einsum('bnqhgd,bnkhd->bnhgqk', qb, k_band, preferred_element_type=jnp.float32) * scale
    s_band = jnp.where(band_ok[None, :, None, None], s_band, NEG_INF)
    s_sink = jnp.broadcast_to(sink.astype(jnp.float32).reshape(1, 1, SWA_HKV, SWA_G, 1, 1),
                              s_meta.shape[:-1] + (1,))
    probs = jax.nn.softmax(jnp.concatenate([s_meta, s_band, s_sink], axis=-1), axis=-1).astype(v.dtype)
    o = (jnp.einsum('bnhgqk,bkhd->bnqhgd', probs[..., :N_META], v_meta)
         + jnp.einsum('bnhgqk,bnkhd->bnqhgd', probs[..., N_META:N_META + 3 * BLK], v_band))
    return o.reshape(B, nb * BLK, SWA_HQ * SWA_DH)[:, P:]

def _diff_attention(q1, q2, k1, k2, v, lam):
    B, L = q1.shape[0], q1.shape[1]
    nq = -(-L // BLK)
    pad_q = ((0, 0), (0, nq * BLK - L), (0, 0), (0, 0))

    def to_blocks(t):
        return jnp.moveaxis(jnp.pad(t, pad_q).reshape(B, nq, BLK, DIFF_H, DIFF_DQ), 1, 0)

    scale = DIFF_DQ ** -0.5

    def one_block(qs):
        a, b = qs
        p1 = jax.nn.softmax(jnp.einsum('bqhd,bkhd->bhqk', a, k1, preferred_element_type=jnp.float32) * scale, axis=-1)
        p2 = jax.nn.softmax(jnp.einsum('bqhd,bkhd->bhqk', b, k2, preferred_element_type=jnp.float32) * scale, axis=-1)
        return jnp.einsum('bhqk,bkhd->bqhd', (p1 - lam * p2).astype(v.dtype), v)

    o = lax.map(one_block, (to_blocks(q1), to_blocks(q2)))
    return jnp.moveaxis(o, 0, 1).reshape(B, nq * BLK, DIFF_H, DIFF_DV)[:, :L]

def _clamped_swiglu(a):
    glu, lin = a[..., :D_FF], a[..., D_FF:]
    glu = jnp.minimum(glu, SWIGLU_LIMIT)
    lin = jnp.clip(lin, -SWIGLU_LIMIT, SWIGLU_LIMIT)
    return glu * jax.nn.sigmoid(SWIGLU_ALPHA * glu) * (lin + 1.0)

def _moe(h, w_router, b_router, w_mlp1, b_mlp1, w_mlp2, b_mlp2):
    T, D = h.shape
    logits = (h @ w_router + b_router).astype(jnp.float32)
    top_val, top_idx = lax.top_k(logits, TOP_K)
    gates = jax.nn.softmax(top_val, axis=-1)
    A = T * TOP_K
    flat_e = top_idx.reshape(A)
    flat_tok = jnp.arange(A, dtype=jnp.int32) // TOP_K
    flat_gate = gates.reshape(A)
    order = jnp.argsort(flat_e)
    e_sorted = flat_e[order]
    counts = jnp.bincount(flat_e, length=N_EXPERTS).astype(jnp.int32)
    padded = (counts + MOE_BLK - 1) // MOE_BLK * MOE_BLK
    pad_end = jnp.cumsum(padded)
    pad_start = pad_end - padded
    start = jnp.cumsum(counts) - counts
    dest = pad_start[e_sorted] + (jnp.arange(A, dtype=jnp.int32) - start[e_sorted])
    n_blocks = -(-A // MOE_BLK) + N_EXPERTS
    n_slots = n_blocks * MOE_BLK
    slot_tok = jnp.full((n_slots,), T, jnp.int32).at[dest].set(flat_tok[order])
    slot_gate = jnp.zeros((n_slots,), jnp.float32).at[dest].set(flat_gate[order])
    block_start = jnp.arange(n_blocks, dtype=jnp.int32) * MOE_BLK
    block_expert = jnp.minimum(jnp.searchsorted(pad_end, block_start, side='right'), N_EXPERTS - 1)
    h_ext = jnp.concatenate([h, jnp.zeros((1, D), h.dtype)], axis=0)
    xs = h_ext[slot_tok].reshape(n_blocks, MOE_BLK, D)

    def expert_block(args):
        xb, e = args
        a = xb @ w_mlp1[e] + b_mlp1[e]
        return _clamped_swiglu(a) @ w_mlp2[e] + b_mlp2[e]

    ys = lax.map(expert_block, (xs, block_expert)).reshape(n_slots, D)
    ys = ys * slot_gate[:, None].astype(ys.dtype)
    return jax.ops.segment_sum(ys, slot_tok, num_segments=T + 1)[:T]

def setup_inputs(seed: int = 0) -> dict:
    key = jax.random.key(seed)
    ks = jax.random.split(key, 24)
    f32 = jnp.float32

    def nrm(k, shape, s):
        return jax.random.normal(k, shape, f32) * s

    def gain(k, shape):
        return 1.0 + 0.05 * jax.random.normal(k, shape, f32)

    return {
        "x": nrm(ks[0], (BATCH, SEQ, D_MODEL), 1.0),
        "meta_tokens": nrm(ks[1], (N_META, D_MODEL), 1.0),
        "g_attn": gain(ks[2], (DEPTH, D_MODEL)),
        "w_in": nrm(ks[3], (DEPTH, D_MODEL, IN_WIDTH), D_MODEL ** -0.5),
        "g_q_swa": gain(ks[4], (DEPTH, SWA_DH)),
        "g_k_swa": gain(ks[5], (DEPTH, SWA_DH)),
        "g_q_diff": gain(ks[6], (DEPTH, DIFF_DQ)),
        "g_k_diff": gain(ks[7], (DEPTH, DIFF_DQ)),
        "sink_swa": nrm(ks[8], (DEPTH, SWA_HQ), 0.5),
        "lambda_q1": nrm(ks[9], (DEPTH, DIFF_DQ), 0.1),
        "lambda_k1": nrm(ks[10], (DEPTH, DIFF_DQ), 0.1),
        "lambda_q2": nrm(ks[11], (DEPTH, DIFF_DQ), 0.1),
        "lambda_k2": nrm(ks[12], (DEPTH, DIFF_DQ), 0.1),
        "g_diff_head": gain(ks[13], (DEPTH, DIFF_DV)),
        "w_out": nrm(ks[14], (DEPTH, MIX_WIDTH, D_MODEL), MIX_WIDTH ** -0.5),
        "g_ffn": gain(ks[15], (DEPTH, D_MODEL)),
        "w_router": nrm(ks[16], (DEPTH, D_MODEL, N_EXPERTS), D_MODEL ** -0.5),
        "b_router": nrm(ks[17], (DEPTH, N_EXPERTS), 0.01),
        "w_mlp1": nrm(ks[18], (DEPTH, N_EXPERTS, D_MODEL, 2 * D_FF), D_MODEL ** -0.5),
        "b_mlp1": nrm(ks[19], (DEPTH, N_EXPERTS, 2 * D_FF), 0.02),
        "w_mlp2": nrm(ks[20], (DEPTH, N_EXPERTS, D_FF, D_MODEL), D_FF ** -0.5),
        "b_mlp2": nrm(ks[21], (DEPTH, N_EXPERTS, D_MODEL), 0.02),
    }

def reference(x, meta_tokens, g_attn, w_in, g_q_swa, g_k_swa, g_q_diff, g_k_diff, sink_swa,
              lambda_q1, lambda_k1, lambda_q2, lambda_k2, g_diff_head, w_out, g_ffn,
              w_router, b_router, w_mlp1, b_mlp1, w_mlp2, b_mlp2):
    B = x.shape[0]
    meta = jnp.broadcast_to(meta_tokens.astype(x.dtype)[None], (B, N_META, D_MODEL))
    h = jnp.concatenate([meta, x], axis=1)
    L = h.shape[1]
    pos = jnp.arange(L, dtype=jnp.int32)
    offs = [0]
    for w in IN_WIDTHS:
        offs.append(offs[-1] + w)
    for l in range(DEPTH):
        lambda_init = 0.8 - 0.6 * math.exp(-0.3 * l)
        u = _rmsnorm(h, g_attn[l])
        proj = u @ w_in[l]
        qa, ka, va, qd, kd, vd = [proj[..., offs[i]:offs[i + 1]] for i in range(6)]
        qa = _rope(_rmsnorm(qa.reshape(B, L, SWA_HQ, SWA_DH), g_q_swa[l]), pos)
        ka = _rope(_rmsnorm(ka.reshape(B, L, SWA_HKV, SWA_DH), g_k_swa[l]), pos)
        va = va.reshape(B, L, SWA_HKV, SWA_DH)
        out_a = _swa_sink_attention(qa, ka, va, sink_swa[l], pos)

        qd = qd.reshape(B, L, DIFF_H, 2, DIFF_DQ)
        kd = kd.reshape(B, L, DIFF_H, 2, DIFF_DQ)
        q1 = _rope(_rmsnorm(qd[..., 0, :], g_q_diff[l]), pos)
        q2 = _rope(_rmsnorm(qd[..., 1, :], g_q_diff[l]), pos)
        k1 = _rope(_rmsnorm(kd[..., 0, :], g_k_diff[l]), pos)
        k2 = _rope(_rmsnorm(kd[..., 1, :], g_k_diff[l]), pos)
        vd = vd.reshape(B, L, DIFF_H, DIFF_DV)
        lam = (jnp.exp(jnp.sum(lambda_q1[l].astype(jnp.float32) * lambda_k1[l].astype(jnp.float32)))
               - jnp.exp(jnp.sum(lambda_q2[l].astype(jnp.float32) * lambda_k2[l].astype(jnp.float32)))
               + lambda_init)
        od = _diff_attention(q1, q2, k1, k2, vd, lam)
        out_b = (_rmsnorm(od, g_diff_head[l], 1e-5) * (1.0 - lambda_init)).reshape(B, L, DIFF_H * DIFF_DV)

        mixed = jnp.concatenate([out_a, out_b], axis=-1)
        h = h + mixed @ w_out[l]
        v = _rmsnorm(h, g_ffn[l]).reshape(B * L, D_MODEL)
        y = _moe(v, w_router[l], b_router[l], w_mlp1[l], b_mlp1[l], w_mlp2[l], b_mlp2[l])
        h = h + y.reshape(B, L, D_MODEL)
    return h[:, N_META:]


_drawn_inputs = setup_inputs


def setup_inputs(seed=0):
    import zlib

    import numpy as np

    out = dict(_drawn_inputs(seed))
    spreads = {}
    factors = {'g_q_swa': 5.522,
     'g_k_swa': 3.717,
     'sink_swa': 8.0,
     'lambda_q2': 3.492,
     'b_mlp1': 5.73,
     'b_mlp2': 6.584}
    for name, (base, spread) in spreads.items():
        noise = np.random.default_rng([zlib.crc32(name.encode()), seed]).standard_normal(out[name].shape)
        drawn = base * np.exp(spread * noise) if base else spread * noise
        out[name] = __import__('jax').numpy.asarray(drawn.astype(out[name].dtype))
    for name, factor in factors.items():
        out[name] = (out[name] * factor).astype(out[name].dtype)
    return out
```

```python
import math
from contextlib import ExitStack

import numpy as np

import concourse.bass as bass
from concourse import mybir

F32 = mybir.dt.float32
F32R = mybir.dt.float32r
I32 = mybir.dt.int32
U32 = mybir.dt.uint32
ALU = mybir.AluOpType
ACT = mybir.ActivationFunctionType
AX = mybir.AxisListType

P = 128
D = 1024
KC = D // P
SEQ = 1024
NT = SEQ // P
N_META = 16
KEYS = SEQ + N_META
EPS = 1e-6
EPS_HEAD = 1e-5
HQ, HKV, DH = 8, 2, 64
G = HQ // HKV
HD, DQ, DV = 8, 32, 64
LAMBDA_INIT = 0.8 - 0.6 * math.exp(0.0)
QA, KA, VA, QD, KD, VD, IN_W = 0, 512, 640, 768, 1280, 1792, 2304
R_KA, R_QD, R_KD, R_W = 512, 640, 1152, 1664
RC = R_W // P
N_EXP, TOP_K = 32, 4
LIMIT, ALPHA = 7.0, 1.702
CAP = SEQ
JOB = 2 * P
MAX_JOBS = N_EXP + SEQ * TOP_K // JOB - 1
NJ = 64
NEG = -1e30


def chained(eng, sem):
    n = [0]

    def step(ins):
        n[0] += 1
        ins.then_inc(sem, 1)
        eng.wait_ge(sem, n[0])
    return step


def project(nc, a, v_all, qk_dram):
    with ExitStack() as ctx:
        sb = lambda n, s, d=F32: ctx.enter_context(nc.sbuf_tensor(n, s, d))
        sem = lambda n: ctx.enter_context(nc.semaphore(n))
        w_sb = sb("w_in_sb", [P, KC, IN_W])
        xs = sb("xs", [P, 2, D])
        us = sb("us", [P, 2, D])
        ut = sb("ut", [P, 2, KC, P])
        g_sb = sb("g_attn_sb", [P, D])
        rope = sb("rope_sb", [P, NT + 1, 96])
        gains = sb("gains_sb", [P, 2, DH])
        gaind = sb("gaind_sb", [P, 2, DQ])
        ident = sb("ident1", [P, P])
        pr = sb("pr", [P, 2, IN_W])
        qn = sb("qn", [P, R_W])
        t1 = sb("t1", [P, R_W])
        t2 = sb("t2", [P, R_W])
        ro = sb("ro", [P, 2, R_W])
        hi = sb("qk_hi", [P, 2, RC, P], F32R)
        lo = sb("qk_lo", [P, 2, RC, P], F32R)
        ss = sb("ss1", [P, NT + 1])
        rs = sb("rs1", [P, NT + 1])
        hs = sb("hs", [P, 42])
        hr = sb("hr", [P, 42])
        eps = sb("eps1", [P, 1])
        ptu = ctx.enter_context(nc.psum_tensor("ptu", [P, 2, 512], F32))
        ptq = ctx.enter_context(nc.psum_tensor("ptq", [P, 2, 512], F32))
        pp = ctx.enter_context(nc.psum_tensor("pp", [P, 4, 512], F32))

        w_in_sem = [sem(f"w_landed{k}") for k in range(KC)]
        x_sem = [sem(f"x_landed{i}") for i in range(2)]
        const_landed, consts_set = sem("const_landed"), sem("consts_set")
        ss_done, std_done, rs_done, u_done = sem("ss_done"), sem("std_done"), sem("rs_done"), sem("u_done")
        ut_ps, ut_a, ut_v = sem("u_transposed"), sem("ut_copied_act"), sem("ut_copied_dve")
        proj_ps, proj_out = sem("proj_ready"), sem("proj_copied")
        sq_done, hs_done, hstd_done = sem("head_squares"), sem("head_sums"), sem("head_std")
        qn_done, gain_done, t1_done, t2_done, ro_done = (sem("qn_done"), sem("gain_done"), sem("t1_done"),
                                                        sem("t2_done"), sem("rotated"))
        qk_ps, hi_done, lo_done = sem("qk_transposed"), sem("hi_done"), sem("lo_done")
        qk_stored = [sem(f"qk_stored{i}") for i in range(2)]
        dve_chain = sem("dve_chain1")

        T = NT + 1
        rows = [P] * NT + [N_META]
        colgroups = [[(0, 512), (512, 1024), (1024, 1536), (1536, 2048), (2048, 2304)]] * NT + \
                    [[(512, 768), (1280, 1792), (1792, 2304)]]
        chunks = [list(range(RC))] * NT + [[4, 9, 10, 11, 12]]
        tgroups = [[c[i:i + 4] for i in range(0, len(c), 4)] for c in chunks]
        ngroups_before = [sum(len(x) for x in colgroups[:t]) for t in range(T + 1)]
        ntg_before = [sum(len(x) for x in tgroups[:t]) for t in range(T + 1)]
        heads_a = [(0, 10)] * NT + [(8, 10)]
        heads_d = [(0, 32)] * NT + [(16, 32)]
        gain_ops = [4] * NT + [2]

        def view_a(ap, t):
            h0, h1 = heads_a[t]
            return ap[:, h0 * DH:h1 * DH].rearrange("p (h d) -> p h d", d=DH)

        def view_d(ap, t, base):
            h0, h1 = heads_d[t]
            return ap[:, base + h0 * DQ:base + h1 * DQ].rearrange("p (h d) -> p h d", d=DQ)

        def halves(ap, t, base):
            r = rows[t]
            va = view_a(ap[0:r], t).rearrange("p h (s d) -> p h s d", s=2)
            vd = view_d(ap[0:r], t, base).rearrange("p h (s d) -> p h s d", s=2)
            return va, vd

        block = ctx.enter_context(nc.Block())

        @block.sync
        def _(sp):
            def load_x(t):
                if t >= 2:
                    sp.wait_ge(u_done, t - 1)
                src = a["x"][0, t * P:(t + 1) * P, :] if t < NT else a["meta_tokens"][:, :]
                sp.dma_start(xs[0:rows[t], t % 2, :], src).then_inc(x_sem[t % 2], 16)
            load_x(0)
            sp.dma_start(g_sb[:, :], a["g_attn"][0, :].partition_broadcast(P)).then_inc(const_landed, 16)
            sp.dma_start(ident[:, :], a["consts"][:, 0:P]).then_inc(const_landed, 16)
            load_x(1)
            for k in range(KC):
                sp.dma_start(w_sb[:, k, :], a["w_in"][0, k * P:(k + 1) * P, :]).then_inc(w_in_sem[k], 16)
                if k == 0:
                    sp.dma_start(rope[:, 0:NT, :], a["rope"][0:SEQ, :].rearrange("(t p) n -> p t n", p=P)
                                 ).then_inc(const_landed, 16)
                    sp.dma_start(rope[0:N_META, NT, :], a["rope"][SEQ:KEYS, :]).then_inc(const_landed, 16)
                    for i, n in enumerate(("g_q_swa", "g_k_swa")):
                        sp.dma_start(gains[:, i, :], a[n][0, :].partition_broadcast(P)).then_inc(const_landed, 16)
                    for i, n in enumerate(("g_q_diff", "g_k_diff")):
                        sp.dma_start(gaind[:, i, :], a[n][0, :].partition_broadcast(P)).then_inc(const_landed, 16)
            load_x(2)
            stored = [0, 0]
            for t in range(T):
                r = rows[t]
                if t + 3 < T:
                    load_x(t + 3)
                sp.wait_ge(hi_done, ntg_before[t + 1])
                sp.wait_ge(lo_done, ntg_before[t + 1])
                c0 = t * P
                for part, buf in ((0, hi), (1, lo)):
                    dst = qk_dram[part].rearrange("(c p) n -> p c n", p=P)[:, :, c0:c0 + r]
                    for x0, x1 in ([(0, RC)] if t < NT else [(4, 5), (9, 13)]):
                        sp.dma_start(dst[:, x0:x1, :], buf[:, t % 2, x0:x1, 0:r].bitcast(F32)).then_inc(qk_stored[t % 2], 16)
                        stored[t % 2] += 16
            for i in range(2):
                sp.wait_ge(qk_stored[i], stored[i])

        stored_before = [0 if t < 2 else 32 * (t // 2) for t in range(T)]

        @block.scalar
        def _(act):
            def norm(t):
                r = rows[t]
                act.wait_ge(x_sem[t % 2], 16 * (t // 2 + 1))
                if t >= 2:
                    act.wait_ge(ut_ps, 2 * (t - 1))
                act.activation(us[0:r, t % 2, :], xs[0:r, t % 2, :], ACT.Square, accum_out=ss[0:r, t:t + 1]).then_inc(ss_done, 1)
                act.wait_ge(ss_done, t + 1)
                act.wait_ge(consts_set, 1)
                act.activation(rs[0:r, t:t + 1], ss[0:r, t:t + 1], ACT.Sqrt, bias=eps[0:r], scale=1.0 / D
                               ).then_inc(std_done, 1)

            def copy_ut(t):
                r = rows[t]
                act.wait_ge(ut_ps, 2 * t + 1)
                if t >= 2:
                    act.wait_ge(proj_ps, ngroups_before[t - 1])
                act.copy(ut[:, t % 2, 0:4, 0:r], ptu[:, 0, :].rearrange("p (c n) -> p c n", n=P)[:, :, 0:r]
                         ).then_inc(ut_a, 1)

            def copy_hi(t):
                r = rows[t]
                if t >= 2:
                    act.wait_ge(qk_stored[t % 2], stored_before[t])
                for i, cs in enumerate(tgroups[t]):
                    n = ntg_before[t] + i
                    act.wait_ge(qk_ps, n + 1)
                    runs = [cs] if cs[-1] - cs[0] == len(cs) - 1 else [cs[:1], cs[1:]]
                    at = 0
                    for run in runs:
                        ins = act.copy(hi[:, t % 2, run[0]:run[-1] + 1, 0:r],
                                       ptq[:, n % 2, at * P:(at + len(run)) * P].rearrange("p (c n) -> p c n", n=P)[:, :, 0:r])
                        at += len(run)
                    ins.then_inc(hi_done, 1)

            norm(0)
            copy_ut(0)
            for t in range(T):
                r = rows[t]
                if t + 1 < T:
                    norm(t + 1)
                if t >= 2:
                    act.wait_ge(ro_done, 4 * (t - 1))
                for i, (c0, c1) in enumerate(colgroups[t]):
                    n = ngroups_before[t] + i
                    act.wait_ge(proj_ps, n + 1)
                    act.copy(pr[0:r, t % 2, c0:c1], pp[0:r, n % 4, 0:c1 - c0]).then_inc(proj_out, 1)
                    if i == 2 and t + 1 < T:
                        copy_ut(t + 1)
                if t >= 1:
                    copy_hi(t - 1)
                act.wait_ge(hs_done, t + 1)
                act.activation(hr[0:r, :], hs[0:r, :], ACT.Sqrt, bias=eps[0:r]).then_inc(hstd_done, 1)
            copy_hi(T - 1)

        @block.vector
        def _(dve):
            step = chained(dve, dve_chain)
            dve.memset(hs[:, :], 1.0)
            dve.memset(eps[:, :], EPS).then_inc(consts_set, 1)
            dve.wait_ge(const_landed, 16 * 8)
            step(dve.tensor_scalar(gains[:, 0, :], gains[:, 0, :], DH ** -0.5, None, ALU.mult))
            step(dve.tensor_scalar(gaind[:, 0, :], gaind[:, 0, :], DQ ** -0.5, None, ALU.mult))

            def norm(t):
                r = rows[t]
                dve.wait_ge(std_done, t + 1)
                dve.reciprocal(rs[0:r, t:t + 1], rs[0:r, t:t + 1]).then_inc(rs_done, 1)
                dve.wait_ge(rs_done, t + 1)
                if t >= 2:
                    dve.wait_ge(ut_ps, 2 * (t - 1))
                dve.scalar_tensor_tensor(out=us[0:r, t % 2, :], in0=xs[0:r, t % 2, :], scalar=rs[0:r, t:t + 1],
                                         in1=g_sb[0:r, :], op0=ALU.mult, op1=ALU.mult).then_inc(u_done, 1)

            def copy_ut(t):
                r = rows[t]
                dve.wait_ge(ut_ps, 2 * t + 2)
                if t >= 2:
                    dve.wait_ge(proj_ps, ngroups_before[t - 1])
                dve.tensor_copy(ut[:, t % 2, 4:8, 0:r], ptu[:, 1, :].rearrange("p (c n) -> p c n", n=P)[:, :, 0:r]
                                ).then_inc(ut_v, 1)

            def head_sums(t):
                r = rows[t]
                (a0, a1), (d0, d1) = heads_a[t], heads_d[t]
                dve.wait_ge(sq_done, 2 * (t + 1))
                step(dve.tensor_reduce(hs[0:r, a0:a1], view_a(t1[0:r], t), AX.X, ALU.add))
                step(dve.tensor_reduce(hs[0:r, 10 + d0:10 + d1], view_d(t1[0:r], t, R_QD), AX.X, ALU.add))
                step(dve.tensor_scalar(hs[0:r, a0:a1], hs[0:r, a0:a1], 1.0 / DH, None, ALU.mult))
                dve.tensor_scalar(hs[0:r, 10 + d0:10 + d1], hs[0:r, 10 + d0:10 + d1], 1.0 / DQ, None,
                                  ALU.mult).then_inc(hs_done, 1)

            def rotate(t):
                r = rows[t]
                (a0, a1), (d0, d1) = heads_a[t], heads_d[t]
                dve.wait_ge(hstd_done, t + 1)
                step(dve.reciprocal(hr[0:r, :], hr[0:r, :]))
                if t >= 1:
                    dve.wait_ge(t1_done, 2 * t)
                    dve.wait_ge(t2_done, 4 * t)
                dve.tensor_tensor(view_a(qn[0:r], t), view_a(pr[0:r, t % 2], t),
                                  hr[0:r, a0:a1].unsqueeze(2).broadcast_to((r, a1 - a0, DH)), ALU.mult).then_inc(qn_done, 1)
                dve.tensor_tensor(view_d(qn[0:r], t, R_QD), view_d(pr[0:r, t % 2], t, QD),
                                  hr[0:r, 10 + d0:10 + d1].unsqueeze(2).broadcast_to((r, d1 - d0, DQ)), ALU.mult).then_inc(qn_done, 1)
                dve.wait_ge(gain_done, sum(gain_ops[:t + 1]))
                qa, qd = halves(qn, t, R_QD)
                ta, td = halves(t1, t, R_QD)
                sa, sd = halves(t2, t, R_QD)
                oa, od = halves(ro[:, t % 2], t, R_QD)
                for q, o, h, c, n in ((qa, ta, a1 - a0, 0, 32), (qd, td, d1 - d0, 64, 16)):
                    cos = rope[0:r, t, c:c + n].unsqueeze(1).broadcast_to((r, h, n))
                    for s in range(2):
                        ins = dve.tensor_tensor(o[:, :, s, :], q[:, :, s, :], cos, ALU.mult)
                    ins.then_inc(t1_done, 1)
                dve.wait_ge(t1_done, 2 * (t + 1))
                dve.wait_ge(t2_done, 4 * (t + 1))
                if t >= 2:
                    dve.wait_ge(qk_ps, ntg_before[t - 1])
                for o, x, y in ((oa, ta, sa), (od, td, sd)):
                    dve.tensor_tensor(o[:, :, 0, :], x[:, :, 0, :], y[:, :, 0, :], ALU.subtract).then_inc(ro_done, 1)
                    dve.tensor_tensor(o[:, :, 1, :], x[:, :, 1, :], y[:, :, 1, :], ALU.add).then_inc(ro_done, 1)

            def low(t):
                r = rows[t]
                if t >= 2:
                    dve.wait_ge(qk_stored[t % 2], stored_before[t])
                for i, cs in enumerate(tgroups[t]):
                    n = ntg_before[t] + i
                    dve.wait_ge(hi_done, n + 1)
                    runs = [cs] if cs[-1] - cs[0] == len(cs) - 1 else [cs[:1], cs[1:]]
                    at = 0
                    for run in runs:
                        k = slice(run[0], run[-1] + 1)
                        ins = dve.tensor_tensor(lo[:, t % 2, k, 0:r],
                                                ptq[:, n % 2, at * P:(at + len(run)) * P].rearrange("p (c n) -> p c n", n=P)[:, :, 0:r],
                                                hi[:, t % 2, k, 0:r].bitcast(F32), ALU.subtract)
                        at += len(run)
                    ins.then_inc(lo_done, 1)

            norm(0)
            copy_ut(0)
            for t in range(T):
                if t + 1 < T:
                    norm(t + 1)
                    copy_ut(t + 1)
                if t >= 1:
                    low(t - 1)
                head_sums(t)
                rotate(t)
            low(T - 1)

        @block.gpsimd
        def _(pool):
            pool.wait_ge(const_landed, 16 * 8)
            for t in range(T):
                r = rows[t]
                (a0, a1), (d0, d1) = heads_a[t], heads_d[t]
                pool.wait_ge(proj_out, ngroups_before[t + 1])
                if t >= 1:
                    pool.wait_ge(ro_done, 4 * t)
                pool.tensor_tensor(view_a(t1[0:r], t), view_a(pr[0:r, t % 2], t), view_a(pr[0:r, t % 2], t),
                                   ALU.mult).then_inc(sq_done, 1)
                pool.tensor_tensor(view_d(t1[0:r], t, R_QD), view_d(pr[0:r, t % 2], t, QD),
                                   view_d(pr[0:r, t % 2], t, QD), ALU.mult).then_inc(sq_done, 1)
                vw = v_all[0:r, t, :]
                pool.tensor_copy(vw[:, 0:128], pr[0:r, t % 2, VA:VA + 128])
                pool.tensor_copy(vw[:, 128:640], pr[0:r, t % 2, VD:VD + 512])
                pool.wait_ge(qn_done, 2 * (t + 1))
                for h0, h1, g in ((0, 8, 0), (8, 10, 1)):
                    if h0 >= a0:
                        v = qn[0:r, h0 * DH:h1 * DH].rearrange("p (h d) -> p h d", d=DH)
                        pool.tensor_tensor(v, v, gains[0:r, g, :].unsqueeze(1).broadcast_to((r, h1 - h0, DH)),
                                           ALU.mult).then_inc(gain_done, 1)
                for h0, h1, g in ((0, 16, 0), (16, 32, 1)):
                    if h0 >= d0:
                        v = qn[0:r, R_QD + h0 * DQ:R_QD + h1 * DQ].rearrange("p (h d) -> p h d", d=DQ)
                        pool.tensor_tensor(v, v, gaind[0:r, g, :].unsqueeze(1).broadcast_to((r, h1 - h0, DQ)),
                                           ALU.mult).then_inc(gain_done, 1)
                pool.wait_ge(gain_done, sum(gain_ops[:t + 1]))
                if t >= 1:
                    pool.wait_ge(ro_done, 4 * t)
                qa, qd = halves(qn, t, R_QD)
                sa, sd = halves(t2, t, R_QD)
                for q, o, h, c, n in ((qa, sa, a1 - a0, 32, 32), (qd, sd, d1 - d0, 80, 16)):
                    sin = rope[0:r, t, c:c + n].unsqueeze(1).broadcast_to((r, h, n))
                    for s in range(2):
                        pool.tensor_tensor(o[:, :, s, :], q[:, :, 1 - s, :], sin, ALU.mult).then_inc(t2_done, 1)

        @block.tensor
        def _(pe):
            def transpose_u(t):
                r = rows[t]
                pe.wait_ge(u_done, t + 1)
                for b in range(2):
                    if t >= 1:
                        pe.wait_ge((ut_a, ut_v)[b], t)
                    for c in range(4):
                        k = 4 * b + c
                        ins = pe.transpose(ptu[:, b, c * P:c * P + r], us[0:r, t % 2, k * P:(k + 1) * P], ident[0:r, 0:r])
                    ins.then_inc(ut_ps, 1)

            def transpose_qk(t):
                r = rows[t]
                pe.wait_ge(ro_done, 4 * (t + 1))
                for i, cs in enumerate(tgroups[t]):
                    n = ntg_before[t] + i
                    if n >= 2:
                        pe.wait_ge(lo_done, n - 1)
                    for j, c in enumerate(cs):
                        ins = pe.transpose(ptq[:, n % 2, j * P:j * P + r], ro[0:r, t % 2, c * P:(c + 1) * P], ident[0:r, 0:r])
                    ins.then_inc(qk_ps, 1)

            pe.wait_ge(const_landed, 16 * 8)
            transpose_u(0)
            for t in range(T):
                r = rows[t]
                pe.wait_ge(ut_a, t + 1)
                pe.wait_ge(ut_v, t + 1)
                for i, (c0, c1) in enumerate(colgroups[t]):
                    n = ngroups_before[t] + i
                    if n >= 4:
                        pe.wait_ge(proj_out, n - 3)
                    for k in range(KC):
                        if n == 0:
                            pe.wait_ge(w_in_sem[k], 16)
                        ins = pe.matmul(pp[0:r, n % 4, 0:c1 - c0], ut[:, t % 2, k, 0:r], w_sb[:, k, c0:c1],
                                        start=(k == 0), stop=(k == KC - 1))
                    ins.then_inc(proj_ps, 1)
                    if i == 1 and t + 1 < T:
                        transpose_u(t + 1)
                if t >= 1:
                    transpose_qk(t - 1)
            transpose_qk(T - 1)


def attend_diff(nc, a, v_all, mixed, qk_dram):
    with ExitStack() as ctx:
        sb = lambda n, s, d=F32: ctx.enter_context(nc.sbuf_tensor(n, s, d))
        sem = lambda n: ctx.enter_context(nc.semaphore(n))
        ps = lambda n, s: ctx.enter_context(nc.psum_tensor(n, s, F32))
        q_st = sb("q_st", [P, 2, 2, SEQ], F32R)
        k_st = sb("k_st", [P, 2, 2, KEYS], F32R)
        e = sb("e", [P, 2, 2, KEYS])
        dsb = sb("dsb", [P, 2, KEYS])
        pt = sb("pt", [P, 2, 9, 512])
        ot = sb("ot", [DV, 512])
        ident = sb("ident2", [P, P])
        lam = sb("lam", [P, 4, DQ])
        lw = sb("lw", [P, 8])
        nm = sb("nm", [P, 4])
        ls = sb("ls", [P, 2, 2])
        rl = sb("rl", [P, 4])
        r1 = sb("r1", [P, 16])
        s_ps = [ps("s_ps0", [P, 3, 512]), ps("s_ps1", [P, 3, 512])]
        t_ps = ps("t_ps", [P, 512])
        o_ps = ps("o_ps", [P, 512])

        const_landed = sem("const_landed2")
        st_sem = [sem(f"stack_landed{i}") for i in range(2)]
        lam_dots, lam_exp, lam_done = sem("lam_dots"), sem("lam_exp"), sem("lam_done")
        scores_ready, max_ready, exp_done = sem("scores_ready"), sem("max_ready"), sem("exp_done")
        combined, t_ready, t_copied = sem("combined"), sem("p_transposed"), sem("pt_copied")
        o_ready, ot_done = sem("o_ready"), sem("ot_copied")
        dve_chain = sem("dve_chain2")

        U = HD * NT
        NG = U // 4
        chunks = [(0, 4), (4, 8), (8, 9)]
        S0 = lambda i: s_ps[i][:, :, :].rearrange("p b n -> p (b n)")[:, 0:KEYS]
        block = ctx.enter_context(nc.Block())

        uses, use_of = 0, {}
        for n in range(U + 6):
            if 1 <= n <= U:
                for g in range(3):
                    use_of[("p", n - 1, g)] = uses
                    uses += 1
            if n >= 9 and (n - 9) % 4 == 0 and (n - 9) // 4 < NG:
                use_of[("o", (n - 9) // 4)] = uses
                uses += 1

        @block.sync
        def _(sp):
            sp.dma_start(ident[:, :], a["consts"][:, 0:P]).then_inc(const_landed, 16)
            for i, n in enumerate(("lambda_q1", "lambda_k1", "lambda_q2", "lambda_k2")):
                sp.dma_start(lam[:, i, :], a[n][0, :].partition_broadcast(P)).then_inc(const_landed, 16)
            for h in range(HD):
                b = h % 2
                if h >= 2:
                    sp.wait_ge(scores_ready, 2 * NT * (h - 1))
                for j in range(4):
                    rows = slice(32 * j, 32 * j + 32)
                    for buf, at, part, n in ((q_st, R_QD, j % 2, SEQ), (k_st, R_KD, j // 2, KEYS)):
                        src = qk_dram[part, at + h * 64:at + h * 64 + 64, 0:n].rearrange("(s d) n -> d s n", s=2)
                        sp.dma_start(buf[rows, b, :, 0:n].bitcast(F32), src).then_inc(st_sem[b], 16)

        @block.scalar
        def _(act):
            def copy_part(u, g):
                n = use_of[("p", u, g)]
                act.wait_ge(t_ready, n + 1)
                act.copy(pt[:, (u // 4) % 2, 0:4, (u % 4) * P:(u % 4 + 1) * P],
                         t_ps[:, :].rearrange("p (c n) -> p c n", n=P)).then_inc(t_copied, 1)

            act.wait_ge(lam_dots, 2)
            act.activation(lw[:, 2:4], lw[:, 0:2], ACT.Exp).then_inc(lam_exp, 1)
            for n in range(U + 6):
                if n < U:
                    for i in range(2):
                        act.wait_ge(max_ready, 2 * n + i + 1)
                        if n >= 2 and i == 0:
                            act.wait_ge(combined, n - 1)
                        k = (2 * n + i) % 4
                        act.activation(e[:, n % 2, i, :], S0(i), ACT.Exp, bias=nm[:, k:k + 1],
                                       accum_out=ls[:, n % 2, i:i + 1]).then_inc(exp_done, 1)
                        if i == 0 and n >= 1:
                            copy_part(n - 1, 0)
                elif n == U:
                    copy_part(n - 1, 0)
                if n >= 8 and (n - 8) % 4 == 0 and (n - 8) // 4 < NG:
                    g = (n - 8) // 4
                    act.wait_ge(o_ready, g + 1)
                    if g >= 1:
                        act.wait_ge(t_ready, use_of[("o", g - 1)] + 1)
                    act.copy(ot[:, :], o_ps[0:DV, :]).then_inc(ot_done, 1)

        @block.vector
        def _(dve):
            step = chained(dve, dve_chain)
            dve.wait_ge(const_landed, 16 * 5)
            for i in range(2):
                dve.tensor_tensor_reduce(lam[:, 2 * i, :], lam[:, 2 * i, :], lam[:, 2 * i + 1, :], 1.0, 0.0,
                                         ALU.mult, ALU.add, lw[:, i:i + 1]).then_inc(lam_dots, 1)
            dve.wait_ge(lam_exp, 1)
            step(dve.tensor_tensor(lw[:, 4:5], lw[:, 3:4], lw[:, 2:3], ALU.subtract))
            dve.tensor_scalar(lw[:, 5:6], lw[:, 4:5], -LAMBDA_INIT, None, ALU.add).then_inc(lam_done, 1)
            dve.wait_ge(lam_done, 1)

            def copy_parts(u):
                for g in (1, 2):
                    n = use_of[("p", u, g)]
                    dve.wait_ge(t_ready, n + 1)
                    dst = pt[:, (u // 4) % 2, :, (u % 4) * P:(u % 4 + 1) * P]
                    if g == 1:
                        ins = dve.tensor_copy(dst[:, 4:8, :], t_ps[:, :].rearrange("p (c n) -> p c n", n=P))
                    else:
                        ins = dve.tensor_copy(dst[0:N_META, 8, :], t_ps[0:N_META, 0:P])
                    ins.then_inc(t_copied, 1)

            def store_out(g):
                h, t0 = g // 2, 4 * (g % 2)
                n = use_of[("o", g)]
                dve.wait_ge(t_ready, n + 1)
                for j in range(4):
                    ins = dve.tensor_scalar(mixed[:, t0 + j, 512 + h * DV:512 + (h + 1) * DV],
                                            t_ps[:, j * DV:(j + 1) * DV], r1[:, (4 * g + j) % 16:(4 * g + j) % 16 + 1],
                                            None, ALU.mult)
                ins.then_inc(t_copied, 1)

            for n in range(U + 6):
                if n < U:
                    for i in range(2):
                        k = (2 * n + i) % 4
                        dve.wait_ge(scores_ready, 2 * n + i + 1)
                        if n >= 2:
                            dve.wait_ge(exp_done, 2 * n + i - 3)
                        dve.tensor_reduce(nm[:, k:k + 1], S0(i), AX.X, ALU.max, negate=True).then_inc(max_ready, 1)
                if 1 <= n <= U:
                    copy_parts(n - 1)
                if n < U:
                    dve.wait_ge(exp_done, 2 * n + 2)
                    if n >= 2:
                        dve.wait_ge(t_ready, use_of[("p", n - 2, 2)] + 1)
                    step(dve.reciprocal(rl[:, 0:1], ls[:, n % 2, 1:2]))
                    step(dve.tensor_scalar(rl[:, 1:2], ls[:, n % 2, 0:1], rl[:, 0:1], lw[:, 5:6], ALU.mult, ALU.mult))
                    dve.scalar_tensor_tensor(out=dsb[:, n % 2, :], in0=e[:, n % 2, 1, :], scalar=rl[:, 1:2],
                                             in1=e[:, n % 2, 0, :], op0=ALU.mult, op1=ALU.add).then_inc(combined, 1)
                    step(dve.reciprocal(r1[:, n % 16:n % 16 + 1], ls[:, n % 2, 0:1]))
                if n >= 9 and (n - 9) % 4 == 0 and (n - 9) // 4 < NG:
                    store_out((n - 9) // 4)

        @block.tensor
        def _(pe):
            fillers = []

            def values(g, c):
                h = g // 2
                r = P if c < 8 else N_META
                if c == 0:
                    pe.wait_ge(t_copied, use_of[("p", 4 * g + 3, 2)] + 1)
                    if g >= 1:
                        pe.wait_ge(ot_done, g)
                vt = v_all[0:r, c, 128 + h * DV:128 + (h + 1) * DV]
                ins = pe.matmul(o_ps[0:DV, :], vt, pt[0:r, g % 2, c, :], start=(c == 0), stop=(c == 8))
                if c == 8:
                    ins.then_inc(o_ready, 1)

            pe.wait_ge(const_landed, 16 * 5)
            for n in range(U + 6):
                if n < U:
                    h, t = n // NT, n % NT
                    if t == 0:
                        pe.wait_ge(st_sem[h % 2], 16 * 8 * (h // 2 + 1))
                    for i in range(2):
                        if n >= 1:
                            pe.wait_ge(exp_done, 2 * n + i - 1)
                        for b, (c0, c1) in enumerate(((0, 512), (512, 1024), (1024, KEYS))):
                            ins = pe.matmul(s_ps[i][:, b, 0:c1 - c0], q_st[:, h % 2, i, t * P:(t + 1) * P],
                                            k_st[:, h % 2, i, c0:c1], start=True, stop=True)
                        ins.then_inc(scores_ready, 1)
                        if fillers:
                            values(*fillers.pop(0))
                if 1 <= n <= U:
                    u = n - 1
                    pe.wait_ge(combined, u + 1)
                    for g, (c0, c1) in enumerate(chunks):
                        k = use_of[("p", u, g)]
                        if k >= 1:
                            pe.wait_ge(t_copied, k)
                        for c in range(c0, c1):
                            w = min(P, KEYS - c * P)
                            ins = pe.transpose(t_ps[0:w, (c - c0) * P:(c - c0 + 1) * P], dsb[:, u % 2, c * P:c * P + w], ident[:, :])
                        ins.then_inc(t_ready, 1)
                        if g < 1 and fillers:
                            values(*fillers.pop(0))
                if n >= 8 and (n - 8) % 4 == 0 or n >= U:
                    while fillers:
                        values(*fillers.pop(0))
                if n >= 9 and (n - 9) % 4 == 0 and (n - 9) // 4 < NG:
                    g = (n - 9) // 4
                    pe.wait_ge(ot_done, g + 1)
                    pe.wait_ge(t_copied, use_of[("o", g)])
                    for j in range(4):
                        ins = pe.transpose(t_ps[:, j * DV:(j + 1) * DV], ot[:, j * P:(j + 1) * P], ident[0:DV, 0:DV])
                    ins.then_inc(t_ready, 1)
                if n >= 4 and n % 4 == 0 and n // 4 - 1 < NG:
                    fillers += [(n // 4 - 1, c) for c in range(9)]


def attend_window(nc, a, v_all, mixed, qk_dram):
    with ExitStack() as ctx:
        sb = lambda n, s, d=F32: ctx.enter_context(nc.sbuf_tensor(n, s, d))
        sem = lambda n: ctx.enter_context(nc.semaphore(n))
        ps = lambda n, s: ctx.enter_context(nc.psum_tensor(n, s, F32))
        BW = 3 * P + N_META
        q_st = sb("qa_st", [P, HQ, SEQ], F32R)
        k_st = sb("ka_st", [P, 2, HKV, KEYS], F32R)
        masks = sb("masks", [P, 3, BW])
        sink = sb("sink", [P, HQ])
        sm = sb("sm", [P, 2, G, BW])
        pt = sb("pta", [P, 2, 4, 512])
        ot = sb("ota", [DV, 2, 512])
        ident = sb("ident3", [P, P])
        mx = sb("mx", [P, 2, G])
        nm = sb("nma", [P, 2, G])
        ls = sb("lsa", [P, 2, G])
        xs = sb("xsink", [P, 2, G])
        rl = sb("rla", [P, 4, G])
        s_ps = ps("sa_ps", [P, 4, 512])
        t_ps = ps("ta_ps", [P, 2, 512])
        o_ps = ps("oa_ps", [P, 512])
        ob_ps = ps("ob_ps", [P, 512])

        landed = sem("window_landed")
        s_ready, masked, mx_done, nm_done, exp_done = (sem("sa_ready"), sem("masked"), sem("maxa"), sem("nm_done"),
                                                       sem("expa_done"))
        sink_in, sink_exp, rl_done = sem("sink_in"), sem("sink_exp"), sem("rl_done")
        t_ready, t_copied = sem("ta_ready"), sem("ta_copied")
        o_ready, ot_done, ob_ready, ob_done = sem("oa_ready"), sem("ota_done"), sem("ob_ready"), sem("ob_done")
        dve_chain = sem("dve_chain3")
        U = NT * HKV
        bands = [[t + d for d in (-1, 0, 1) if 0 <= t + d < NT] for t in range(NT)]
        which = [0 if t == 0 else 2 if t == NT - 1 else 1 for t in range(NT)]
        nchunk = [len(bands[u // HKV]) + 1 for u in range(U)]
        before = [sum(nchunk[:u]) for u in range(U + 1)]
        width = lambda u: P * (nchunk[u] - 1) + N_META
        block = ctx.enter_context(nc.Block())

        @block.sync
        def _(sp):
            sp.dma_start(ident[:, :], a["consts"][:, 0:P]).then_inc(landed, 16)
            sp.dma_start(masks[:, :, :], a["masks"][:, :, :]).then_inc(landed, 16)
            sp.dma_start(sink[:, :], a["sink_swa"][0, :].partition_broadcast(P)).then_inc(landed, 16)
            for part in range(2):
                rows = slice(64 * part, 64 * part + 64)
                src = qk_dram[part, 0:HQ * DH, 0:SEQ].rearrange("(h d) n -> d h n", d=DH)
                sp.dma_start(q_st[rows, :, :].bitcast(F32), src).then_inc(landed, 16)
                for twice in range(2):
                    src = qk_dram[part, R_KA:R_KA + HKV * DH, :].rearrange("(h d) n -> d h n", d=DH)
                    sp.dma_start(k_st[64 * twice:64 * twice + 64, part, :, :].bitcast(F32), src).then_inc(landed, 16)

        @block.tensor
        def _(pe):
            pe.wait_ge(landed, 16 * 9)

            def scores(u):
                t, g = u // HKV, u % HKV
                k0, nb = bands[t][0] * P, (nchunk[u] - 1) * P
                for j in range(G):
                    if u >= 1:
                        pe.wait_ge(masked, G * (u - 1) + j + 1)
                    q = q_st[:, g * G + j, t * P:(t + 1) * P]
                    for part in range(2):
                        pe.matmul(s_ps[:, j, 0:nb], q, k_st[:, part, g, k0:k0 + nb], start=(part == 0), stop=(part == 1))
                    for part in range(2):
                        ins = pe.matmul(s_ps[:, j, nb:nb + N_META], q, k_st[:, part, g, SEQ:KEYS],
                                        start=(part == 0), stop=(part == 1))
                    ins.then_inc(s_ready, 1)

            def weigh(u):
                t, g = u // HKV, u % HKV
                pe.wait_ge(exp_done, G * (u + 1))
                for c in range(nchunk[u]):
                    n = before[u] + c
                    w = P if c < nchunk[u] - 1 else N_META
                    if n >= 2:
                        pe.wait_ge(t_copied, n - 1)
                    for j in range(G):
                        ins = pe.transpose(t_ps[0:w, n % 2, j * P:(j + 1) * P], sm[:, u % 2, j, c * P:c * P + w], ident[:, :])
                    ins.then_inc(t_ready, 1)

            def values(u):
                t, g = u // HKV, u % HKV
                for c in range(nchunk[u]):
                    w = P if c < nchunk[u] - 1 else N_META
                    tile = bands[t][c] if w == P else NT
                    pe.wait_ge(t_copied, before[u] + c + 1)
                    if c == 0 and u >= 1:
                        pe.wait_ge(ot_done, u)
                    ins = pe.matmul(o_ps[0:DV, :], v_all[0:w, tile, g * DH:(g + 1) * DH], pt[0:w, u % 2, c, :],
                                    start=(c == 0), stop=(c == nchunk[u] - 1))
                ins.then_inc(o_ready, 1)

            def back(u):
                pe.wait_ge(ot_done, u + 1)
                if u >= 1:
                    pe.wait_ge(ob_done, u)
                for j in range(G):
                    ins = pe.transpose(ob_ps[:, j * DV:(j + 1) * DV], ot[:, u % 2, j * P:(j + 1) * P], ident[0:DV, 0:DV])
                ins.then_inc(ob_ready, 1)

            for n in range(U + 3):
                if n < U:
                    scores(n)
                if 1 <= n <= U:
                    weigh(n - 1)
                if 2 <= n <= U + 1:
                    values(n - 2)
                if n >= 3:
                    back(n - 3)

        def copy_chunk(op, eng, u, c):
            n = before[u] + c
            w = P if c < nchunk[u] - 1 else N_META
            eng.wait_ge(t_ready, n + 1)
            if n >= 1:
                eng.wait_ge(t_copied, n)
            if u >= 2 and c < 2:
                eng.wait_ge(o_ready, u - 1)
            op(pt[0:w, u % 2, c, :], t_ps[0:w, n % 2, :]).then_inc(t_copied, 1)

        @block.vector
        def _(dve):
            step = chained(dve, dve_chain)
            dve.wait_ge(landed, 16 * 9)
            for n in range(U + 3):
                if n < U:
                    t, g, b, w = n // HKV, n % HKV, n % 2, width(n)
                    if n >= 2:
                        dve.wait_ge(t_ready, before[n - 1])
                    for j in range(G):
                        dve.wait_ge(s_ready, G * n + j + 1)
                        dve.tensor_tensor_reduce(sm[:, b, j, 0:w], s_ps[:, j, 0:w], masks[:, which[t], 0:w], 1.0, NEG,
                                                 ALU.add, ALU.max, mx[:, b, j:j + 1]).then_inc(masked, 1)
                    dve.wait_ge(masked, G * (n + 1))
                    step(dve.tensor_tensor(mx[:, b, :], mx[:, b, :], sink[:, g * G:(g + 1) * G], ALU.max))
                    dve.tensor_scalar(nm[:, b, :], mx[:, b, :], -1.0, None, ALU.mult).then_inc(nm_done, 1)
                    dve.tensor_tensor(xs[:, b, :], sink[:, g * G:(g + 1) * G], mx[:, b, :], ALU.subtract).then_inc(sink_in, 1)
                if 1 <= n <= U:
                    u = n - 1
                    dve.wait_ge(sink_exp, u + 1)
                    dve.wait_ge(exp_done, G * (u + 1))
                    step(dve.tensor_tensor(ls[:, u % 2, :], ls[:, u % 2, :], xs[:, u % 2, :], ALU.add))
                    dve.reciprocal(rl[:, u % 4, :], ls[:, u % 2, :]).then_inc(rl_done, 1)
                    for c in range(1, nchunk[u], 2):
                        copy_chunk(dve.tensor_copy, dve, u, c)
                if n >= 3:
                    u = n - 3
                    t, g = u // HKV, u % HKV
                    dve.wait_ge(ob_ready, u + 1)
                    dve.wait_ge(rl_done, u + 1)
                    for j in range(G):
                        hcol = (g * G + j) * DH
                        ins = dve.tensor_scalar(mixed[:, t, hcol:hcol + DH], ob_ps[:, j * DV:(j + 1) * DV],
                                                rl[:, u % 4, j:j + 1], None, ALU.mult)
                    ins.then_inc(ob_done, 1)

        @block.scalar
        def _(act):
            for n in range(U + 2):
                if n < U:
                    b, w = n % 2, width(n)
                    act.wait_ge(nm_done, n + 1)
                    if n >= 2:
                        act.wait_ge(rl_done, n - 1)
                    for j in range(G):
                        act.activation(sm[:, b, j, 0:w], sm[:, b, j, 0:w], ACT.Exp, bias=nm[:, b, j:j + 1],
                                       accum_out=ls[:, b, j:j + 1]).then_inc(exp_done, 1)
                    act.wait_ge(sink_in, n + 1)
                    act.activation(xs[:, b, :], xs[:, b, :], ACT.Exp).then_inc(sink_exp, 1)
                if 1 <= n <= U:
                    for c in range(0, nchunk[n - 1], 2):
                        copy_chunk(act.copy, act, n - 1, c)
                if n >= 2:
                    u = n - 2
                    act.wait_ge(o_ready, u + 1)
                    if u >= 2:
                        act.wait_ge(ob_ready, u - 1)
                    act.copy(ot[:, u % 2, :], o_ps[0:DV, :]).then_inc(ot_done, 1)


C_ID, C_TRI, C_EXP, C_BASE, C_JOB, C_STEP, C_W = 0, 128, 256, 288, 320, 384, 388


def route(nc, a, mixed, gates, jobs, h2_dram, v_dram, slot_dram):
    with ExitStack() as ctx:
        sb = lambda n, s, d=F32: ctx.enter_context(nc.sbuf_tensor(n, s, d))
        sem = lambda n: ctx.enter_context(nc.semaphore(n))
        ps = lambda n, s: ctx.enter_context(nc.psum_tensor(n, s, F32))
        w_sb = sb("w_out_sb", [P, KC, D])
        wr = sb("w_router_sb", [P, KC, N_EXP])
        br = sb("b_router_sb", [P, N_EXP])
        gd = sb("g_head_sb", [P, DV])
        gf = sb("g_ffn_sb", [P, D])
        cst = sb("cst", [P, C_W])
        ones = sb("ones", [P, P])
        xs = sb("xs4", [P, 2, D])
        hsq = sb("hsq", [P, HD * DV])
        hs = sb("hs4", [P, HD])
        hr = sb("hr4", [P, HD])
        mt = sb("mt", [P, 2, KC, P])
        h2 = sb("h2", [P, 2, D])
        vs = sb("vs", [P, 2, D])
        vt = sb("vt", [P, KC, P])
        ss = sb("ss4", [P, NT])
        rs = sb("rs4", [P, NT])
        eps = sb("eps4", [P, 2])
        lg = sb("lg", [P, N_EXP])
        top = sb("top", [P, NT, 8])
        idx = sb("idx", [P, 8], U32)
        idf = sb("idf", [P, 8])
        oh = sb("oh", [P, TOP_K, N_EXP])
        sel = sb("sel", [P, N_EXP])
        acc = sb("acc", [P, N_EXP])
        pos = sb("pos", [P, N_EXP])
        junk = sb("junk", [P, N_EXP])
        dst = sb("dst", [P, NT, TOP_K])
        dsti = sb("dsti", [P, NT, TOP_K], U32)
        code = sb("code", [P, NT, TOP_K, 2], U32)
        none = sb("none", [P, N_EXP * CAP * 2 // P], U32)
        gsum = sb("gsum", [P, NT])
        ec = sb("ec", [N_EXP, 8])
        ej = sb("ej", [N_EXP, 3, NJ])
        jf = sb("jf", [1, 6, NJ])
        tm_ps, tv_ps = ps("tm_ps", [P, 2, 512]), ps("tv_ps", [P, 512])
        o_ps, r_ps = ps("o4_ps", [P, 4, 512]), ps("r_ps", [P, 512])

        landed = sem("route_landed")
        x_sem = [sem(f"x4_landed{i}") for i in range(2)]
        h2_sem = [sem(f"h2_stored{i}") for i in range(2)]
        v_sem = [sem(f"v_stored{i}") for i in range(2)]
        cleared, scattered = sem("slots_cleared"), sem("slots_written")
        ready, ones_set, codes_set = sem("consts4_set"), sem("ones_set"), sem("codes_set")
        hs_done, hstd_done, head_done = sem("hs4_done"), sem("hstd4_done"), sem("head_done")
        tm_ready, mt_a, mt_v = sem("tm_ready"), sem("mt_act"), sem("mt_dve")
        o_ready, h2_done = sem("o4_ready"), sem("h2_done")
        ss_done, std_done, v_done = sem("ss4_done"), sem("std4_done"), sem("v_done")
        tv_ready, vt_done = sem("tv_ready"), sem("vt_done")
        r_ready, lg_done, sel_done, rank_ready, dst_done = (sem("r_ready"), sem("lg_done"), sem("sel_done"),
                                                            sem("rank_ready"), sem("dst_done"))
        gates_in, gates_exp = sem("gates_in"), sem("gates_exp")
        cnt_ready, jobs_step, jobs_in = sem("cnt_ready"), sem("jobs_step"), sem("jobs_in")
        dve_chain = sem("dve_chain4")
        block = ctx.enter_context(nc.Block())
        NL = 8

        @block.sync
        def _(sp):
            sp.dma_start(cst[:, :], a["consts"][:, :]).then_inc(landed, 16)
            sp.dma_start(gd[:, :], a["g_diff_head"][0, :].partition_broadcast(P)).then_inc(landed, 16)

            def load_x(t):
                if t >= 2:
                    sp.wait_ge(h2_done, 2 * (t - 1))
                sp.dma_start(xs[:, t % 2, :], a["x"][0, t * P:(t + 1) * P, :]).then_inc(x_sem[t % 2], 16)
            load_x(0)
            load_x(1)
            for c in range(2):
                sp.dma_start(w_sb[:, 4 * c:4 * c + 4, :],
                             a["w_out"][0, 512 * c:512 * c + 512, :].rearrange("(k p) n -> p k n", p=P)).then_inc(landed, 16)
            sp.dma_start(gf[:, :], a["g_ffn"][0, :].partition_broadcast(P)).then_inc(landed, 16)
            sp.dma_start(br[:, :], a["b_router"][0, :].partition_broadcast(P)).then_inc(landed, 16)
            with nc.allow_non_contiguous_dma("128 byte rows, once"):
                sp.dma_start(wr[:, :, :], a["w_router"][0].rearrange("(k p) n -> p k n", p=P)).then_inc(landed, 16)
            sp.dma_start(ones[:, :], a["ones"][:, :]).then_inc(landed, 16)
            for t in range(NT):
                sp.wait_ge(h2_done, 2 * (t + 1))
                sp.dma_start(h2_dram[t * P:(t + 1) * P, :], h2[:, t % 2, :]).then_inc(h2_sem[t % 2], 16)
                if t + 2 < NT:
                    load_x(t + 2)
                sp.wait_ge(v_done, t + 1)
                sp.dma_start(v_dram[t * P:(t + 1) * P, :], vs[:, t % 2, :]).then_inc(v_sem[t % 2], 16)
            for i in range(2):
                sp.wait_ge(h2_sem[i], 16 * (NT // 2))
                sp.wait_ge(v_sem[i], 16 * (NT // 2))

        @block.gpsimd
        def _(pool):
            pool.memset(none[:, :], SEQ * TOP_K).then_inc(ready, 1)
            pool.iota(code[:, :, :, 0], pattern=[[P * TOP_K, NT], [1, TOP_K]], base=0, channel_multiplier=TOP_K
                      ).then_inc(codes_set, 1)
            pool.iota(code[:, :, :, 1], pattern=[[P, NT], [0, TOP_K]], base=0, channel_multiplier=1
                      ).then_inc(codes_set, 1)
            pool.wait_ge(ready, 1)
            pool.dma_start(slot_dram.rearrange("(p n) c -> p (n c)", p=P), none[:, :]).then_inc(cleared, 16)
            pool.wait_ge(cleared, 16)
            pool.wait_ge(codes_set, 2)
            for t in range(NT):
                pool.wait_ge(dst_done, t + 1)
                for k in range(TOP_K):
                    pool.indirect_dma_start(out=slot_dram[:, :],
                                            out_offset=bass.IndirectOffsetOnAxis(ap=dsti[:, t, k:k + 1], axis=0),
                                            in_=code[:, t, k, :], in_offset=None).then_inc(scattered, 16)
            pool.wait_ge(scattered, 16 * NT * TOP_K)

        @block.scalar
        def _(act):
            act.wait_ge(ones_set, 1)

            def head_std(t):
                act.wait_ge(hs_done, t + 1)
                act.activation(hr[:, :], hs[:, :], ACT.Sqrt, bias=eps[:, 1:2], scale=1.0 / DV).then_inc(hstd_done, 1)

            head_std(0)
            for t in range(NT + 1):
                if t + 1 < NT:
                    head_std(t + 1)
                if t < NT:
                    act.wait_ge(tm_ready, 2 * t + 1)
                    if t >= 2:
                        act.wait_ge(o_ready, 2 * (t - 1))
                    act.copy(mt[:, t % 2, 0:4, :], tm_ps[:, 0, :].rearrange("p (c n) -> p c n", n=P)).then_inc(mt_a, 1)
                    act.wait_ge(h2_done, 2 * (t + 1))
                    if t >= 2:
                        act.wait_ge(tv_ready, 2 * (t - 1))
                        act.wait_ge(v_sem[t % 2], 16 * (t // 2))
                    act.activation(vs[:, t % 2, :], h2[:, t % 2, :], ACT.Square, accum_out=ss[:, t:t + 1]).then_inc(ss_done, 1)
                    act.wait_ge(ss_done, t + 1)
                    act.activation(rs[:, t:t + 1], ss[:, t:t + 1], ACT.Sqrt, bias=eps[:, 0:1], scale=1.0 / D).then_inc(std_done, 1)
                if t >= 1:
                    u = t - 1
                    for b in range(2):
                        act.wait_ge(tv_ready, 2 * u + b + 1)
                        if b == 0 and u >= 1:
                            act.wait_ge(r_ready, u)
                        act.copy(vt[:, 4 * b:4 * b + 4, :], tv_ps[:, :].rearrange("p (c n) -> p c n", n=P)).then_inc(vt_done, 1)
            act.wait_ge(gates_in, 1)
            act.activation(gates[:, :, :], gates[:, :, :], ACT.Exp).then_inc(gates_exp, 1)

        @block.vector
        def _(dve):
            step = chained(dve, dve_chain)
            dve.memset(acc[:, :], 0.0)
            dve.memset(eps[:, 0:1], EPS)
            step(dve.memset(eps[:, 1:2], EPS_HEAD))
            dve.wait_ge(landed, 16 * NL)
            dve.tensor_scalar(gd[:, :], gd[:, :], 1.0 - LAMBDA_INIT, None, ALU.mult).then_inc(ones_set, 1)
            dve.wait_ge(ones_set, 1)

            def heads(t):
                m = mixed[:, t, 512:1024]
                v = m.rearrange("p (h d) -> p h d", d=DV)
                step(dve.tensor_tensor(hsq[:, :], m, m, ALU.mult))
                if t >= 1:
                    dve.wait_ge(head_done, t)
                dve.tensor_reduce(hs[:, :], hsq[:, :].rearrange("p (h d) -> p h d", d=DV), AX.X, ALU.add).then_inc(hs_done, 1)
                dve.wait_ge(hstd_done, t + 1)
                step(dve.reciprocal(hr[:, :], hr[:, :]))
                step(dve.tensor_tensor(v, v, hr[:, :].unsqueeze(2).broadcast_to((P, HD, DV)), ALU.mult))
                dve.tensor_tensor(v, v, gd[:, :].unsqueeze(1).broadcast_to((P, HD, DV)), ALU.mult).then_inc(head_done, 1)

            heads(0)
            for t in range(NT + 2):
                if t + 1 < NT:
                    heads(t + 1)
                if t < NT:
                    dve.wait_ge(tm_ready, 2 * t + 2)
                    if t >= 2:
                        dve.wait_ge(o_ready, 2 * (t - 1))
                    dve.tensor_copy(mt[:, t % 2, 4:8, :], tm_ps[:, 1, :].rearrange("p (c n) -> p c n", n=P)).then_inc(mt_v, 1)
                if t < NT:
                    dve.wait_ge(x_sem[t % 2], 16 * (t // 2 + 1))
                    if t >= 2:
                        dve.wait_ge(v_done, t - 1)
                        dve.wait_ge(h2_sem[t % 2], 16 * (t // 2))
                    for b in range(2):
                        dve.wait_ge(o_ready, 2 * t + b + 1)
                        dve.tensor_tensor(h2[:, t % 2, 512 * b:512 * b + 512], o_ps[:, 2 * (t % 2) + b, :],
                                          xs[:, t % 2, 512 * b:512 * b + 512], ALU.add).then_inc(h2_done, 1)
                if t < NT:
                    dve.wait_ge(std_done, t + 1)
                    step(dve.reciprocal(rs[:, t:t + 1], rs[:, t:t + 1]))
                    dve.scalar_tensor_tensor(out=vs[:, t % 2, :], in0=h2[:, t % 2, :], scalar=rs[:, t:t + 1], in1=gf[:, :],
                                             op0=ALU.mult, op1=ALU.mult).then_inc(v_done, 1)
                if 1 <= t <= NT:
                    u = t - 1
                    dve.wait_ge(r_ready, u + 1)
                    step(dve.tensor_tensor(lg[:, :], r_ps[:, 0:N_EXP], br[:, :], ALU.add))
                    step(dve.max(top[:, u, :], lg[:, :]))
                    step(dve.max_index(idx[:, :], top[:, u, :], lg[:, :]))
                    step(dve.tensor_copy(idf[:, :], idx[:, :]))
                    for k in range(TOP_K):
                        ins = dve.tensor_scalar(oh[:, k, :], cst[:, C_EXP:C_EXP + N_EXP], idf[:, k:k + 1], None, ALU.is_equal)
                    step(ins)
                    dve.tensor_reduce(sel[:, :], oh[:, :, :].rearrange("p k e -> p e k"), AX.X, ALU.add).then_inc(sel_done, 1)
                    dve.wait_ge(rank_ready, u + 1)
                    step(dve.tensor_tensor(pos[:, :], r_ps[:, 32:64], cst[:, C_BASE:C_BASE + N_EXP], ALU.add))
                    for k in range(TOP_K):
                        step(dve.tensor_tensor_reduce(junk[:, :], oh[:, k, :], pos[:, :], 1.0, 0.0, ALU.mult, ALU.add,
                                                      dst[:, u, k:k + 1]))
                    step(dve.tensor_tensor(acc[:, :], acc[:, :], sel[:, :], ALU.add))
                    dve.tensor_copy(dsti[:, u, :], dst[:, u, :]).then_inc(dst_done, 1)
            dve.tensor_tensor(gates[:, :, :], top[:, :, 0:TOP_K], top[:, :, 0:1].broadcast_to((P, NT, TOP_K)),
                              ALU.subtract).then_inc(gates_in, 1)
            dve.wait_ge(gates_exp, 1)
            step(dve.tensor_reduce(gsum[:, :], gates[:, :, :], AX.X, ALU.add))
            step(dve.reciprocal(gsum[:, :], gsum[:, :]))
            step(dve.tensor_tensor(gates[:, :, :], gates[:, :, :], gsum[:, :].unsqueeze(2).broadcast_to((P, NT, TOP_K)), ALU.mult))
            step(dve.memset(ec[:, :], 1.0))
            dve.wait_ge(cnt_ready, 1)
            step(dve.tensor_copy(ec[:, 2:3], r_ps[0:N_EXP, 64:65]))
            step(dve.tensor_scalar(ej[:, 0, 0:4], cst[0:N_EXP, C_STEP:C_STEP + 4], ec[:, 2:3], None, ALU.is_lt))
            dve.tensor_reduce(ec[:, 1:2], ej[:, 0, 0:4], AX.X, ALU.add).then_inc(jobs_step, 1)
            dve.wait_ge(jobs_step, 1)
            dve.wait_ge(cnt_ready, 2)
            step(dve.tensor_copy(ec[:, 4:5], r_ps[0:N_EXP, 65:66]))
            step(dve.tensor_tensor(ec[:, 3:4], ec[:, 4:5], ec[:, 1:2], ALU.add))
            step(dve.tensor_scalar(ej[:, 0, :], cst[0:N_EXP, C_JOB:C_JOB + NJ], ec[:, 3:4], None, ALU.is_ge))
            step(dve.tensor_scalar(ej[:, 1, :], cst[0:N_EXP, C_JOB:C_JOB + NJ], ec[:, 4:5], None, ALU.is_ge))
            dve.tensor_tensor(ej[:, 2, :], ej[:, 1, :], ej[:, 0, :], ALU.subtract).then_inc(jobs_step, 1)
            dve.wait_ge(cnt_ready, 3)
            step(dve.tensor_copy(jf[0:1, 0:3, :], r_ps[0:1, 128:128 + 3 * NJ].rearrange("p (r n) -> p r n", n=NJ)))
            step(dve.tensor_tensor(jf[0:1, 3, :], cst[0:1, C_JOB:C_JOB + NJ], jf[0:1, 1, :], ALU.subtract))
            step(dve.scalar_tensor_tensor(out=jf[0:1, 4, :], in0=jf[0:1, 3, :], scalar=-float(JOB), in1=jf[0:1, 2, :],
                                          op0=ALU.mult, op1=ALU.add))
            step(dve.tensor_scalar(jf[0:1, 5, :], jf[0:1, 4, :], float(P), None, ALU.is_gt))
            step(dve.tensor_scalar(jf[0:1, 0, :], jf[0:1, 0, :], float(N_EXP - 1), None, ALU.min))
            step(dve.tensor_scalar(jf[0:1, 3, :], jf[0:1, 3, :], 3.0, None, ALU.min))
            step(dve.tensor_scalar(jf[0:1, 3, :], jf[0:1, 3, :], float(JOB), None, ALU.mult))
            step(dve.scalar_tensor_tensor(out=jf[0:1, 4, :], in0=jf[0:1, 0, :], scalar=float(CAP), in1=jf[0:1, 3, :],
                                          op0=ALU.mult, op1=ALU.add))
            step(dve.tensor_copy(jobs[0:1, 0, :], jf[0:1, 0, :]))
            step(dve.tensor_copy(jobs[0:1, 1, :], jf[0:1, 4, :]))
            step(dve.tensor_copy(jobs[0:1, 2, :], jf[0:1, 5, :]))
            step(dve.tensor_copy(jobs[0:1, 3, 0:1], r_ps[0:1, 127:128]))

        @block.tensor
        def _(pe):
            ident = cst[:, C_ID:C_ID + P]
            pe.wait_ge(landed, 16 * NL)
            pe.wait_ge(ones_set, 1)

            def transpose_mixed(t):
                pe.wait_ge(head_done, t + 1)
                for b in range(2):
                    if t >= 1:
                        pe.wait_ge((mt_a, mt_v)[b], t)
                    for c in range(4):
                        k = 4 * b + c
                        ins = pe.transpose(tm_ps[:, b, c * P:(c + 1) * P], mixed[:, t, k * P:(k + 1) * P], ident)
                    ins.then_inc(tm_ready, 1)

            def project_out(t):
                pe.wait_ge(mt_a, t + 1)
                pe.wait_ge(mt_v, t + 1)
                if t >= 2:
                    pe.wait_ge(h2_done, 2 * (t - 1))
                for b in range(2):
                    for k in range(KC):
                        ins = pe.matmul(o_ps[:, 2 * (t % 2) + b, :], mt[:, t % 2, k, :], w_sb[:, k, 512 * b:512 * b + 512],
                                        start=(k == 0), stop=(k == KC - 1))
                    ins.then_inc(o_ready, 1)

            def router(t):
                pe.wait_ge(v_done, t + 1)
                for b in range(2):
                    if 2 * t + b >= 1:
                        pe.wait_ge(vt_done, 2 * t + b)
                    for c in range(4):
                        k = 4 * b + c
                        ins = pe.transpose(tv_ps[:, c * P:(c + 1) * P], vs[:, t % 2, k * P:(k + 1) * P], ident)
                    ins.then_inc(tv_ready, 1)
                pe.wait_ge(vt_done, 2 * t + 2)
                if t >= 1:
                    pe.wait_ge(dst_done, t)
                for k in range(KC):
                    ins = pe.matmul(r_ps[:, 0:N_EXP], vt[:, k, :], wr[:, k, :], start=(k == 0), stop=(k == KC - 1))
                ins.then_inc(r_ready, 1)
                pe.wait_ge(sel_done, t + 1)
                pe.matmul(r_ps[:, 32:64], ones[:, :], acc[:, :], start=True, stop=False)
                pe.matmul(r_ps[:, 32:64], cst[:, C_TRI:C_TRI + P], sel[:, :], start=False, stop=True).then_inc(rank_ready, 1)

            transpose_mixed(0)
            for t in range(NT):
                project_out(t)
                if t + 1 < NT:
                    transpose_mixed(t + 1)
                if t >= 1:
                    router(t - 1)
            router(NT - 1)
            pe.wait_ge(dst_done, NT)
            pe.matmul(r_ps[0:N_EXP, 64:65], acc[:, :], ones[:, 0:1], start=True, stop=True).then_inc(cnt_ready, 1)
            pe.wait_ge(jobs_step, 1)
            pe.matmul(r_ps[0:1, 127:128], ec[:, 1:2], ones[0:N_EXP, 0:1], start=True, stop=True)
            pe.matmul(r_ps[0:N_EXP, 65:66], cst[0:N_EXP, C_TRI:C_TRI + N_EXP], ec[:, 1:2], start=True, stop=True
                      ).then_inc(cnt_ready, 1)
            pe.wait_ge(jobs_step, 2)
            pe.matmul(r_ps[0:1, 128:128 + NJ], ones[0:N_EXP, 0:1], ej[:, 0, :], start=True, stop=True)
            pe.matmul(r_ps[0:1, 128 + NJ:128 + 2 * NJ], ec[:, 1:2], ej[:, 0, :], start=True, stop=True)
            pe.matmul(r_ps[0:1, 128 + 2 * NJ:128 + 3 * NJ], ec[:, 2:3], ej[:, 2, :], start=True, stop=True).then_inc(cnt_ready, 1)


def experts(nc, a, jobs, v_dram, slot_dram, y_dram):
    with ExitStack() as ctx:
        sb = lambda n, s, d=F32: ctx.enter_context(nc.sbuf_tensor(n, s, d))
        sem = lambda n: ctx.enter_context(nc.semaphore(n))
        ps = lambda n, s: ctx.enter_context(nc.psum_tensor(n, s, F32))
        NC, NP = 6, 12
        RAW, SPL, AHEAD = 3, 4, 3
        PK = KC // 2
        raw = sb("raw", [P, RAW, KC, 512])
        whi = sb("whi", [P, SPL, PK, 512], F32R)
        wlo = sb("wlo", [P, SPL, PK, 512], F32R)
        xg = sb("xg", [P, 2, D])
        xt_hi = sb("xt_hi", [P, 2, KC, P], F32R)
        xt_lo = sb("xt_lo", [P, 2, KC, P], F32R)
        ht_hi = sb("ht_hi", [P, 2, KC, P], F32R)
        ht_lo = sb("ht_lo", [P, 2, KC, P], F32R)
        gl = sb("gl", [P, 512])
        gc = sb("gc", [P, 256])
        sg = sb("sg", [P, 256])
        hh = sb("hh", [P, 2, 2, 256])
        ys = sb("ys", [P, 2, D])
        brow = sb("brow", [1, 3 * D])
        bias = sb("bias", [P, 3 * D])
        idn = sb("idn", [P, 2, 2], U32)
        idc = sb("idc", [P, 2], U32)
        ident = sb("ident5", [P, P])
        m_ps = ps("m_ps", [P, 4, 512])
        y_ps = ps("y_ps", [P, 2, 512])
        t_ps = ps("t5_ps", [P, 2, 512])

        w_sem = [sem(f"w_landed{i}") for i in range(RAW)]
        ident_landed, setup = sem("ident_landed"), sem("setup5")
        hi_done, lo_done, w_used, a_ready = sem("hi_split"), sem("lo_split"), sem("w_used"), sem("a_ready")
        m_read = [sem("m_read_a"), sem("m_read_b")]
        g_ready, sig_done = [sem("g_ready_a"), sem("g_ready_b")], [sem("sig_a"), sem("sig_b")]
        h_ready = [sem("h_ready_a"), sem("h_ready_b")]
        t_ready = [sem("t_ready_a"), sem("t_ready_b")]
        t_hi, t_lo = [sem("t_hi_a"), sem("t_hi_b")], [sem("t_lo_a"), sem("t_lo_b")]
        y_done = [sem("y_done_a"), sem("y_done_b")]
        y_stored = [sem("y_stored_a"), sem("y_stored_b")]
        x_landed = [sem("x_gathered_a"), sem("x_gathered_b")]
        idx_landed, idx_kept, brow_landed = sem("idx_landed"), sem("idx_kept"), sem("brow_landed")
        bias1, bias2 = sem("bias1_spread"), sem("bias2_spread")
        dve_chain = sem("dve_chain5")
        passed = sem("wait_passed")
        block = ctx.enter_context(nc.Block())

        w1 = a["w_mlp1"][0].rearrange("e (k p) (s c n) -> e p k s c n", p=P, s=2, c=4)
        w2 = a["w_mlp2"][0].rearrange("e (k p) (c n) -> e p k c n", p=P, c=2)
        M_BANK = lambda c, half: 2 * (c % 2) + half
        L = bass.ds

        def job_value(eng, row, j, top):
            return eng.value_load(jobs[0:1, row, L(j, 1)], min_val=0, max_val=top)

        def job_count(eng):
            return eng.value_load(jobs[0:1, 3, 0:1], min_val=1, max_val=MAX_JOBS)

        @block.sync
        def _(sp):
            sp.dma_start(ident[:, :], a["consts"][:, C_ID:C_ID + P]).then_inc(ident_landed, 16)

            def load(c, e):
                s = c % RAW
                if c % NC < 4:
                    for part in range(2):
                        dst = raw[:, s, :, 256 * part:256 * part + 256]
                        sp.dma_start(dst, w1[L(e, 1), :, :, part, c % NC, :].rearrange("o p k n -> (o p) k n")
                                     ).then_inc(w_sem[s], 16)
                else:
                    for part in range(2):
                        sp.dma_start(raw[:, s, 4 * part:4 * part + 4, :],
                                     w2[L(e, 1), :, 4 * part:4 * part + 4, c % NC - 4, :].rearrange("o p k n -> (o p) k n")
                                     ).then_inc(w_sem[s], 16)
            n = job_count(sp)
            e0 = job_value(sp, 0, 0, N_EXP - 1)
            load(0, e0)
            load(1, e0)
            with sp.Fori(0, n) as j:
                e = job_value(sp, 0, j, N_EXP - 1)
                nxt = job_value(sp, 0, j + 1, N_EXP - 1)
                for c in range(2, NC + 2):
                    sp.wait_ge(hi_done, j * NP + (2 * c + 2))
                    sp.wait_ge(lo_done, j * NP + (2 * c + 2))
                    load(c, e if c < NC else nxt)
            sp.wait_ge(w_sem[0], n * 64 + 32)
            sp.wait_ge(w_sem[1], n * 64 + 32)
            sp.wait_ge(w_sem[2], n * 64)
            sp.sem_inc(passed, 1)

        @block.gpsimd
        def _(pool):
            pool.memset(xg[:, :, :], 0.0).then_inc(setup, 1)
            pool.memset(ys[:, :, :], 0.0).then_inc(setup, 1)
            pool.wait_ge(setup, 2)

            def load_idx(j):
                base = job_value(pool, 1, j, N_EXP * CAP - JOB)
                src = slot_dram[L(base, JOB), :].rearrange("(h p) c -> p h c", p=P)
                pool.dma_start(idn[:, :, :], src).then_inc(idx_landed, 16)

            def gather():
                for half in range(2):
                    pool.indirect_dma_start(out=xg[:, half, :], out_offset=None, in_=v_dram[:, :],
                                            in_offset=bass.IndirectOffsetOnAxis(ap=idn[:, half, 1:2], axis=0),
                                            bounds_check=SEQ - 1, oob_is_err=False).then_inc(x_landed[half], 16)

            def load_bias(e):
                for s in range(2):
                    pool.dma_start(brow[0:1, 0:2 * D].rearrange("p (c s n) -> p s c n", c=4, s=2)[:, s],
                                   a["b_mlp1"][0][L(e, 1), s * D:(s + 1) * D].rearrange("o (c n) -> o c n", c=4)
                                   ).then_inc(brow_landed, 16)
                pool.dma_start(brow[0:1, 2 * D:3 * D], a["b_mlp2"][0][L(e, 1), :]).then_inc(brow_landed, 16)

            load_idx(0)
            pool.wait_ge(idx_landed, 16)
            gather()
            load_bias(job_value(pool, 0, 0, N_EXP - 1))
            pool.tensor_copy(idc[:, :], idn[:, :, 0]).then_inc(idx_kept, 1)
            pool.wait_ge(brow_landed, 48)
            pool.partition_broadcast(bias[:, 0:2 * D], brow[0:1, 0:2 * D]).then_inc(bias1, 1)
            pool.partition_broadcast(bias[:, 2 * D:3 * D], brow[0:1, 2 * D:3 * D]).then_inc(bias2, 1)
            n = job_count(pool)
            with pool.Fori(0, n) as j:
                for half in range(2):
                    pool.wait_ge(x_landed[half], j * 16 + 16)
                pool.wait_ge(idx_kept, j + 1)
                pool.sem_inc(passed, 1)
                load_idx(j + 1)
                pool.wait_ge(idx_landed, j * 16 + 32)
                for half in range(2):
                    pool.wait_ge(t_ready[half], j * 6 + 2)
                pool.sem_inc(passed, 1)
                gather()
                pool.wait_ge(bias1, j + 1)
                pool.wait_ge(bias2, j + 1)
                pool.sem_inc(passed, 1)
                load_bias(job_value(pool, 0, j + 1, N_EXP - 1))
                pool.wait_ge(brow_landed, j * 48 + 96)
                for half in range(2):
                    pool.wait_ge(m_read[half], j * 4 + 6)
                pool.sem_inc(passed, 1)
                pool.partition_broadcast(bias[:, 0:2 * D], brow[0:1, 0:2 * D]).then_inc(bias1, 1)
                for half in range(2):
                    pool.wait_ge(y_done[half], j * 2 + 4)
                    pool.sem_inc(passed, 1)
                    pool.indirect_dma_start(out=y_dram[:, :],
                                            out_offset=bass.IndirectOffsetOnAxis(ap=idc[:, half:half + 1], axis=0),
                                            in_=ys[:, half, :], in_offset=None,
                                            bounds_check=SEQ * TOP_K - 1, oob_is_err=False).then_inc(y_stored[half], 16)
                pool.partition_broadcast(bias[:, 2 * D:3 * D], brow[0:1, 2 * D:3 * D]).then_inc(bias2, 1)
                for half in range(2):
                    pool.wait_ge(y_stored[half], j * 16 + 16)
                pool.sem_inc(passed, 1)
                pool.tensor_copy(idc[:, :], idn[:, :, 0]).then_inc(idx_kept, 1)
            for half in range(2):
                pool.wait_ge(x_landed[half], n * 16 + 16)
                pool.wait_ge(idx_landed, n * 16 + 16)
            pool.sem_inc(passed, 1)

        @block.scalar
        def _(act):
            act.sem_inc(hi_done, 2 * RAW)

            def split(j, k):
                s, c = k % SPL, k // 2
                act.wait_ge(w_sem[c % RAW], j * 64 + 32 * (c // RAW + 1))
                act.wait_ge(w_used, j * NP + (k + 1))
                act.copy(whi[:, s, :, :], raw[:, c % RAW, PK * (k % 2):PK * (k % 2) + PK, :]).then_inc(hi_done, 1)

            def keep_hi(half, buf, k0, n, j, g):
                act.wait_ge(t_ready[half], j * 6 + (g + 3))
                act.copy(buf[:, half, k0:k0 + n, :], t_ps[:, half, 0:n * P].rearrange("p (k m) -> p k m", m=P)
                         ).then_inc(t_hi[half], 1)

            def body(j, halves):
                for k in range(NP):
                    c = k // 2
                    if k == 2 and len(halves) == 1:
                        act.wait_ge(t_hi[1], j * 6 + 2)
                        act.sem_inc(sig_done[1], 4)
                        act.sem_inc(t_hi[1], 4)
                    if k % 2 == 0 and 1 <= c <= 4:
                        for half in halves:
                            act.wait_ge(g_ready[half], j * 4 + c)
                            act.activation(sg[:, :], gc[:, :], ACT.Sigmoid, scale=ALPHA).then_inc(sig_done[half], 1)
                    if k % 2 == 1 and 1 <= c <= 4:
                        for half in halves:
                            keep_hi(half, ht_hi, 2 * (c - 1), 2, j, c - 1)
                    if k == 11:
                        for half in range(2):
                            keep_hi(half, xt_hi, 0, 4, j, 4)
                    split(j, k + AHEAD)
                for half in range(2):
                    keep_hi(half, xt_hi, 4, 4, j, 5)

            for g in range(2):
                for half in range(2):
                    act.wait_ge(t_ready[half], g + 1)
                    act.copy(xt_hi[:, half, 4 * g:4 * g + 4, :], t_ps[:, half, :].rearrange("p (k m) -> p k m", m=P)
                             ).then_inc(t_hi[half], 1)
            for k in range(AHEAD):
                split(0, k)
            n = job_count(act)
            with act.Fori(0, n) as j:
                both = job_value(act, 2, j, 1)
                with act.If(both > 0):
                    body(j, (0, 1))
                with act.Else():
                    body(j, (0,))

        @block.vector
        def _(dve):
            dve.sem_inc(lo_done, 2 * RAW)
            for half in range(2):
                dve.sem_inc(m_read[half], 2)
                dve.sem_inc(y_done[half], 2)

            def split(j, k):
                s, c = k % SPL, k // 2
                dve.wait_ge(hi_done, j * NP + (2 * RAW + k + 1))
                dve.tensor_tensor(wlo[:, s, :, :], raw[:, c % RAW, PK * (k % 2):PK * (k % 2) + PK, :],
                                  whi[:, s, :, :].bitcast(F32), ALU.subtract).then_inc(lo_done, 1)

            def keep_lo(half, hi, lo, k0, n, j, g):
                dve.wait_ge(t_hi[half], j * 6 + (g + 3))
                dve.tensor_tensor(lo[:, half, k0:k0 + n, :], t_ps[:, half, 0:n * P].rearrange("p (k m) -> p k m", m=P),
                                  hi[:, half, k0:k0 + n, :].bitcast(F32), ALU.subtract).then_inc(t_lo[half], 1)

            def products(j, c, half, halves):
                if half == halves[-1]:
                    dve.wait_ge(w_used, j * NP + (SPL + 2 * c + 2))
                else:
                    dve.wait_ge(a_ready, j * NC + (c + 1))

            def swiglu(j, c, half, halves, at):
                products(j, c, half, halves)
                if c == 0:
                    dve.wait_ge(bias1, j + 1)
                if c >= 2:
                    dve.wait_ge(t_ready[half], j * 6 + (c + 1))
                dve.tensor_tensor(gl[:, :], m_ps[:, M_BANK(c, half), :], bias[:, 512 * c:512 * c + 512], ALU.add
                                  ).then_inc(m_read[half], 1)
                dve.wait_ge(m_read[half], j * 4 + (c + 3))
                dve.tensor_scalar(gc[:, :], gl[:, 0:256], LIMIT, None, ALU.min).then_inc(g_ready[half], 1)
                dve.tensor_scalar(gl[:, 256:512], gl[:, 256:512], LIMIT, -LIMIT, ALU.min, ALU.max).then_inc(dve_chain, 1)
                dve.wait_ge(dve_chain, at + 1)
                dve.wait_ge(g_ready[half], j * 4 + (c + 1))
                dve.scalar_tensor_tensor(out=gl[:, 0:256], in0=gl[:, 256:512], scalar=1.0, in1=gc[:, :],
                                         op0=ALU.add, op1=ALU.mult).then_inc(dve_chain, 1)
                dve.wait_ge(dve_chain, at + 2)
                dve.wait_ge(sig_done[half], j * 4 + (c + 1))
                dve.tensor_tensor(hh[:, half, c % 2, :], gl[:, 0:256], sg[:, :], ALU.mult).then_inc(h_ready[half], 1)
                dve.wait_ge(h_ready[half], j * 4 + (c + 1))

            def finish(j, q, half, halves):
                products(j, 4 + q, half, halves)
                if q == 0:
                    dve.wait_ge(bias2, j + 1)
                    dve.wait_ge(idx_kept, j + 1)
                src = y_ps[:, q, :] if half == 0 else m_ps[:, 2 * q + 1, :]
                dve.tensor_tensor(ys[:, half, 512 * q:512 * q + 512], src, bias[:, 2 * D + 512 * q:2 * D + 512 * q + 512],
                                  ALU.add).then_inc(y_done[half], 1)

            def body(j, halves):
                for k in range(NP):
                    c = k // 2
                    if k == 2 and len(halves) == 1:
                        dve.wait_ge(t_lo[1], j * 6 + 2)
                        dve.wait_ge(y_done[1], j * 2 + 2)
                        for s, m in ((m_read, 4), (g_ready, 4), (h_ready, 4), (t_lo, 4), (y_done, 2)):
                            dve.sem_inc(s[1], m)
                    if k % 2 == 0 and 1 <= c <= 4:
                        for half in halves:
                            swiglu(j, c - 1, half, halves, j * 16 + 4 * (c - 1) + 2 * half)
                        if len(halves) == 1:
                            dve.sem_inc(dve_chain, 2)
                    if k % 2 == 1 and 1 <= c <= 4:
                        for half in halves:
                            keep_lo(half, ht_hi, ht_lo, 2 * (c - 1), 2, j, c - 1)
                    if k == 11:
                        for half in range(2):
                            keep_lo(half, xt_hi, xt_lo, 0, 4, j, 4)
                        for half in halves:
                            finish(j, 0, half, halves)
                    split(j, k + AHEAD)
                for half in range(2):
                    keep_lo(half, xt_hi, xt_lo, 4, 4, j, 5)
                for half in halves:
                    finish(j, 1, half, halves)

            for g in range(2):
                for half in range(2):
                    dve.wait_ge(t_hi[half], g + 1)
                    dve.tensor_tensor(xt_lo[:, half, 4 * g:4 * g + 4, :], t_ps[:, half, :].rearrange("p (k m) -> p k m", m=P),
                                      xt_hi[:, half, 4 * g:4 * g + 4, :].bitcast(F32), ALU.subtract).then_inc(t_lo[half], 1)
            for k in range(AHEAD):
                split(0, k)
            n = job_count(dve)
            with dve.Fori(0, n) as j:
                both = job_value(dve, 2, j, 1)
                with dve.If(both > 0):
                    body(j, (0, 1))
                with dve.Else():
                    body(j, (0,))

        @block.tensor
        def _(pe):
            pe.sem_inc(w_used, SPL)

            def transpose_x(half, g):
                for c in range(4):
                    k = 4 * g + c
                    ins = pe.transpose(t_ps[:, half, c * P:(c + 1) * P], xg[:, half, k * P:(k + 1) * P], ident[:, :])
                ins.then_inc(t_ready[half], 1)

            def transpose_h(j, c, half):
                pe.wait_ge(h_ready[half], j * 4 + (c + 1))
                pe.wait_ge(t_lo[half], j * 6 + (c + 2))
                for i in range(2):
                    ins = pe.transpose(t_ps[:, half, i * P:(i + 1) * P], hh[:, half, c % 2, i * P:(i + 1) * P], ident[:, :])
                ins.then_inc(t_ready[half], 1)

            def multiply(j, k, half):
                c, s = k // 2, k % SPL
                first = k < 8
                xh, xl = (xt_hi, xt_lo) if first else (ht_hi, ht_lo)
                if first:
                    bank = m_ps[:, M_BANK(c, half), :]
                else:
                    bank = y_ps[:, c - 4, :] if half == 0 else m_ps[:, 2 * (c - 4) + 1, :]
                if k % 2 == 0:
                    if first:
                        pe.wait_ge(m_read[half], j * 4 + (c + 1))
                    elif half == 0:
                        pe.wait_ge(y_done[0], j * 2 + (c - 3))
                    else:
                        pe.wait_ge(m_read[1], j * 4 + (c + 1))
                    if half == 1 and k in (0, 2):
                        pe.wait_ge(y_done[1], j * 2 + 2)
                need = {0: 1, 1: 2, 8: 4, 9: 6}.get(k)
                if need is not None:
                    pe.wait_ge(t_lo[half], j * 6 + need)
                n = 0
                for i in range(PK):
                    kc = PK * (k % 2) + i
                    for x, w in ((xh, whi), (xh, wlo), (xl, whi)):
                        n += 1
                        ins = pe.matmul(bank, x[:, half, kc, :], w[:, s, i, :], start=(k % 2 == 0 and n == 1),
                                        stop=(k % 2 == 1 and n == 3 * PK), skip_group_check=True)
                return ins

            def body(j, halves):
                for k in range(NP):
                    c = k // 2
                    pe.wait_ge(hi_done, j * NP + (2 * RAW + k + 1))
                    pe.wait_ge(lo_done, j * NP + (2 * RAW + k + 1))
                    if k == 2 and len(halves) == 1:
                        skip_b(j)
                    for half in halves:
                        ins = multiply(j, k, half)
                        if half != halves[-1] and k % 2 == 1:
                            ins.then_inc(a_ready, 1)
                    ins.then_inc(w_used, 1)
                    if k % 2 == 0 and 1 <= c <= 4:
                        for half in halves:
                            transpose_h(j, c - 1, half)
                    if k >= 10:
                        for half in range(2):
                            if k == 10:
                                pe.wait_ge(x_landed[half], j * 16 + 32)
                                pe.wait_ge(t_lo[half], j * 6 + 6)
                            else:
                                pe.wait_ge(t_lo[half], j * 6 + 7)
                            transpose_x(half, k - 10)

            def skip_b(j):
                pe.wait_ge(t_lo[1], j * 6 + 2)
                pe.wait_ge(y_done[0], j * 2 + 2)
                pe.sem_inc(t_ready[1], 4)
                pe.sem_inc(a_ready, NC)

            pe.wait_ge(ident_landed, 16)
            for g in range(2):
                for half in range(2):
                    if g == 0:
                        pe.wait_ge(x_landed[half], 16)
                    else:
                        pe.wait_ge(t_lo[half], 1)
                    transpose_x(half, g)
            n = job_count(pe)
            with pe.Fori(0, n) as j:
                both = job_value(pe, 2, j, 1)
                with pe.If(both > 0):
                    body(j, (0, 1))
                with pe.Else():
                    body(j, (0,))


def combine(nc, gates, h2_dram, y_dram, out):
    with ExitStack() as ctx:
        sb = lambda n, s, d=F32: ctx.enter_context(nc.sbuf_tensor(n, s, d))
        sem = lambda n: ctx.enter_context(nc.semaphore(n))
        yk = sb("yk", [P, 2, TOP_K * D])
        h2 = sb("h2_in", [P, 2, D])
        y_sem = [sem(f"yk_landed{i}") for i in range(2)]
        o_sem = [sem(f"out_stored{i}") for i in range(2)]
        added = sem("added")
        block = ctx.enter_context(nc.Block())

        @block.sync
        def _(sp):
            for t in range(NT):
                b = t % 2
                if t >= 2:
                    sp.wait_ge(added, TOP_K * (t - 1))
                    sp.wait_ge(o_sem[b], 16 * (t // 2))
                sp.dma_start(yk[:, b, :], y_dram[t * P * TOP_K:(t + 1) * P * TOP_K, :].rearrange("(p k) d -> p (k d)", k=TOP_K)
                             ).then_inc(y_sem[b], 16)
                sp.dma_start(h2[:, b, :], h2_dram[t * P:(t + 1) * P, :]).then_inc(y_sem[b], 16)

        @block.scalar
        def _(act):
            for t in range(NT):
                act.wait_ge(added, TOP_K * (t + 1))
                act.dma_start(out[0, t * P:(t + 1) * P, :], h2[:, t % 2, :]).then_inc(o_sem[t % 2], 16)
            for b in range(2):
                act.wait_ge(o_sem[b], 16 * (NT // 2))

        @block.vector
        def _(dve):
            for t in range(NT):
                b = t % 2
                dve.wait_ge(y_sem[b], 32 * (t // 2 + 1))
                for k in range(TOP_K):
                    if k:
                        dve.wait_ge(added, TOP_K * t + k)
                    dve.scalar_tensor_tensor(out=h2[:, b, :], in0=yk[:, b, k * D:(k + 1) * D], scalar=gates[:, t, k:k + 1],
                                             in1=h2[:, b, :], op0=ALU.mult, op1=ALU.add).then_inc(added, 1)


def build(nc, a, out):
    dram = lambda n, s, d=F32: nc.dram_tensor(n, s, d, kind="Internal").ap()
    qk_dram = dram("qk_dram", [2, R_W, KEYS])
    h2_dram, v_dram = dram("h2_dram", [SEQ, D]), dram("v_dram", [SEQ, D])
    y_dram = dram("y_dram", [SEQ * TOP_K, D])
    slot_dram = dram("slot_dram", [N_EXP * CAP, 2], U32)
    with nc.sbuf_tensor("gates", [P, NT, TOP_K], F32) as gates, nc.sbuf_tensor("jobs", [1, 4, NJ], I32) as jobs:
        with nc.sbuf_tensor("v_all", [P, NT + 1, 640], F32) as v_all:
            project(nc, a, v_all, qk_dram)
            with nc.sbuf_tensor("mixed", [P, NT, D], F32) as mixed:
                attend_window(nc, a, v_all, mixed, qk_dram)
                attend_diff(nc, a, v_all, mixed, qk_dram)
                route(nc, a, mixed, gates, jobs, h2_dram, v_dram, slot_dram)
        experts(nc, a, jobs, v_dram, slot_dram, y_dram)
        combine(nc, gates, h2_dram, y_dram, out)


def rope_table():
    pos = np.concatenate([np.arange(N_META, KEYS), np.arange(N_META)]).astype(np.float32)
    cols = []
    for d in (DH, DQ):
        inv = (np.float32(10000.0) ** (-np.arange(0, d, 2, dtype=np.float32) / np.float32(d))).astype(np.float32)
        ang = pos[:, None] * inv[None, :]
        cols += [np.cos(ang), np.sin(ang)]
    return np.concatenate(cols, 1).astype(np.float32)


def band_masks():
    q, k = np.arange(P)[:, None], np.arange(P)[None, :]
    prev, nxt = np.where(k >= q, 0.0, NEG), np.where(k <= q, 0.0, NEG)
    m = np.zeros((P, 3, 3 * P + N_META), np.float32)
    m[:, 0, P:2 * P] = nxt
    m[:, 1, 0:P], m[:, 1, 2 * P:3 * P] = prev, nxt
    m[:, 2, 0:P] = prev
    return m


def constants():
    c = np.zeros((P, C_W), np.float32)
    i = np.arange(P)
    c[:, C_ID:C_ID + P] = np.eye(P)
    c[:, C_TRI:C_TRI + P] = i[:, None] < i[None, :]
    c[:, C_EXP:C_EXP + N_EXP] = np.arange(N_EXP)
    c[:, C_BASE:C_BASE + N_EXP] = np.arange(N_EXP) * CAP
    c[:, C_JOB:C_JOB + NJ] = np.arange(NJ)
    c[:, C_STEP:C_STEP + 4] = np.arange(4) * JOB
    return c


_INS = ["x", "meta_tokens", "g_attn", "w_in", "g_q_swa", "g_k_swa", "g_q_diff", "g_k_diff", "sink_swa",
        "lambda_q1", "lambda_k1", "lambda_q2", "lambda_k2", "g_diff_head", "w_out", "g_ffn",
        "w_router", "b_router", "w_mlp1", "b_mlp1", "w_mlp2", "b_mlp2"]


def kernel(**inputs):
    import concourse.bacc as bacc
    from concourse.bass_utils import run_bass_kernel_spmd

    nc = bacc.Bacc("TRN2", target_bir_lowering=False, num_devices=1)
    arrays = {f"in_{n}": np.ascontiguousarray(inputs[n]) for n in _INS}
    arrays |= {"in_rope": rope_table(), "in_masks": band_masks(), "in_consts": constants(),
               "in_ones": np.ones((P, P), np.float32)}
    aps = {n[3:]: nc.dram_tensor(n, v.shape, mybir.dt.from_np(v.dtype), kind="ExternalInput").ap()
           for n, v in arrays.items()}
    out = nc.dram_tensor("out_h", (1, SEQ, D), F32, kind="ExternalOutput").ap()
    build(nc, aps, out)
    r = run_bass_kernel_spmd(nc, [arrays], core_ids=[0])
    return r.results[0]["out_h"]
```

```python
import math
from contextlib import ExitStack

import numpy as np

import concourse.bass as bass
from concourse import mybir

F32 = mybir.dt.float32
F32R = mybir.dt.float32r
I32 = mybir.dt.int32
U32 = mybir.dt.uint32
ALU = mybir.AluOpType
ACT = mybir.ActivationFunctionType
AX = mybir.AxisListType

P = 128
D = 1024
KC = D // P
SEQ = 1024
NT = SEQ // P
N_META = 16
KEYS = SEQ + N_META
EPS = 1e-6
EPS_HEAD = 1e-5
HQ, HKV, DH = 8, 2, 64
G = HQ // HKV
HD, DQ, DV = 8, 32, 64
LAMBDA_INIT = 0.8 - 0.6 * math.exp(0.0)
QA, KA, VA, QD, KD, VD, IN_W = 0, 512, 640, 768, 1280, 1792, 2304
R_KA, R_QD, R_KD, R_W = 512, 640, 1152, 1664
RC = R_W // P
N_EXP, TOP_K = 32, 4
LIMIT, ALPHA = 7.0, 1.702
GLU_LIMIT = LIMIT / (1.0 + math.exp(-ALPHA * LIMIT))
CAP = SEQ
JOB = 2 * P
MAX_JOBS = N_EXP + SEQ * TOP_K // JOB - 1
NJ = 64
NEG = -1e30


def chained(eng, sem):
    n = [0]

    def step(ins):
        n[0] += 1
        ins.then_inc(sem, 1)
        eng.wait_ge(sem, n[0])
    return step


def project(nc, a, v_all, qk_dram):
    with ExitStack() as ctx:
        sb = lambda n, s, d=F32: ctx.enter_context(nc.sbuf_tensor(n, s, d))
        sem = lambda n: ctx.enter_context(nc.semaphore(n))
        w_sb = sb("w_in_sb", [P, KC, IN_W])
        xs = sb("xs", [P, 2, D])
        us = sb("us", [P, 2, D])
        ut = sb("ut", [P, 2, KC, P])
        g_sb = sb("g_attn_sb", [P, D])
        rope = sb("rope_sb", [P, NT + 1, 96])
        gains = sb("gains_sb", [P, 2, DH])
        gaind = sb("gaind_sb", [P, 2, DQ])
        ident = sb("ident1", [P, P])
        pr = sb("pr", [P, 2, IN_W])
        qn = sb("qn", [P, R_W])
        t1 = sb("t1", [P, R_W])
        t2 = sb("t2", [P, R_W])
        ro = sb("ro", [P, 2, R_W])
        hi = sb("qk_hi", [P, 2, RC, P], F32R)
        lo = sb("qk_lo", [P, 2, RC, P], F32R)
        ss = sb("ss1", [P, NT + 1])
        rs = sb("rs1", [P, NT + 1])
        hs = sb("hs", [P, 42])
        hr = sb("hr", [P, 42])
        eps = sb("eps1", [P, 1])
        ptu = ctx.enter_context(nc.psum_tensor("ptu", [P, 2, 512], F32))
        ptq = ctx.enter_context(nc.psum_tensor("ptq", [P, 2, 512], F32))
        pp = ctx.enter_context(nc.psum_tensor("pp", [P, 4, 512], F32))

        w_in_sem = [sem(f"w_landed{k}") for k in range(KC)]
        x_sem = [sem(f"x_landed{i}") for i in range(2)]
        const_landed, consts_set = sem("const_landed"), sem("consts_set")
        ss_done, std_done, rs_done, u_done = sem("ss_done"), sem("std_done"), sem("rs_done"), sem("u_done")
        ut_ps, ut_a, ut_v = sem("u_transposed"), sem("ut_copied_act"), sem("ut_copied_dve")
        proj_ps, proj_out = sem("proj_ready"), sem("proj_copied")
        sq_done, hs_done, hstd_done = sem("head_squares"), sem("head_sums"), sem("head_std")
        qn_done, gain_done, t1_done, t2_done, ro_done = (sem("qn_done"), sem("gain_done"), sem("t1_done"),
                                                        sem("t2_done"), sem("rotated"))
        qk_ps, hi_done, lo_done = sem("qk_transposed"), sem("hi_done"), sem("lo_done")
        qk_stored = [sem(f"qk_stored{i}") for i in range(2)]
        dve_chain = sem("dve_chain1")

        T = NT + 1
        rows = [P] * NT + [N_META]
        colgroups = [[(0, 512), (512, 1024), (1024, 1536), (1536, 2048), (2048, 2304)]] * NT + \
                    [[(512, 768), (1280, 1792), (1792, 2304)]]
        chunks = [list(range(RC))] * NT + [[4, 9, 10, 11, 12]]
        tgroups = [[c[i:i + 4] for i in range(0, len(c), 4)] for c in chunks]
        ngroups_before = [sum(len(x) for x in colgroups[:t]) for t in range(T + 1)]
        ntg_before = [sum(len(x) for x in tgroups[:t]) for t in range(T + 1)]
        heads_a = [(0, 10)] * NT + [(8, 10)]
        heads_d = [(0, 32)] * NT + [(16, 32)]
        gain_ops = [4] * NT + [2]

        def view_a(ap, t):
            h0, h1 = heads_a[t]
            return ap[:, h0 * DH:h1 * DH].rearrange("p (h d) -> p h d", d=DH)

        def view_d(ap, t, base):
            h0, h1 = heads_d[t]
            return ap[:, base + h0 * DQ:base + h1 * DQ].rearrange("p (h d) -> p h d", d=DQ)

        def halves(ap, t, base):
            r = rows[t]
            va = view_a(ap[0:r], t).rearrange("p h (s d) -> p h s d", s=2)
            vd = view_d(ap[0:r], t, base).rearrange("p h (s d) -> p h s d", s=2)
            return va, vd

        block = ctx.enter_context(nc.Block())

        @block.sync
        def _(sp):
            def load_x(t):
                if t >= 2:
                    sp.wait_ge(u_done, t - 1)
                src = a["x"][0, t * P:(t + 1) * P, :] if t < NT else a["meta_tokens"][:, :]
                sp.dma_start(xs[0:rows[t], t % 2, :], src).then_inc(x_sem[t % 2], 16)
            load_x(0)
            sp.dma_start(g_sb[:, :], a["g_attn"][0, :].partition_broadcast(P)).then_inc(const_landed, 16)
            sp.dma_start(ident[:, :], a["consts"][:, 0:P]).then_inc(const_landed, 16)
            load_x(1)
            for k in range(KC):
                sp.dma_start(w_sb[:, k, :], a["w_in"][0, k * P:(k + 1) * P, :]).then_inc(w_in_sem[k], 16)
                if k == 0:
                    sp.dma_start(rope[:, 0:NT, :], a["rope"][0:SEQ, :].rearrange("(t p) n -> p t n", p=P)
                                 ).then_inc(const_landed, 16)
                    sp.dma_start(rope[0:N_META, NT, :], a["rope"][SEQ:KEYS, :]).then_inc(const_landed, 16)
                    for i, n in enumerate(("g_q_swa", "g_k_swa")):
                        sp.dma_start(gains[:, i, :], a[n][0, :].partition_broadcast(P)).then_inc(const_landed, 16)
                    for i, n in enumerate(("g_q_diff", "g_k_diff")):
                        sp.dma_start(gaind[:, i, :], a[n][0, :].partition_broadcast(P)).then_inc(const_landed, 16)
            load_x(2)
            stored = [0, 0]
            for t in range(T):
                r = rows[t]
                if t + 3 < T:
                    load_x(t + 3)
                sp.wait_ge(hi_done, ntg_before[t + 1])
                sp.wait_ge(lo_done, ntg_before[t + 1])
                c0 = t * P
                for part, buf in ((0, hi), (1, lo)):
                    dst = qk_dram[part].rearrange("(c p) n -> p c n", p=P)[:, :, c0:c0 + r]
                    for x0, x1 in ([(0, RC)] if t < NT else [(4, 5), (9, 13)]):
                        sp.dma_start(dst[:, x0:x1, :], buf[:, t % 2, x0:x1, 0:r].bitcast(F32)).then_inc(qk_stored[t % 2], 16)
                        stored[t % 2] += 16
            for i in range(2):
                sp.wait_ge(qk_stored[i], stored[i])

        stored_before = [0 if t < 2 else 32 * (t // 2) for t in range(T)]

        @block.scalar
        def _(act):
            def norm(t):
                r = rows[t]
                act.wait_ge(x_sem[t % 2], 16 * (t // 2 + 1))
                if t >= 2:
                    act.wait_ge(ut_ps, 2 * (t - 1))
                act.activation(us[0:r, t % 2, :], xs[0:r, t % 2, :], ACT.Square, accum_out=ss[0:r, t:t + 1]).then_inc(ss_done, 1)
                act.wait_ge(ss_done, t + 1)
                act.wait_ge(consts_set, 1)
                act.activation(rs[0:r, t:t + 1], ss[0:r, t:t + 1], ACT.Sqrt, bias=eps[0:r], scale=1.0 / D
                               ).then_inc(std_done, 1)

            def copy_ut(t):
                r = rows[t]
                act.wait_ge(ut_ps, 2 * t + 1)
                if t >= 2:
                    act.wait_ge(proj_ps, ngroups_before[t - 1])
                act.copy(ut[:, t % 2, 0:4, 0:r], ptu[:, 0, :].rearrange("p (c n) -> p c n", n=P)[:, :, 0:r]
                         ).then_inc(ut_a, 1)

            def copy_hi(t):
                r = rows[t]
                if t >= 2:
                    act.wait_ge(qk_stored[t % 2], stored_before[t])
                for i, cs in enumerate(tgroups[t]):
                    n = ntg_before[t] + i
                    act.wait_ge(qk_ps, n + 1)
                    runs = [cs] if cs[-1] - cs[0] == len(cs) - 1 else [cs[:1], cs[1:]]
                    at = 0
                    for run in runs:
                        ins = act.copy(hi[:, t % 2, run[0]:run[-1] + 1, 0:r],
                                       ptq[:, n % 2, at * P:(at + len(run)) * P].rearrange("p (c n) -> p c n", n=P)[:, :, 0:r])
                        at += len(run)
                    ins.then_inc(hi_done, 1)

            norm(0)
            copy_ut(0)
            for t in range(T):
                r = rows[t]
                if t + 1 < T:
                    norm(t + 1)
                if t >= 2:
                    act.wait_ge(ro_done, 4 * (t - 1))
                for i, (c0, c1) in enumerate(colgroups[t]):
                    n = ngroups_before[t] + i
                    act.wait_ge(proj_ps, n + 1)
                    act.copy(pr[0:r, t % 2, c0:c1], pp[0:r, n % 4, 0:c1 - c0]).then_inc(proj_out, 1)
                    if i == 2 and t + 1 < T:
                        copy_ut(t + 1)
                if t >= 1:
                    copy_hi(t - 1)
                act.wait_ge(hs_done, t + 1)
                act.activation(hr[0:r, :], hs[0:r, :], ACT.Sqrt, bias=eps[0:r]).then_inc(hstd_done, 1)
            copy_hi(T - 1)

        @block.vector
        def _(dve):
            step = chained(dve, dve_chain)
            dve.memset(hs[:, :], 1.0)
            dve.memset(eps[:, :], EPS).then_inc(consts_set, 1)
            dve.wait_ge(const_landed, 16 * 8)
            step(dve.tensor_scalar(gains[:, 0, :], gains[:, 0, :], DH ** -0.5, None, ALU.mult))
            step(dve.tensor_scalar(gaind[:, 0, :], gaind[:, 0, :], DQ ** -0.5, None, ALU.mult))

            def norm(t):
                r = rows[t]
                dve.wait_ge(std_done, t + 1)
                dve.reciprocal(rs[0:r, t:t + 1], rs[0:r, t:t + 1]).then_inc(rs_done, 1)
                dve.wait_ge(rs_done, t + 1)
                if t >= 2:
                    dve.wait_ge(ut_ps, 2 * (t - 1))
                dve.scalar_tensor_tensor(out=us[0:r, t % 2, :], in0=xs[0:r, t % 2, :], scalar=rs[0:r, t:t + 1],
                                         in1=g_sb[0:r, :], op0=ALU.mult, op1=ALU.mult).then_inc(u_done, 1)

            def copy_ut(t):
                r = rows[t]
                dve.wait_ge(ut_ps, 2 * t + 2)
                if t >= 2:
                    dve.wait_ge(proj_ps, ngroups_before[t - 1])
                dve.tensor_copy(ut[:, t % 2, 4:8, 0:r], ptu[:, 1, :].rearrange("p (c n) -> p c n", n=P)[:, :, 0:r]
                                ).then_inc(ut_v, 1)

            def head_sums(t):
                r = rows[t]
                (a0, a1), (d0, d1) = heads_a[t], heads_d[t]
                dve.wait_ge(sq_done, 2 * (t + 1))
                step(dve.tensor_reduce(hs[0:r, a0:a1], view_a(t1[0:r], t), AX.X, ALU.add))
                step(dve.tensor_reduce(hs[0:r, 10 + d0:10 + d1], view_d(t1[0:r], t, R_QD), AX.X, ALU.add))
                step(dve.tensor_scalar(hs[0:r, a0:a1], hs[0:r, a0:a1], 1.0 / DH, None, ALU.mult))
                dve.tensor_scalar(hs[0:r, 10 + d0:10 + d1], hs[0:r, 10 + d0:10 + d1], 1.0 / DQ, None,
                                  ALU.mult).then_inc(hs_done, 1)

            def rotate(t):
                r = rows[t]
                (a0, a1), (d0, d1) = heads_a[t], heads_d[t]
                dve.wait_ge(hstd_done, t + 1)
                step(dve.reciprocal(hr[0:r, :], hr[0:r, :]))
                if t >= 1:
                    dve.wait_ge(t1_done, 2 * t)
                    dve.wait_ge(t2_done, 4 * t)
                dve.tensor_tensor(view_a(qn[0:r], t), view_a(pr[0:r, t % 2], t),
                                  hr[0:r, a0:a1].unsqueeze(2).broadcast_to((r, a1 - a0, DH)), ALU.mult).then_inc(qn_done, 1)
                dve.tensor_tensor(view_d(qn[0:r], t, R_QD), view_d(pr[0:r, t % 2], t, QD),
                                  hr[0:r, 10 + d0:10 + d1].unsqueeze(2).broadcast_to((r, d1 - d0, DQ)), ALU.mult).then_inc(qn_done, 1)
                dve.wait_ge(gain_done, sum(gain_ops[:t + 1]))
                qa, qd = halves(qn, t, R_QD)
                ta, td = halves(t1, t, R_QD)
                sa, sd = halves(t2, t, R_QD)
                oa, od = halves(ro[:, t % 2], t, R_QD)
                for q, o, h, c, n in ((qa, ta, a1 - a0, 0, 32), (qd, td, d1 - d0, 64, 16)):
                    cos = rope[0:r, t, c:c + n].unsqueeze(1).broadcast_to((r, h, n))
                    for s in range(2):
                        ins = dve.tensor_tensor(o[:, :, s, :], q[:, :, s, :], cos, ALU.mult)
                    ins.then_inc(t1_done, 1)
                dve.wait_ge(t1_done, 2 * (t + 1))
                dve.wait_ge(t2_done, 4 * (t + 1))
                if t >= 2:
                    dve.wait_ge(qk_ps, ntg_before[t - 1])
                for o, x, y in ((oa, ta, sa), (od, td, sd)):
                    dve.tensor_tensor(o[:, :, 0, :], x[:, :, 0, :], y[:, :, 0, :], ALU.subtract).then_inc(ro_done, 1)
                    dve.tensor_tensor(o[:, :, 1, :], x[:, :, 1, :], y[:, :, 1, :], ALU.add).then_inc(ro_done, 1)

            def low(t):
                r = rows[t]
                if t >= 2:
                    dve.wait_ge(qk_stored[t % 2], stored_before[t])
                for i, cs in enumerate(tgroups[t]):
                    n = ntg_before[t] + i
                    dve.wait_ge(hi_done, n + 1)
                    runs = [cs] if cs[-1] - cs[0] == len(cs) - 1 else [cs[:1], cs[1:]]
                    at = 0
                    for run in runs:
                        k = slice(run[0], run[-1] + 1)
                        ins = dve.tensor_tensor(lo[:, t % 2, k, 0:r],
                                                ptq[:, n % 2, at * P:(at + len(run)) * P].rearrange("p (c n) -> p c n", n=P)[:, :, 0:r],
                                                hi[:, t % 2, k, 0:r].bitcast(F32), ALU.subtract)
                        at += len(run)
                    ins.then_inc(lo_done, 1)

            norm(0)
            copy_ut(0)
            for t in range(T):
                if t + 1 < T:
                    norm(t + 1)
                    copy_ut(t + 1)
                if t >= 1:
                    low(t - 1)
                head_sums(t)
                rotate(t)
            low(T - 1)

        @block.gpsimd
        def _(pool):
            pool.wait_ge(const_landed, 16 * 8)
            for t in range(T):
                r = rows[t]
                (a0, a1), (d0, d1) = heads_a[t], heads_d[t]
                pool.wait_ge(proj_out, ngroups_before[t + 1])
                if t >= 1:
                    pool.wait_ge(ro_done, 4 * t)
                pool.tensor_tensor(view_a(t1[0:r], t), view_a(pr[0:r, t % 2], t), view_a(pr[0:r, t % 2], t),
                                   ALU.mult).then_inc(sq_done, 1)
                pool.tensor_tensor(view_d(t1[0:r], t, R_QD), view_d(pr[0:r, t % 2], t, QD),
                                   view_d(pr[0:r, t % 2], t, QD), ALU.mult).then_inc(sq_done, 1)
                vw = v_all[0:r, t, :]
                pool.tensor_copy(vw[:, 0:128], pr[0:r, t % 2, VA:VA + 128])
                pool.tensor_copy(vw[:, 128:640], pr[0:r, t % 2, VD:VD + 512])
                pool.wait_ge(qn_done, 2 * (t + 1))
                for h0, h1, g in ((0, 8, 0), (8, 10, 1)):
                    if h0 >= a0:
                        v = qn[0:r, h0 * DH:h1 * DH].rearrange("p (h d) -> p h d", d=DH)
                        pool.tensor_tensor(v, v, gains[0:r, g, :].unsqueeze(1).broadcast_to((r, h1 - h0, DH)),
                                           ALU.mult).then_inc(gain_done, 1)
                for h0, h1, g in ((0, 16, 0), (16, 32, 1)):
                    if h0 >= d0:
                        v = qn[0:r, R_QD + h0 * DQ:R_QD + h1 * DQ].rearrange("p (h d) -> p h d", d=DQ)
                        pool.tensor_tensor(v, v, gaind[0:r, g, :].unsqueeze(1).broadcast_to((r, h1 - h0, DQ)),
                                           ALU.mult).then_inc(gain_done, 1)
                pool.wait_ge(gain_done, sum(gain_ops[:t + 1]))
                if t >= 1:
                    pool.wait_ge(ro_done, 4 * t)
                qa, qd = halves(qn, t, R_QD)
                sa, sd = halves(t2, t, R_QD)
                for q, o, h, c, n in ((qa, sa, a1 - a0, 32, 32), (qd, sd, d1 - d0, 80, 16)):
                    sin = rope[0:r, t, c:c + n].unsqueeze(1).broadcast_to((r, h, n))
                    for s in range(2):
                        pool.tensor_tensor(o[:, :, s, :], q[:, :, 1 - s, :], sin, ALU.mult).then_inc(t2_done, 1)

        @block.tensor
        def _(pe):
            def transpose_u(t):
                r = rows[t]
                pe.wait_ge(u_done, t + 1)
                for b in range(2):
                    if t >= 1:
                        pe.wait_ge((ut_a, ut_v)[b], t)
                    for c in range(4):
                        k = 4 * b + c
                        ins = pe.transpose(ptu[:, b, c * P:c * P + r], us[0:r, t % 2, k * P:(k + 1) * P], ident[0:r, 0:r])
                    ins.then_inc(ut_ps, 1)

            def transpose_qk(t):
                r = rows[t]
                pe.wait_ge(ro_done, 4 * (t + 1))
                for i, cs in enumerate(tgroups[t]):
                    n = ntg_before[t] + i
                    if n >= 2:
                        pe.wait_ge(lo_done, n - 1)
                    for j, c in enumerate(cs):
                        ins = pe.transpose(ptq[:, n % 2, j * P:j * P + r], ro[0:r, t % 2, c * P:(c + 1) * P], ident[0:r, 0:r])
                    ins.then_inc(qk_ps, 1)

            pe.wait_ge(const_landed, 16 * 8)
            transpose_u(0)
            for t in range(T):
                r = rows[t]
                pe.wait_ge(ut_a, t + 1)
                pe.wait_ge(ut_v, t + 1)
                for i, (c0, c1) in enumerate(colgroups[t]):
                    n = ngroups_before[t] + i
                    if n >= 4:
                        pe.wait_ge(proj_out, n - 3)
                    for k in range(KC):
                        if n == 0:
                            pe.wait_ge(w_in_sem[k], 16)
                        ins = pe.matmul(pp[0:r, n % 4, 0:c1 - c0], ut[:, t % 2, k, 0:r], w_sb[:, k, c0:c1],
                                        start=(k == 0), stop=(k == KC - 1))
                    ins.then_inc(proj_ps, 1)
                    if i == 1 and t + 1 < T:
                        transpose_u(t + 1)
                if t >= 1:
                    transpose_qk(t - 1)
            transpose_qk(T - 1)


def attend_diff(nc, a, v_all, mixed, qk_dram):
    with ExitStack() as ctx:
        sb = lambda n, s, d=F32: ctx.enter_context(nc.sbuf_tensor(n, s, d))
        sem = lambda n: ctx.enter_context(nc.semaphore(n))
        ps = lambda n, s: ctx.enter_context(nc.psum_tensor(n, s, F32))
        q_st = sb("q_st", [P, 2, 2, SEQ], F32R)
        k_st = sb("k_st", [P, 2, 2, KEYS], F32R)
        e = sb("e", [P, 2, 2, KEYS])
        dsb = sb("dsb", [P, 2, KEYS])
        pt = sb("pt", [P, 2, 9, 512])
        ot = sb("ot", [DV, 512])
        ident = sb("ident2", [P, P])
        lam = sb("lam", [P, 4, DQ])
        lw = sb("lw", [P, 8])
        meta_s = sb("meta_s", [P, 2, 2 * NT, N_META])
        meta_nm = sb("meta_nm", [P, 2, 2 * NT])
        seq_nm = sb("seq_nm", [P, 4])
        nm = sb("nm", [P, 4])
        ls = sb("ls", [P, 2, 2, 2])
        total = sb("total", [P, 16, 2])
        inverse = sb("inverse", [P, 16, 2])
        ratio = sb("ratio", [P, 2])
        s_ps = [ps("s_ps0", [P, 2, 512]), ps("s_ps1", [P, 2, 512])]
        t_ps = ps("t_ps", [P, 2, 512])
        x_ps = ps("x_ps", [P, 512])
        o_ps = ps("o_ps", [P, 512])
        S = lambda i: s_ps[i][:, :, :].rearrange("p b n -> p (b n)")

        const_landed = sem("const_landed2")
        st_sem = [sem(f"stack_landed{i}") for i in range(2)]
        lam_dots, lam_exp, lam_done = sem("lam_dots"), sem("lam_exp"), sem("lam_done")
        scores_ready, max_ready, exp_done = sem("scores_ready"), sem("max_ready"), sem("exp_done")
        nm_ready, s_used = sem("nm_ready"), sem("scores_used")
        inverted = sem("inverted")
        total_done, ratio_done, combined = sem("total_done"), sem("ratio_done"), sem("combined")
        t_ready, t_copied = sem("p_transposed"), sem("pt_copied")
        x_ready, x_copied, meta_max = sem("x_ready"), sem("x_copied"), sem("meta_max")
        o_ready, ot_done = sem("o_ready"), sem("ot_copied")
        dve_chain = sem("dve_chain2")

        U = HD * NT
        NG = U // 4
        STEPS = U + 8
        block = ctx.enter_context(nc.Block())

        copied_in = lambda n: (n - 9) // 4 if n >= 9 and (n - 9) % 4 == 0 and (n - 9) // 4 < NG else None
        back_in = lambda n: copied_in(n - 1)
        order = [("scores", 0)]
        for n in range(STEPS):
            if 2 <= n <= U + 1:
                order.append(("meta", n - 2))
            if back_in(n) is not None:
                order.append(("back", back_in(n)))
            if n % NT == NT - 1 and n + 1 < U:
                order.append(("scores", (n + 1) // NT))
        use_of = {what: k for k, what in enumerate(order)}

        @block.sync
        def _(sp):
            sp.dma_start(ident[:, :], a["consts"][:, 0:P]).then_inc(const_landed, 16)
            for i, n in enumerate(("lambda_q1", "lambda_k1", "lambda_q2", "lambda_k2")):
                sp.dma_start(lam[:, i, :], a[n][0, :].partition_broadcast(P)).then_inc(const_landed, 16)
            for h in range(HD):
                b = h % 2
                if h >= 2:
                    sp.wait_ge(scores_ready, 2 * NT * (h - 1))
                for j in range(4):
                    rows = slice(32 * j, 32 * j + 32)
                    for buf, at, part, n in ((q_st, R_QD, j % 2, SEQ), (k_st, R_KD, j // 2, KEYS)):
                        src = qk_dram[part, at + h * 64:at + h * 64 + 64, 0:n].rearrange("(s d) n -> d s n", s=2)
                        sp.dma_start(buf[rows, b, :, 0:n].bitcast(F32), src).then_inc(st_sem[b], 16)

        @block.scalar
        def _(act):
            def copy_part(u, g):
                act.wait_ge(t_ready, 2 * u + g + 1)
                if g == 0 and u % 4 == 0 and u >= 8:
                    act.wait_ge(o_ready, u // 4 - 1)
                act.copy(pt[:, (u // 4) % 2, 4 * g:4 * g + 4, (u % 4) * P:(u % 4 + 1) * P],
                         t_ps[:, g, :].rearrange("p (c n) -> p c n", n=P)).then_inc(t_copied, 1)

            act.wait_ge(lam_dots, 2)
            act.activation(lw[:, 2:4], lw[:, 0:2], ACT.Exp).then_inc(lam_exp, 1)
            for n in range(STEPS):
                for i in range(2):
                    if n < U:
                        act.wait_ge(nm_ready, 2 * n + i + 1)
                        if n >= 2 and i == 0:
                            act.wait_ge(combined, n - 1)
                            act.wait_ge(total_done, n - 1)
                        k = (2 * n + i) % 4
                        act.activation(e[:, n % 2, i, 0:SEQ], S(i), ACT.Exp, bias=nm[:, k:k + 1],
                                       accum_out=ls[:, n % 2, 0, i:i + 1]).then_inc(s_used, 1)
                        act.activation(e[:, n % 2, i, SEQ:KEYS], meta_s[:, (n // NT) % 2, 2 * (n % NT) + i, :], ACT.Exp,
                                       bias=nm[:, k:k + 1], accum_out=ls[:, n % 2, 1, i:i + 1]).then_inc(exp_done, 1)
                    if i == 0 and 2 <= n <= U + 1:
                        copy_part(n - 2, 0)
                        copy_part(n - 2, 1)
                g = copied_in(n)
                if g is not None:
                    act.wait_ge(o_ready, g + 1)
                    if g >= 1:
                        act.wait_ge(x_ready, use_of[("back", g - 1)] + 1)
                    act.copy(ot[:, :], o_ps[0:DV, :]).then_inc(ot_done, 1)

        @block.vector
        def _(dve):
            step = chained(dve, dve_chain)
            dve.wait_ge(const_landed, 16 * 5)
            for i in range(2):
                dve.tensor_tensor_reduce(lam[:, 2 * i, :], lam[:, 2 * i, :], lam[:, 2 * i + 1, :], 1.0, 0.0,
                                         ALU.mult, ALU.add, lw[:, i:i + 1]).then_inc(lam_dots, 1)
            dve.wait_ge(lam_exp, 1)
            step(dve.tensor_tensor(lw[:, 4:5], lw[:, 3:4], lw[:, 2:3], ALU.subtract))
            dve.tensor_scalar(lw[:, 5:6], lw[:, 4:5], -LAMBDA_INIT, None, ALU.add).then_inc(lam_done, 1)
            dve.wait_ge(lam_done, 1)

            def meta_scores(h):
                dve.wait_ge(x_ready, use_of[("scores", h)] + 1)
                if h >= 2:
                    dve.wait_ge(exp_done, 2 * NT * (h - 1))
                x = x_ps[:, 0:2 * NT * N_META].rearrange("p (u m) -> p u m", m=N_META)
                dve.tensor_reduce(meta_nm[:, h % 2, :], x, AX.X, ALU.max, negate=True).then_inc(meta_max, 1)
                dve.tensor_copy(meta_s[:, h % 2, :, :], x).then_inc(x_copied, 1)

            def maximum(n, i):
                k = (2 * n + i) % 4
                dve.wait_ge(scores_ready, 2 * n + i + 1)
                if n >= 2:
                    dve.wait_ge(nm_ready, 2 * n + i - 3)
                dve.tensor_reduce(seq_nm[:, k:k + 1], S(i), AX.X, ALU.max, negate=True).then_inc(max_ready, 1)
                if n % NT == 0 and i == 0:
                    dve.wait_ge(meta_max, n // NT + 1)
                if n >= 2:
                    dve.wait_ge(exp_done, 2 * n + i - 3)
                dve.wait_ge(max_ready, 2 * n + i + 1)
                at = 2 * (n % NT) + i
                dve.tensor_tensor(nm[:, k:k + 1], seq_nm[:, k:k + 1], meta_nm[:, (n // NT) % 2, at:at + 1],
                                  ALU.min).then_inc(nm_ready, 1)

            def invert(u):
                dve.wait_ge(total_done, u + 1)
                dve.reciprocal(inverse[:, u % 16, :], total[:, u % 16, :]).then_inc(inverted, 1)

            def combine_halves(u):
                b = u % 2
                dve.wait_ge(s_used, 2 * u + 2)
                dve.wait_ge(exp_done, 2 * u + 2)
                if u >= 2:
                    dve.wait_ge(t_ready, 2 * u - 2)
                    dve.wait_ge(x_ready, use_of[("meta", u - 2)] + 1)
                dve.wait_ge(ratio_done, u + 1)
                dve.scalar_tensor_tensor(out=dsb[:, b, :], in0=e[:, b, 1, :], scalar=ratio[:, b:b + 1],
                                         in1=e[:, b, 0, :], op0=ALU.mult, op1=ALU.add).then_inc(combined, 1)

            def copy_meta(u):
                dve.wait_ge(x_ready, use_of[("meta", u)] + 1)
                if u % 4 == 0 and u >= 8:
                    dve.wait_ge(o_ready, u // 4 - 1)
                dve.tensor_copy(pt[0:N_META, (u // 4) % 2, 8, (u % 4) * P:(u % 4 + 1) * P],
                                x_ps[0:N_META, 0:P]).then_inc(x_copied, 1)

            def store_out(g):
                h, t0 = g // 2, 4 * (g % 2)
                dve.wait_ge(x_ready, use_of[("back", g)] + 1)
                dve.wait_ge(inverted, 4 * g + 4)
                for j in range(4):
                    ins = dve.tensor_scalar(mixed[:, t0 + j, 512 + h * DV:512 + (h + 1) * DV],
                                            x_ps[:, j * DV:(j + 1) * DV], inverse[:, (4 * g + j) % 16, 0:1],
                                            None, ALU.mult)
                ins.then_inc(x_copied, 1)

            meta_scores(0)
            for n in range(STEPS):
                if n < U:
                    maximum(n, 0)
                if 1 <= n <= U:
                    invert(n - 1)
                if 2 <= n <= U + 1:
                    copy_meta(n - 2)
                if n < U:
                    maximum(n, 1)
                if 1 <= n <= U:
                    combine_halves(n - 1)
                if back_in(n) is not None:
                    store_out(back_in(n))
                if n % NT == NT - 1 and n + 1 < U:
                    meta_scores((n + 1) // NT)

        @block.gpsimd
        def _(pool):
            pool.wait_ge(lam_done, 1)
            for u in range(U):
                pool.wait_ge(s_used, 2 * u + 2)
                pool.wait_ge(exp_done, 2 * u + 2)
                if u >= 16:
                    pool.wait_ge(x_copied, use_of[("back", u // 4 - 4)] + 1)
                pool.tensor_tensor(total[:, u % 16, :], ls[:, u % 2, 0, :], ls[:, u % 2, 1, :], ALU.add).then_inc(total_done, 1)
                if u >= 2:
                    pool.wait_ge(combined, u - 1)
                pool.wait_ge(inverted, u + 1)
                pool.tensor_scalar(ratio[:, u % 2:u % 2 + 1], total[:, u % 16, 0:1], inverse[:, u % 16, 1:2], lw[:, 5:6],
                                   ALU.mult, ALU.mult).then_inc(ratio_done, 1)

        @block.tensor
        def _(pe):
            due = []

            def scores(n, i):
                h, t = n // NT, n % NT
                if n >= 1:
                    pe.wait_ge(s_used, 2 * n + i - 1)
                for c in range(2):
                    ins = pe.matmul(s_ps[i][:, c, :], q_st[:, h % 2, i, t * P:(t + 1) * P],
                                    k_st[:, h % 2, i, c * 512:(c + 1) * 512], start=True, stop=True)
                ins.then_inc(scores_ready, 1)

            def free_x(what):
                if use_of[what] >= 1:
                    pe.wait_ge(x_copied, use_of[what])

            def meta_scores(h):
                pe.wait_ge(st_sem[h % 2], 16 * 8 * (h // 2 + 1))
                free_x(("scores", h))
                for t in range(NT):
                    for i in range(2):
                        k = 2 * t + i
                        ins = pe.matmul(x_ps[:, k * N_META:(k + 1) * N_META], q_st[:, h % 2, i, t * P:(t + 1) * P],
                                        k_st[:, h % 2, i, SEQ:KEYS], start=True, stop=True)
                ins.then_inc(x_ready, 1)

            def transpose_part(u, g):
                if u >= 1:
                    pe.wait_ge(t_copied, 2 * u + g - 1)
                for c in range(4 * g, 4 * g + 4):
                    ins = pe.transpose(t_ps[:, g, (c % 4) * P:(c % 4 + 1) * P], dsb[:, u % 2, c * P:(c + 1) * P], ident[:, :])
                ins.then_inc(t_ready, 1)

            def transpose_meta(u):
                free_x(("meta", u))
                pe.transpose(x_ps[0:N_META, 0:P], dsb[:, u % 2, SEQ:KEYS], ident[:, :]).then_inc(x_ready, 1)

            def values(k):
                for g, c in due[:k]:
                    h = g // 2
                    r = P if c < 8 else N_META
                    if c == 0:
                        pe.wait_ge(t_copied, 2 * (4 * g + 4))
                        pe.wait_ge(x_copied, use_of[("meta", 4 * g + 3)] + 1)
                        if g >= 1:
                            pe.wait_ge(ot_done, g)
                    vt = v_all[0:r, c, 128 + h * DV:128 + (h + 1) * DV]
                    ins = pe.matmul(o_ps[0:DV, :], vt, pt[0:r, g % 2, c, :], start=(c == 0), stop=(c == 8))
                    if c == 8:
                        ins.then_inc(o_ready, 1)
                del due[:k]

            pe.wait_ge(const_landed, 16 * 5)
            meta_scores(0)
            for n in range(STEPS):
                if n >= 6 and (n - 6) % 4 == 0 and (n - 6) // 4 < NG:
                    due += [((n - 6) // 4, c) for c in range(9)]
                if n < U:
                    scores(n, 0)
                if 2 <= n <= U + 1:
                    pe.wait_ge(combined, n - 1)
                    transpose_part(n - 2, 0)
                    transpose_part(n - 2, 1)
                    transpose_meta(n - 2)
                values(1 if n % 4 == 1 else 0)
                if n < U:
                    scores(n, 1)
                g = back_in(n)
                if g is not None:
                    pe.wait_ge(ot_done, g + 1)
                    free_x(("back", g))
                    for j in range(4):
                        ins = pe.transpose(x_ps[:, j * DV:(j + 1) * DV], ot[:, j * P:(j + 1) * P], ident[0:DV, 0:DV])
                    ins.then_inc(x_ready, 1)
                if n % NT == NT - 1 and n + 1 < U:
                    meta_scores((n + 1) // NT)
                values(2)


def attend_window(nc, a, v_all, mixed, qk_dram):
    with ExitStack() as ctx:
        sb = lambda n, s, d=F32: ctx.enter_context(nc.sbuf_tensor(n, s, d))
        sem = lambda n: ctx.enter_context(nc.semaphore(n))
        ps = lambda n, s: ctx.enter_context(nc.psum_tensor(n, s, F32))
        BW = 3 * P + N_META
        q_st = sb("qa_st", [P, HQ, SEQ], F32R)
        k_st = sb("ka_st", [P, 2, HKV, KEYS], F32R)
        masks = sb("masks", [P, 3, BW])
        sink = sb("sink", [P, HQ])
        sm = sb("sm", [P, 2, G, BW])
        pt = sb("pta", [P, 2, 4, 512])
        ot = sb("ota", [DV, 2, 512])
        ident = sb("ident3", [P, P])
        mx = sb("mx", [P, 2, G])
        nm = sb("nma", [P, 2, G])
        ls = sb("lsa", [P, 2, G])
        xs = sb("xsink", [P, 2, G])
        rl = sb("rla", [P, 4, G])
        s_ps = ps("sa_ps", [P, 4, 512])
        t_ps = ps("ta_ps", [P, 2, 512])
        o_ps = ps("oa_ps", [P, 512])
        ob_ps = ps("ob_ps", [P, 512])

        landed = sem("window_landed")
        s_ready, masked, mx_done, nm_done, exp_done = (sem("sa_ready"), sem("masked"), sem("maxa"), sem("nm_done"),
                                                       sem("expa_done"))
        sink_in, sink_exp, rl_done = sem("sink_in"), sem("sink_exp"), sem("rl_done")
        t_ready, t_copied = sem("ta_ready"), sem("ta_copied")
        o_ready, ot_done, ob_ready, ob_done = sem("oa_ready"), sem("ota_done"), sem("ob_ready"), sem("ob_done")
        dve_chain = sem("dve_chain3")
        U = NT * HKV
        bands = [[t + d for d in (-1, 0, 1) if 0 <= t + d < NT] for t in range(NT)]
        which = [0 if t == 0 else 2 if t == NT - 1 else 1 for t in range(NT)]
        nchunk = [len(bands[u // HKV]) + 1 for u in range(U)]
        before = [sum(nchunk[:u]) for u in range(U + 1)]
        width = lambda u: P * (nchunk[u] - 1) + N_META
        block = ctx.enter_context(nc.Block())

        @block.sync
        def _(sp):
            sp.dma_start(ident[:, :], a["consts"][:, 0:P]).then_inc(landed, 16)
            sp.dma_start(masks[:, :, :], a["masks"][:, :, :]).then_inc(landed, 16)
            sp.dma_start(sink[:, :], a["sink_swa"][0, :].partition_broadcast(P)).then_inc(landed, 16)
            for part in range(2):
                rows = slice(64 * part, 64 * part + 64)
                src = qk_dram[part, 0:HQ * DH, 0:SEQ].rearrange("(h d) n -> d h n", d=DH)
                sp.dma_start(q_st[rows, :, :].bitcast(F32), src).then_inc(landed, 16)
                for twice in range(2):
                    src = qk_dram[part, R_KA:R_KA + HKV * DH, :].rearrange("(h d) n -> d h n", d=DH)
                    sp.dma_start(k_st[64 * twice:64 * twice + 64, part, :, :].bitcast(F32), src).then_inc(landed, 16)

        @block.tensor
        def _(pe):
            pe.wait_ge(landed, 16 * 9)

            def scores(u):
                t, g = u // HKV, u % HKV
                k0, nb = bands[t][0] * P, (nchunk[u] - 1) * P
                for j in range(G):
                    if u >= 1:
                        pe.wait_ge(masked, G * (u - 1) + j + 1)
                    q = q_st[:, g * G + j, t * P:(t + 1) * P]
                    for part in range(2):
                        pe.matmul(s_ps[:, j, 0:nb], q, k_st[:, part, g, k0:k0 + nb], start=(part == 0), stop=(part == 1))
                    for part in range(2):
                        ins = pe.matmul(s_ps[:, j, nb:nb + N_META], q, k_st[:, part, g, SEQ:KEYS],
                                        start=(part == 0), stop=(part == 1))
                    ins.then_inc(s_ready, 1)

            def weigh(u, chunks):
                t, g = u // HKV, u % HKV
                pe.wait_ge(exp_done, G * (u + 1))
                for c in chunks:
                    n = before[u] + c
                    w = P if c < nchunk[u] - 1 else N_META
                    if n >= 2:
                        pe.wait_ge(t_copied, n - 1)
                    for j in range(G):
                        ins = pe.transpose(t_ps[0:w, n % 2, j * P:(j + 1) * P], sm[:, u % 2, j, c * P:c * P + w], ident[:, :])
                    ins.then_inc(t_ready, 1)

            def values(u):
                t, g = u // HKV, u % HKV
                for c in range(nchunk[u]):
                    w = P if c < nchunk[u] - 1 else N_META
                    tile = bands[t][c] if w == P else NT
                    pe.wait_ge(t_copied, before[u] + c + 1)
                    if c == 0 and u >= 1:
                        pe.wait_ge(ot_done, u)
                    ins = pe.matmul(o_ps[0:DV, :], v_all[0:w, tile, g * DH:(g + 1) * DH], pt[0:w, u % 2, c, :],
                                    start=(c == 0), stop=(c == nchunk[u] - 1))
                ins.then_inc(o_ready, 1)

            def back(u):
                pe.wait_ge(ot_done, u + 1)
                if u >= 1:
                    pe.wait_ge(ob_done, u)
                for j in range(G):
                    ins = pe.transpose(ob_ps[:, j * DV:(j + 1) * DV], ot[:, u % 2, j * P:(j + 1) * P], ident[0:DV, 0:DV])
                ins.then_inc(ob_ready, 1)

            for n in range(U + 3):
                if n < U:
                    scores(n)
                if 1 <= n <= U:
                    weigh(n - 1, (0, 1))
                if 2 <= n <= U + 1:
                    values(n - 2)
                if 1 <= n <= U:
                    weigh(n - 1, range(2, nchunk[n - 1]))
                if n >= 3:
                    back(n - 3)

        def copy_chunk(op, eng, u, c):
            n = before[u] + c
            w = P if c < nchunk[u] - 1 else N_META
            eng.wait_ge(t_ready, n + 1)
            if n >= 1:
                eng.wait_ge(t_copied, n)
            if u >= 2 and c < 2:
                eng.wait_ge(o_ready, u - 1)
            op(pt[0:w, u % 2, c, :], t_ps[0:w, n % 2, :]).then_inc(t_copied, 1)

        @block.vector
        def _(dve):
            step = chained(dve, dve_chain)
            dve.wait_ge(landed, 16 * 9)
            for n in range(U + 3):
                if n < U:
                    t, g, b, w = n // HKV, n % HKV, n % 2, width(n)
                    if n >= 2:
                        dve.wait_ge(t_ready, before[n - 1])
                    for j in range(G):
                        dve.wait_ge(s_ready, G * n + j + 1)
                        dve.tensor_tensor_reduce(sm[:, b, j, 0:w], s_ps[:, j, 0:w], masks[:, which[t], 0:w], 1.0, NEG,
                                                 ALU.add, ALU.max, mx[:, b, j:j + 1]).then_inc(masked, 1)
                    dve.wait_ge(masked, G * (n + 1))
                    step(dve.tensor_tensor(mx[:, b, :], mx[:, b, :], sink[:, g * G:(g + 1) * G], ALU.max))
                    dve.tensor_scalar(nm[:, b, :], mx[:, b, :], -1.0, None, ALU.mult).then_inc(nm_done, 1)
                    dve.tensor_tensor(xs[:, b, :], sink[:, g * G:(g + 1) * G], mx[:, b, :], ALU.subtract).then_inc(sink_in, 1)
                if 1 <= n <= U:
                    u = n - 1
                    dve.wait_ge(sink_exp, u + 1)
                    dve.wait_ge(exp_done, G * (u + 1))
                    step(dve.tensor_tensor(ls[:, u % 2, :], ls[:, u % 2, :], xs[:, u % 2, :], ALU.add))
                    dve.reciprocal(rl[:, u % 4, :], ls[:, u % 2, :]).then_inc(rl_done, 1)
                    for c in range(2, nchunk[u]):
                        copy_chunk(dve.tensor_copy, dve, u, c)
                if n >= 3:
                    u = n - 3
                    t, g = u // HKV, u % HKV
                    dve.wait_ge(ob_ready, u + 1)
                    dve.wait_ge(rl_done, u + 1)
                    for j in range(G):
                        hcol = (g * G + j) * DH
                        ins = dve.tensor_scalar(mixed[:, t, hcol:hcol + DH], ob_ps[:, j * DV:(j + 1) * DV],
                                                rl[:, u % 4, j:j + 1], None, ALU.mult)
                    ins.then_inc(ob_done, 1)

        @block.scalar
        def _(act):
            for n in range(U + 2):
                if 1 <= n <= U:
                    for c in range(2):
                        copy_chunk(act.copy, act, n - 1, c)
                if n < U:
                    b, w = n % 2, width(n)
                    act.wait_ge(nm_done, n + 1)
                    if n >= 2:
                        act.wait_ge(rl_done, n - 1)
                    for j in range(G):
                        act.activation(sm[:, b, j, 0:w], sm[:, b, j, 0:w], ACT.Exp, bias=nm[:, b, j:j + 1],
                                       accum_out=ls[:, b, j:j + 1]).then_inc(exp_done, 1)
                    act.wait_ge(sink_in, n + 1)
                    act.activation(xs[:, b, :], xs[:, b, :], ACT.Exp).then_inc(sink_exp, 1)
                if n >= 2:
                    u = n - 2
                    act.wait_ge(o_ready, u + 1)
                    if u >= 2:
                        act.wait_ge(ob_ready, u - 1)
                    act.copy(ot[:, u % 2, :], o_ps[0:DV, :]).then_inc(ot_done, 1)


C_ID, C_TRI, C_EXP, C_BASE, C_JOB, C_STEP, C_W = 0, 128, 256, 288, 320, 384, 388


def route(nc, a, mixed, gates, jobs, h2_dram, v_dram, slot_dram):
    with ExitStack() as ctx:
        sb = lambda n, s, d=F32: ctx.enter_context(nc.sbuf_tensor(n, s, d))
        sem = lambda n: ctx.enter_context(nc.semaphore(n))
        ps = lambda n, s: ctx.enter_context(nc.psum_tensor(n, s, F32))
        w_sb = sb("w_out_sb", [P, KC, D])
        wr = sb("w_router_sb", [P, KC, N_EXP])
        br = sb("b_router_sb", [P, N_EXP])
        gd = sb("g_head_sb", [P, DV])
        gf = sb("g_ffn_sb", [P, D])
        cst = sb("cst", [P, C_W])
        ones = sb("ones", [P, P])
        xs = sb("xs4", [P, 2, D])
        hsq = sb("hsq", [P, HD * DV])
        hs = sb("hs4", [P, HD])
        hr = sb("hr4", [P, HD])
        mt = sb("mt", [P, 2, KC, P])
        h2 = sb("h2", [P, 2, D])
        vs = sb("vs", [P, 2, D])
        vt = sb("vt", [P, KC, P])
        ss = sb("ss4", [P, NT])
        rs = sb("rs4", [P, NT])
        eps = sb("eps4", [P, 2])
        lg = sb("lg", [P, N_EXP])
        top = sb("top", [P, NT, 8])
        idx = sb("idx", [P, 8], U32)
        idf = sb("idf", [P, 8])
        oh = sb("oh", [P, TOP_K, N_EXP])
        sel = sb("sel", [P, N_EXP])
        acc = sb("acc", [P, N_EXP])
        pos = sb("pos", [P, N_EXP])
        junk = sb("junk", [P, N_EXP])
        dst = sb("dst", [P, NT, TOP_K])
        dsti = sb("dsti", [P, NT, TOP_K], U32)
        code = sb("code", [P, NT, TOP_K, 2], U32)
        none = sb("none", [P, N_EXP * CAP * 2 // P], U32)
        gsum = sb("gsum", [P, NT])
        ec = sb("ec", [N_EXP, 8])
        ej = sb("ej", [N_EXP, 3, NJ])
        jf = sb("jf", [1, 6, NJ])
        tm_ps, tv_ps = ps("tm_ps", [P, 2, 512]), ps("tv_ps", [P, 512])
        o_ps, r_ps = ps("o4_ps", [P, 4, 512]), ps("r_ps", [P, 512])

        landed = sem("route_landed")
        x_sem = [sem(f"x4_landed{i}") for i in range(2)]
        h2_sem = [sem(f"h2_stored{i}") for i in range(2)]
        v_sem = [sem(f"v_stored{i}") for i in range(2)]
        cleared, scattered = sem("slots_cleared"), sem("slots_written")
        ready, ones_set, codes_set = sem("consts4_set"), sem("ones_set"), sem("codes_set")
        hs_done, hstd_done, head_done = sem("hs4_done"), sem("hstd4_done"), sem("head_done")
        tm_ready, mt_a, mt_v = sem("tm_ready"), sem("mt_act"), sem("mt_dve")
        o_ready, h2_done = sem("o4_ready"), sem("h2_done")
        ss_done, std_done, v_done = sem("ss4_done"), sem("std4_done"), sem("v_done")
        tv_ready, vt_done = sem("tv_ready"), sem("vt_done")
        r_ready, lg_done, sel_done, rank_ready, dst_done = (sem("r_ready"), sem("lg_done"), sem("sel_done"),
                                                            sem("rank_ready"), sem("dst_done"))
        gates_in, gates_exp = sem("gates_in"), sem("gates_exp")
        cnt_ready, jobs_step, jobs_in = sem("cnt_ready"), sem("jobs_step"), sem("jobs_in")
        dve_chain = sem("dve_chain4")
        block = ctx.enter_context(nc.Block())
        NL = 8

        @block.sync
        def _(sp):
            sp.dma_start(cst[:, :], a["consts"][:, :]).then_inc(landed, 16)
            sp.dma_start(gd[:, :], a["g_diff_head"][0, :].partition_broadcast(P)).then_inc(landed, 16)

            def load_x(t):
                if t >= 2:
                    sp.wait_ge(h2_done, 2 * (t - 1))
                sp.dma_start(xs[:, t % 2, :], a["x"][0, t * P:(t + 1) * P, :]).then_inc(x_sem[t % 2], 16)
            load_x(0)
            load_x(1)
            for c in range(2):
                sp.dma_start(w_sb[:, 4 * c:4 * c + 4, :],
                             a["w_out"][0, 512 * c:512 * c + 512, :].rearrange("(k p) n -> p k n", p=P)).then_inc(landed, 16)
            sp.dma_start(gf[:, :], a["g_ffn"][0, :].partition_broadcast(P)).then_inc(landed, 16)
            sp.dma_start(br[:, :], a["b_router"][0, :].partition_broadcast(P)).then_inc(landed, 16)
            with nc.allow_non_contiguous_dma("128 byte rows, once"):
                sp.dma_start(wr[:, :, :], a["w_router"][0].rearrange("(k p) n -> p k n", p=P)).then_inc(landed, 16)
            sp.dma_start(ones[:, :], a["ones"][:, :]).then_inc(landed, 16)
            for t in range(NT):
                sp.wait_ge(h2_done, 2 * (t + 1))
                sp.dma_start(h2_dram[t * P:(t + 1) * P, :], h2[:, t % 2, :]).then_inc(h2_sem[t % 2], 16)
                if t + 2 < NT:
                    load_x(t + 2)
                sp.wait_ge(v_done, t + 1)
                sp.dma_start(v_dram[t * P:(t + 1) * P, :], vs[:, t % 2, :]).then_inc(v_sem[t % 2], 16)
            for i in range(2):
                sp.wait_ge(h2_sem[i], 16 * (NT // 2))
                sp.wait_ge(v_sem[i], 16 * (NT // 2))

        @block.gpsimd
        def _(pool):
            pool.memset(none[:, :], SEQ * TOP_K).then_inc(ready, 1)
            pool.iota(code[:, :, :, 0], pattern=[[P * TOP_K, NT], [1, TOP_K]], base=0, channel_multiplier=TOP_K
                      ).then_inc(codes_set, 1)
            pool.iota(code[:, :, :, 1], pattern=[[P, NT], [0, TOP_K]], base=0, channel_multiplier=1
                      ).then_inc(codes_set, 1)
            pool.wait_ge(ready, 1)
            pool.dma_start(slot_dram.rearrange("(p n) c -> p (n c)", p=P), none[:, :]).then_inc(cleared, 16)
            pool.wait_ge(cleared, 16)
            pool.wait_ge(codes_set, 2)
            for t in range(NT):
                pool.wait_ge(dst_done, t + 1)
                for k in range(TOP_K):
                    pool.indirect_dma_start(out=slot_dram[:, :],
                                            out_offset=bass.IndirectOffsetOnAxis(ap=dsti[:, t, k:k + 1], axis=0),
                                            in_=code[:, t, k, :], in_offset=None).then_inc(scattered, 16)
            pool.wait_ge(scattered, 16 * NT * TOP_K)

        @block.scalar
        def _(act):
            act.wait_ge(ones_set, 1)

            def head_std(t):
                act.wait_ge(hs_done, t + 1)
                act.activation(hr[:, :], hs[:, :], ACT.Sqrt, bias=eps[:, 1:2], scale=1.0 / DV).then_inc(hstd_done, 1)

            head_std(0)
            for t in range(NT + 1):
                if t + 1 < NT:
                    head_std(t + 1)
                if t < NT:
                    act.wait_ge(tm_ready, 2 * t + 1)
                    if t >= 2:
                        act.wait_ge(o_ready, 2 * (t - 1))
                    act.copy(mt[:, t % 2, 0:4, :], tm_ps[:, 0, :].rearrange("p (c n) -> p c n", n=P)).then_inc(mt_a, 1)
                    act.wait_ge(h2_done, 2 * (t + 1))
                    if t >= 2:
                        act.wait_ge(tv_ready, 2 * (t - 1))
                        act.wait_ge(v_sem[t % 2], 16 * (t // 2))
                    act.activation(vs[:, t % 2, :], h2[:, t % 2, :], ACT.Square, accum_out=ss[:, t:t + 1]).then_inc(ss_done, 1)
                    act.wait_ge(ss_done, t + 1)
                    act.activation(rs[:, t:t + 1], ss[:, t:t + 1], ACT.Sqrt, bias=eps[:, 0:1], scale=1.0 / D).then_inc(std_done, 1)
                if t >= 1:
                    u = t - 1
                    for b in range(2):
                        act.wait_ge(tv_ready, 2 * u + b + 1)
                        if b == 0 and u >= 1:
                            act.wait_ge(r_ready, u)
                        act.copy(vt[:, 4 * b:4 * b + 4, :], tv_ps[:, :].rearrange("p (c n) -> p c n", n=P)).then_inc(vt_done, 1)
            act.wait_ge(gates_in, 1)
            act.activation(gates[:, :, :], gates[:, :, :], ACT.Exp).then_inc(gates_exp, 1)

        @block.vector
        def _(dve):
            step = chained(dve, dve_chain)
            dve.memset(acc[:, :], 0.0)
            dve.memset(eps[:, 0:1], EPS)
            step(dve.memset(eps[:, 1:2], EPS_HEAD))
            dve.wait_ge(landed, 16 * NL)
            dve.tensor_scalar(gd[:, :], gd[:, :], 1.0 - LAMBDA_INIT, None, ALU.mult).then_inc(ones_set, 1)
            dve.wait_ge(ones_set, 1)

            def heads(t):
                m = mixed[:, t, 512:1024]
                v = m.rearrange("p (h d) -> p h d", d=DV)
                step(dve.tensor_tensor(hsq[:, :], m, m, ALU.mult))
                if t >= 1:
                    dve.wait_ge(head_done, t)
                dve.tensor_reduce(hs[:, :], hsq[:, :].rearrange("p (h d) -> p h d", d=DV), AX.X, ALU.add).then_inc(hs_done, 1)
                dve.wait_ge(hstd_done, t + 1)
                step(dve.reciprocal(hr[:, :], hr[:, :]))
                step(dve.tensor_tensor(v, v, hr[:, :].unsqueeze(2).broadcast_to((P, HD, DV)), ALU.mult))
                dve.tensor_tensor(v, v, gd[:, :].unsqueeze(1).broadcast_to((P, HD, DV)), ALU.mult).then_inc(head_done, 1)

            heads(0)
            for t in range(NT + 2):
                if t + 1 < NT:
                    heads(t + 1)
                if t < NT:
                    dve.wait_ge(tm_ready, 2 * t + 2)
                    if t >= 2:
                        dve.wait_ge(o_ready, 2 * (t - 1))
                    dve.tensor_copy(mt[:, t % 2, 4:8, :], tm_ps[:, 1, :].rearrange("p (c n) -> p c n", n=P)).then_inc(mt_v, 1)
                if t < NT:
                    dve.wait_ge(x_sem[t % 2], 16 * (t // 2 + 1))
                    if t >= 2:
                        dve.wait_ge(v_done, t - 1)
                        dve.wait_ge(h2_sem[t % 2], 16 * (t // 2))
                    for b in range(2):
                        dve.wait_ge(o_ready, 2 * t + b + 1)
                        dve.tensor_tensor(h2[:, t % 2, 512 * b:512 * b + 512], o_ps[:, 2 * (t % 2) + b, :],
                                          xs[:, t % 2, 512 * b:512 * b + 512], ALU.add).then_inc(h2_done, 1)
                if t < NT:
                    dve.wait_ge(std_done, t + 1)
                    step(dve.reciprocal(rs[:, t:t + 1], rs[:, t:t + 1]))
                    dve.scalar_tensor_tensor(out=vs[:, t % 2, :], in0=h2[:, t % 2, :], scalar=rs[:, t:t + 1], in1=gf[:, :],
                                             op0=ALU.mult, op1=ALU.mult).then_inc(v_done, 1)
                if 1 <= t <= NT:
                    u = t - 1
                    dve.wait_ge(r_ready, u + 1)
                    step(dve.tensor_tensor(lg[:, :], r_ps[:, 0:N_EXP], br[:, :], ALU.add))
                    step(dve.max(top[:, u, :], lg[:, :]))
                    step(dve.max_index(idx[:, :], top[:, u, :], lg[:, :]))
                    step(dve.tensor_copy(idf[:, :], idx[:, :]))
                    for k in range(TOP_K):
                        ins = dve.tensor_scalar(oh[:, k, :], cst[:, C_EXP:C_EXP + N_EXP], idf[:, k:k + 1], None, ALU.is_equal)
                    step(ins)
                    dve.tensor_reduce(sel[:, :], oh[:, :, :].rearrange("p k e -> p e k"), AX.X, ALU.add).then_inc(sel_done, 1)
                    dve.wait_ge(rank_ready, u + 1)
                    step(dve.tensor_tensor(pos[:, :], r_ps[:, 32:64], cst[:, C_BASE:C_BASE + N_EXP], ALU.add))
                    for k in range(TOP_K):
                        step(dve.tensor_tensor_reduce(junk[:, :], oh[:, k, :], pos[:, :], 1.0, 0.0, ALU.mult, ALU.add,
                                                      dst[:, u, k:k + 1]))
                    step(dve.tensor_tensor(acc[:, :], acc[:, :], sel[:, :], ALU.add))
                    dve.tensor_copy(dsti[:, u, :], dst[:, u, :]).then_inc(dst_done, 1)
            dve.tensor_tensor(gates[:, :, :], top[:, :, 0:TOP_K], top[:, :, 0:1].broadcast_to((P, NT, TOP_K)),
                              ALU.subtract).then_inc(gates_in, 1)
            dve.wait_ge(gates_exp, 1)
            step(dve.tensor_reduce(gsum[:, :], gates[:, :, :], AX.X, ALU.add))
            step(dve.reciprocal(gsum[:, :], gsum[:, :]))
            step(dve.tensor_tensor(gates[:, :, :], gates[:, :, :], gsum[:, :].unsqueeze(2).broadcast_to((P, NT, TOP_K)), ALU.mult))
            step(dve.memset(ec[:, :], 1.0))
            dve.wait_ge(cnt_ready, 1)
            step(dve.tensor_copy(ec[:, 2:3], r_ps[0:N_EXP, 64:65]))
            step(dve.tensor_scalar(ej[:, 0, 0:4], cst[0:N_EXP, C_STEP:C_STEP + 4], ec[:, 2:3], None, ALU.is_lt))
            dve.tensor_reduce(ec[:, 1:2], ej[:, 0, 0:4], AX.X, ALU.add).then_inc(jobs_step, 1)
            dve.wait_ge(jobs_step, 1)
            dve.wait_ge(cnt_ready, 2)
            step(dve.tensor_copy(ec[:, 4:5], r_ps[0:N_EXP, 65:66]))
            step(dve.tensor_tensor(ec[:, 3:4], ec[:, 4:5], ec[:, 1:2], ALU.add))
            step(dve.tensor_scalar(ej[:, 0, :], cst[0:N_EXP, C_JOB:C_JOB + NJ], ec[:, 3:4], None, ALU.is_ge))
            step(dve.tensor_scalar(ej[:, 1, :], cst[0:N_EXP, C_JOB:C_JOB + NJ], ec[:, 4:5], None, ALU.is_ge))
            dve.tensor_tensor(ej[:, 2, :], ej[:, 1, :], ej[:, 0, :], ALU.subtract).then_inc(jobs_step, 1)
            dve.wait_ge(cnt_ready, 3)
            step(dve.tensor_copy(jf[0:1, 0:3, :], r_ps[0:1, 128:128 + 3 * NJ].rearrange("p (r n) -> p r n", n=NJ)))
            step(dve.tensor_tensor(jf[0:1, 3, :], cst[0:1, C_JOB:C_JOB + NJ], jf[0:1, 1, :], ALU.subtract))
            step(dve.scalar_tensor_tensor(out=jf[0:1, 4, :], in0=jf[0:1, 3, :], scalar=-float(JOB), in1=jf[0:1, 2, :],
                                          op0=ALU.mult, op1=ALU.add))
            step(dve.tensor_scalar(jf[0:1, 5, :], jf[0:1, 4, :], float(P), None, ALU.is_gt))
            step(dve.tensor_scalar(jf[0:1, 0, :], jf[0:1, 0, :], float(N_EXP - 1), None, ALU.min))
            step(dve.tensor_scalar(jf[0:1, 3, :], jf[0:1, 3, :], 3.0, None, ALU.min))
            step(dve.tensor_scalar(jf[0:1, 3, :], jf[0:1, 3, :], float(JOB), None, ALU.mult))
            step(dve.scalar_tensor_tensor(out=jf[0:1, 4, :], in0=jf[0:1, 0, :], scalar=float(CAP), in1=jf[0:1, 3, :],
                                          op0=ALU.mult, op1=ALU.add))
            step(dve.tensor_copy(jobs[0:1, 0, :], jf[0:1, 0, :]))
            step(dve.tensor_copy(jobs[0:1, 1, :], jf[0:1, 4, :]))
            step(dve.tensor_copy(jobs[0:1, 2, :], jf[0:1, 5, :]))
            step(dve.tensor_copy(jobs[0:1, 3, 0:1], r_ps[0:1, 127:128]))

        @block.tensor
        def _(pe):
            ident = cst[:, C_ID:C_ID + P]
            pe.wait_ge(landed, 16 * NL)
            pe.wait_ge(ones_set, 1)

            def transpose_mixed(t):
                pe.wait_ge(head_done, t + 1)
                for b in range(2):
                    if t >= 1:
                        pe.wait_ge((mt_a, mt_v)[b], t)
                    for c in range(4):
                        k = 4 * b + c
                        ins = pe.transpose(tm_ps[:, b, c * P:(c + 1) * P], mixed[:, t, k * P:(k + 1) * P], ident)
                    ins.then_inc(tm_ready, 1)

            def project_out(t):
                pe.wait_ge(mt_a, t + 1)
                pe.wait_ge(mt_v, t + 1)
                if t >= 2:
                    pe.wait_ge(h2_done, 2 * (t - 1))
                for b in range(2):
                    for k in range(KC):
                        ins = pe.matmul(o_ps[:, 2 * (t % 2) + b, :], mt[:, t % 2, k, :], w_sb[:, k, 512 * b:512 * b + 512],
                                        start=(k == 0), stop=(k == KC - 1))
                    ins.then_inc(o_ready, 1)

            def router(t):
                pe.wait_ge(v_done, t + 1)
                for b in range(2):
                    if 2 * t + b >= 1:
                        pe.wait_ge(vt_done, 2 * t + b)
                    for c in range(4):
                        k = 4 * b + c
                        ins = pe.transpose(tv_ps[:, c * P:(c + 1) * P], vs[:, t % 2, k * P:(k + 1) * P], ident)
                    ins.then_inc(tv_ready, 1)
                pe.wait_ge(vt_done, 2 * t + 2)
                if t >= 1:
                    pe.wait_ge(dst_done, t)
                for k in range(KC):
                    ins = pe.matmul(r_ps[:, 0:N_EXP], vt[:, k, :], wr[:, k, :], start=(k == 0), stop=(k == KC - 1))
                ins.then_inc(r_ready, 1)
                pe.wait_ge(sel_done, t + 1)
                pe.matmul(r_ps[:, 32:64], ones[:, :], acc[:, :], start=True, stop=False)
                pe.matmul(r_ps[:, 32:64], cst[:, C_TRI:C_TRI + P], sel[:, :], start=False, stop=True).then_inc(rank_ready, 1)

            transpose_mixed(0)
            for t in range(NT):
                project_out(t)
                if t + 1 < NT:
                    transpose_mixed(t + 1)
                if t >= 1:
                    router(t - 1)
            router(NT - 1)
            pe.wait_ge(dst_done, NT)
            pe.matmul(r_ps[0:N_EXP, 64:65], acc[:, :], ones[:, 0:1], start=True, stop=True).then_inc(cnt_ready, 1)
            pe.wait_ge(jobs_step, 1)
            pe.matmul(r_ps[0:1, 127:128], ec[:, 1:2], ones[0:N_EXP, 0:1], start=True, stop=True)
            pe.matmul(r_ps[0:N_EXP, 65:66], cst[0:N_EXP, C_TRI:C_TRI + N_EXP], ec[:, 1:2], start=True, stop=True
                      ).then_inc(cnt_ready, 1)
            pe.wait_ge(jobs_step, 2)
            pe.matmul(r_ps[0:1, 128:128 + NJ], ones[0:N_EXP, 0:1], ej[:, 0, :], start=True, stop=True)
            pe.matmul(r_ps[0:1, 128 + NJ:128 + 2 * NJ], ec[:, 1:2], ej[:, 0, :], start=True, stop=True)
            pe.matmul(r_ps[0:1, 128 + 2 * NJ:128 + 3 * NJ], ec[:, 2:3], ej[:, 2, :], start=True, stop=True).then_inc(cnt_ready, 1)


def experts(nc, a, jobs, v_dram, slot_dram, y_dram):
    with ExitStack() as ctx:
        sb = lambda n, s, d=F32: ctx.enter_context(nc.sbuf_tensor(n, s, d))
        sem = lambda n: ctx.enter_context(nc.semaphore(n))
        ps = lambda n, s: ctx.enter_context(nc.psum_tensor(n, s, F32))
        NC, NP = 6, 12
        RAW, SPL, AHEAD = 3, 4, 3
        PK = KC // 2
        raw = sb("raw", [P, RAW, KC, 512])
        whi = sb("whi", [P, SPL, PK, 512], F32R)
        wlo = sb("wlo", [P, SPL, PK, 512], F32R)
        xg = sb("xg", [P, 2, D])
        xt_hi = sb("xt_hi", [P, 2, KC, P], F32R)
        xt_lo = sb("xt_lo", [P, 2, KC, P], F32R)
        ht_hi = sb("ht_hi", [P, 2, KC, P], F32R)
        ht_lo = sb("ht_lo", [P, 2, KC, P], F32R)
        gl = sb("gl", [P, 512])
        sg = sb("sg", [P, 256])
        hh = sb("hh", [P, 2, 2, 256])
        ys = sb("ys", [P, 2, D])
        brow = sb("brow", [1, 3 * D])
        bias = sb("bias", [P, 3 * D])
        idn = sb("idn", [P, 2, 2], U32)
        idc = sb("idc", [P, 2], U32)
        ident = sb("ident5", [P, P])
        m_ps = ps("m_ps", [P, 4, 512])
        y_ps = ps("y_ps", [P, 2, 512])
        t_ps = ps("t5_ps", [P, 2, 512])

        w_sem = [sem(f"w_landed{i}") for i in range(RAW)]
        ident_landed, setup = sem("ident_landed"), sem("setup5")
        hi_done, lo_done, w_used, a_ready = sem("hi_split"), sem("lo_split"), sem("w_used"), sem("a_ready")
        m_read = [sem("m_read_a"), sem("m_read_b")]
        sig_done = [sem("sig_a"), sem("sig_b")]
        h_ready = [sem("h_ready_a"), sem("h_ready_b")]
        t_ready = [sem("t_ready_a"), sem("t_ready_b")]
        t_hi, t_lo = [sem("t_hi_a"), sem("t_hi_b")], [sem("t_lo_a"), sem("t_lo_b")]
        y_done = [sem("y_done_a"), sem("y_done_b")]
        y_stored = [sem("y_stored_a"), sem("y_stored_b")]
        x_landed = [sem("x_gathered_a"), sem("x_gathered_b")]
        idx_landed, idx_kept, brow_landed = sem("idx_landed"), sem("idx_kept"), sem("brow_landed")
        bias1, bias2, one_added = sem("bias1_spread"), sem("bias2_spread"), sem("one_added")
        dve_chain = sem("dve_chain5")
        passed = sem("wait_passed")
        block = ctx.enter_context(nc.Block())

        w1 = a["w_mlp1"][0].rearrange("e (k p) (s c n) -> e p k s c n", p=P, s=2, c=4)
        w2 = a["w_mlp2"][0].rearrange("e (c k p) n -> e c p k n", c=2, p=P)
        M_BANK = lambda c, half: 2 * (c % 2) + half
        L = bass.ds

        def piece(k):
            k %= NP
            chunk = raw[:, (k // 2) % RAW, :, :]
            if k < 8:
                return chunk[:, PK * (k % 2):PK * (k % 2) + PK, :]
            return chunk.rearrange("p k n -> p (k n)").rearrange("p (k q n) -> p k q n", k=PK, q=2)[:, :, k % 2, :]

        def job_value(eng, row, j, top):
            return eng.value_load(jobs[0:1, row, L(j, 1)], min_val=0, max_val=top)

        def job_count(eng):
            return eng.value_load(jobs[0:1, 3, 0:1], min_val=1, max_val=MAX_JOBS)

        @block.sync
        def _(sp):
            sp.dma_start(ident[:, :], a["consts"][:, C_ID:C_ID + P]).then_inc(ident_landed, 16)

            def load(c, e):
                s = c % RAW
                if c % NC < 4:
                    for part in range(2):
                        dst = raw[:, s, :, 256 * part:256 * part + 256]
                        sp.dma_start(dst, w1[L(e, 1), :, :, part, c % NC, :].rearrange("o p k n -> (o p) k n")
                                     ).then_inc(w_sem[s], 16)
                else:
                    for part in range(2):
                        sp.dma_start(raw[:, s, :, :].rearrange("p k n -> p (k n)").rearrange("p (k n) -> p k n", k=4)[:, 2 * part:2 * part + 2, :],
                                     w2[L(e, 1), c % NC - 4, :, 2 * part:2 * part + 2, :].rearrange("o p k n -> (o p) k n")
                                     ).then_inc(w_sem[s], 16)
            n = job_count(sp)
            e0 = job_value(sp, 0, 0, N_EXP - 1)
            load(0, e0)
            load(1, e0)
            with sp.Fori(0, n) as j:
                e = job_value(sp, 0, j, N_EXP - 1)
                nxt = job_value(sp, 0, j + 1, N_EXP - 1)
                for c in range(2, NC + 2):
                    sp.wait_ge(hi_done, j * NP + (2 * c + 2))
                    sp.wait_ge(lo_done, j * NP + (2 * c + 2))
                    load(c, e if c < NC else nxt)
            sp.wait_ge(w_sem[0], n * 64 + 32)
            sp.wait_ge(w_sem[1], n * 64 + 32)
            sp.wait_ge(w_sem[2], n * 64)
            sp.sem_inc(passed, 1)

        @block.gpsimd
        def _(pool):
            pool.memset(xg[:, :, :], 0.0).then_inc(setup, 1)
            pool.memset(ys[:, :, :], 0.0).then_inc(setup, 1)
            pool.wait_ge(setup, 2)

            def load_idx(j):
                base = job_value(pool, 1, j, N_EXP * CAP - JOB)
                src = slot_dram[L(base, JOB), :].rearrange("(h p) c -> p h c", p=P)
                pool.dma_start(idn[:, :, :], src).then_inc(idx_landed, 16)

            def gather():
                for half in range(2):
                    pool.indirect_dma_start(out=xg[:, half, :], out_offset=None, in_=v_dram[:, :],
                                            in_offset=bass.IndirectOffsetOnAxis(ap=idn[:, half, 1:2], axis=0),
                                            bounds_check=SEQ - 1, oob_is_err=False).then_inc(x_landed[half], 16)

            def load_bias(e):
                for s in range(2):
                    pool.dma_start(brow[0:1, 0:2 * D].rearrange("p (c s n) -> p s c n", c=4, s=2)[:, s],
                                   a["b_mlp1"][0][L(e, 1), s * D:(s + 1) * D].rearrange("o (c n) -> o c n", c=4)
                                   ).then_inc(brow_landed, 16)
                pool.dma_start(brow[0:1, 2 * D:3 * D], a["b_mlp2"][0][L(e, 1), :]).then_inc(brow_landed, 16)

            def add_one(ahead):
                v = brow[0:1, 0:2 * D].rearrange("p (c s n) -> p s c n", c=4, s=2)[:, 1]
                pool.tensor_scalar(v, v, 1.0, None, ALU.add).then_inc(one_added, 1)
                pool.wait_ge(one_added, ahead)
                pool.sem_inc(passed, 1)

            load_idx(0)
            pool.wait_ge(idx_landed, 16)
            gather()
            load_bias(job_value(pool, 0, 0, N_EXP - 1))
            pool.tensor_copy(idc[:, :], idn[:, :, 0]).then_inc(idx_kept, 1)
            pool.wait_ge(brow_landed, 48)
            add_one(1)
            pool.partition_broadcast(bias[:, 0:2 * D], brow[0:1, 0:2 * D]).then_inc(bias1, 1)
            pool.partition_broadcast(bias[:, 2 * D:3 * D], brow[0:1, 2 * D:3 * D]).then_inc(bias2, 1)
            n = job_count(pool)
            with pool.Fori(0, n) as j:
                for half in range(2):
                    pool.wait_ge(x_landed[half], j * 16 + 16)
                pool.wait_ge(idx_kept, j + 1)
                pool.sem_inc(passed, 1)
                load_idx(j + 1)
                pool.wait_ge(idx_landed, j * 16 + 32)
                for half in range(2):
                    pool.wait_ge(t_ready[half], j * 6 + 2)
                pool.sem_inc(passed, 1)
                gather()
                pool.wait_ge(bias1, j + 1)
                pool.wait_ge(bias2, j + 1)
                pool.sem_inc(passed, 1)
                load_bias(job_value(pool, 0, j + 1, N_EXP - 1))
                pool.wait_ge(brow_landed, j * 48 + 96)
                for half in range(2):
                    pool.wait_ge(m_read[half], j * 4 + 6)
                pool.sem_inc(passed, 1)
                add_one(j + 2)
                pool.partition_broadcast(bias[:, 0:2 * D], brow[0:1, 0:2 * D]).then_inc(bias1, 1)
                for half in range(2):
                    pool.wait_ge(y_done[half], j * 2 + 4)
                    pool.sem_inc(passed, 1)
                    pool.indirect_dma_start(out=y_dram[:, :],
                                            out_offset=bass.IndirectOffsetOnAxis(ap=idc[:, half:half + 1], axis=0),
                                            in_=ys[:, half, :], in_offset=None,
                                            bounds_check=SEQ * TOP_K - 1, oob_is_err=False).then_inc(y_stored[half], 16)
                pool.partition_broadcast(bias[:, 2 * D:3 * D], brow[0:1, 2 * D:3 * D]).then_inc(bias2, 1)
                for half in range(2):
                    pool.wait_ge(y_stored[half], j * 16 + 16)
                pool.sem_inc(passed, 1)
                pool.tensor_copy(idc[:, :], idn[:, :, 0]).then_inc(idx_kept, 1)
            for half in range(2):
                pool.wait_ge(x_landed[half], n * 16 + 16)
                pool.wait_ge(idx_landed, n * 16 + 16)
            pool.sem_inc(passed, 1)

        @block.scalar
        def _(act):
            act.sem_inc(hi_done, 2 * RAW)

            def split(j, k):
                s, c = k % SPL, k // 2
                act.wait_ge(w_sem[c % RAW], j * 64 + 32 * (c // RAW + 1))
                act.wait_ge(w_used, j * NP + (k + 1))
                act.copy(whi[:, s, :, :], piece(k)).then_inc(hi_done, 1)

            def keep_hi(half, buf, k0, n, j, g):
                act.wait_ge(t_ready[half], j * 6 + (g + 3))
                act.copy(buf[:, half, k0:k0 + n, :], t_ps[:, half, 0:n * P].rearrange("p (k m) -> p k m", m=P)
                         ).then_inc(t_hi[half], 1)

            def body(j, halves):
                for k in range(NP):
                    c = k // 2
                    if k == 2 and len(halves) == 1:
                        act.wait_ge(t_hi[1], j * 6 + 2)
                        act.sem_inc(sig_done[1], 4)
                        act.sem_inc(t_hi[1], 4)
                    if k % 2 == 0 and 1 <= c <= 4:
                        for half in halves:
                            act.wait_ge(m_read[half], j * 4 + (c + 2))
                            act.activation(sg[:, :], gl[:, 0:256], ACT.Gelu_apprx_sigmoid).then_inc(sig_done[half], 1)
                    if k % 2 == 1 and 1 <= c <= 4:
                        for half in halves:
                            keep_hi(half, ht_hi, 2 * (c - 1), 2, j, c - 1)
                    if k >= 10:
                        for half in range(2):
                            keep_hi(half, xt_hi, 4 * (k - 10), 4, j, k - 6)
                    split(j, k + AHEAD)

            for g in range(2):
                for half in range(2):
                    act.wait_ge(t_ready[half], g + 1)
                    act.copy(xt_hi[:, half, 4 * g:4 * g + 4, :], t_ps[:, half, :].rearrange("p (k m) -> p k m", m=P)
                             ).then_inc(t_hi[half], 1)
            for k in range(AHEAD):
                split(0, k)
            n = job_count(act)
            with act.Fori(0, n) as j:
                both = job_value(act, 2, j, 1)
                with act.If(both > 0):
                    body(j, (0, 1))
                with act.Else():
                    body(j, (0,))

        @block.vector
        def _(dve):
            dve.sem_inc(lo_done, 2 * RAW)
            for half in range(2):
                dve.sem_inc(m_read[half], 2)
                dve.sem_inc(y_done[half], 2)

            def split(j, k):
                s = k % SPL
                dve.wait_ge(hi_done, j * NP + (2 * RAW + k + 1))
                dve.tensor_tensor(wlo[:, s, :, :], piece(k), whi[:, s, :, :].bitcast(F32), ALU.subtract).then_inc(lo_done, 1)

            def keep_lo(half, hi, lo, k0, n, j, g):
                dve.wait_ge(t_hi[half], j * 6 + (g + 3))
                dve.tensor_tensor(lo[:, half, k0:k0 + n, :], t_ps[:, half, 0:n * P].rearrange("p (k m) -> p k m", m=P),
                                  hi[:, half, k0:k0 + n, :].bitcast(F32), ALU.subtract).then_inc(t_lo[half], 1)

            def products(j, k, half, halves):
                if half == halves[-1]:
                    dve.wait_ge(w_used, j * NP + (SPL + k + 1))
                else:
                    dve.wait_ge(a_ready, j * NC + {1: 1, 3: 2, 5: 3, 7: 4, 10: 5, 11: 6}[k])

            def swiglu(j, c, half, halves, at):
                products(j, 2 * c + 1, half, halves)
                if c == 0:
                    dve.wait_ge(bias1, j + 1)
                if c >= 2:
                    dve.wait_ge(t_ready[half], j * 6 + (c + 1))
                dve.tensor_tensor(gl[:, :], m_ps[:, M_BANK(c, half), :], bias[:, 512 * c:512 * c + 512], ALU.add
                                  ).then_inc(m_read[half], 1)
                dve.wait_ge(m_read[half], j * 4 + (c + 3))
                dve.tensor_scalar(gl[:, 256:512], gl[:, 256:512], LIMIT + 1.0, 1.0 - LIMIT, ALU.min, ALU.max).then_inc(dve_chain, 1)
                dve.wait_ge(dve_chain, at + 1)
                dve.wait_ge(sig_done[half], j * 4 + (c + 1))
                dve.scalar_tensor_tensor(out=hh[:, half, c % 2, :], in0=sg[:, :], scalar=GLU_LIMIT, in1=gl[:, 256:512],
                                         op0=ALU.min, op1=ALU.mult).then_inc(h_ready[half], 1)
                dve.wait_ge(h_ready[half], j * 4 + (c + 1))

            def finish(j, q, half, halves):
                products(j, 10 + q, half, halves)
                if q == 0:
                    dve.wait_ge(bias2, j + 1)
                    dve.wait_ge(idx_kept, j + 1)
                src = y_ps[:, q, :] if half == 0 else m_ps[:, 2 * q + 1, :]
                dve.tensor_tensor(ys[:, half, 512 * q:512 * q + 512], src, bias[:, 2 * D + 512 * q:2 * D + 512 * q + 512],
                                  ALU.add).then_inc(y_done[half], 1)

            def body(j, halves):
                for k in range(NP):
                    c = k // 2
                    if k == 2 and len(halves) == 1:
                        dve.wait_ge(t_lo[1], j * 6 + 2)
                        dve.wait_ge(y_done[1], j * 2 + 2)
                        for s, m in ((m_read, 4), (h_ready, 4), (t_lo, 4), (y_done, 2)):
                            dve.sem_inc(s[1], m)
                    if k % 2 == 0 and 1 <= c <= 4:
                        for half in halves:
                            swiglu(j, c - 1, half, halves, j * 8 + 2 * (c - 1) + half)
                        if len(halves) == 1:
                            dve.sem_inc(dve_chain, 1)
                    if k % 2 == 1 and 1 <= c <= 4:
                        for half in halves:
                            keep_lo(half, ht_hi, ht_lo, 2 * (c - 1), 2, j, c - 1)
                    if k >= 10:
                        for half in range(2):
                            keep_lo(half, xt_hi, xt_lo, 4 * (k - 10), 4, j, k - 6)
                    if k == 11:
                        for half in halves:
                            finish(j, 0, half, halves)
                    split(j, k + AHEAD)
                for half in halves:
                    finish(j, 1, half, halves)

            for g in range(2):
                for half in range(2):
                    dve.wait_ge(t_hi[half], g + 1)
                    dve.tensor_tensor(xt_lo[:, half, 4 * g:4 * g + 4, :], t_ps[:, half, :].rearrange("p (k m) -> p k m", m=P),
                                      xt_hi[:, half, 4 * g:4 * g + 4, :].bitcast(F32), ALU.subtract).then_inc(t_lo[half], 1)
            for k in range(AHEAD):
                split(0, k)
            n = job_count(dve)
            with dve.Fori(0, n) as j:
                both = job_value(dve, 2, j, 1)
                with dve.If(both > 0):
                    body(j, (0, 1))
                with dve.Else():
                    body(j, (0,))

        @block.tensor
        def _(pe):
            pe.sem_inc(w_used, SPL)

            def transpose_x(half, g):
                for c in range(4):
                    k = 4 * g + c
                    ins = pe.transpose(t_ps[:, half, c * P:(c + 1) * P], xg[:, half, k * P:(k + 1) * P], ident[:, :])
                ins.then_inc(t_ready[half], 1)

            def transpose_h(j, c, half):
                pe.wait_ge(h_ready[half], j * 4 + (c + 1))
                pe.wait_ge(t_lo[half], j * 6 + (c + 2))
                for i in range(2):
                    ins = pe.transpose(t_ps[:, half, i * P:(i + 1) * P], hh[:, half, c % 2, i * P:(i + 1) * P], ident[:, :])
                ins.then_inc(t_ready[half], 1)

            def multiply(j, k, half):
                c, s = k // 2, k % SPL
                first = k < 8
                q = k % 2
                xh, xl = (xt_hi, xt_lo) if first else (ht_hi, ht_lo)
                if first:
                    bank = m_ps[:, M_BANK(c, half), :]
                else:
                    bank = y_ps[:, q, :] if half == 0 else m_ps[:, 2 * q + 1, :]
                if first and k % 2 == 0:
                    pe.wait_ge(m_read[half], j * 4 + (c + 1))
                    if half == 1 and k in (0, 2):
                        pe.wait_ge(y_done[1], j * 2 + 2)
                if k in (8, 9):
                    if half == 0:
                        pe.wait_ge(y_done[0], j * 2 + (q + 1))
                    else:
                        pe.wait_ge(m_read[1], j * 4 + (q + 5))
                need = {0: 1, 1: 2, 8: 4, 10: 6}.get(k)
                if need is not None:
                    pe.wait_ge(t_lo[half], j * 6 + need)
                n = 0
                for i in range(PK):
                    kc = PK * (k % 2 if first else (k - 8) // 2) + i
                    start = k % 2 == 0 if first else k in (8, 9)
                    stop = k % 2 == 1 if first else k in (10, 11)
                    for x, w in ((xh, whi), (xh, wlo), (xl, whi)):
                        n += 1
                        ins = pe.matmul(bank, x[:, half, kc, :], w[:, s, i, :], start=(start and n == 1),
                                        stop=(stop and n == 3 * PK), skip_group_check=True)
                return ins

            def body(j, halves):
                for k in range(NP):
                    c = k // 2
                    pe.wait_ge(hi_done, j * NP + (2 * RAW + k + 1))
                    pe.wait_ge(lo_done, j * NP + (2 * RAW + k + 1))
                    if k == 2 and len(halves) == 1:
                        skip_b(j)
                    for half in halves:
                        ins = multiply(j, k, half)
                        if half != halves[-1] and k in (1, 3, 5, 7, 10, 11):
                            ins.then_inc(a_ready, 1)
                    ins.then_inc(w_used, 1)
                    if k % 2 == 0 and 1 <= c <= 4:
                        for half in halves:
                            transpose_h(j, c - 1, half)
                    if k in (9, 10):
                        for half in range(2):
                            if k == 9:
                                pe.wait_ge(x_landed[half], j * 16 + 32)
                                pe.wait_ge(t_lo[half], j * 6 + 6)
                            else:
                                pe.wait_ge(t_lo[half], j * 6 + 7)
                            transpose_x(half, k - 9)

            def skip_b(j):
                pe.wait_ge(t_lo[1], j * 6 + 2)
                pe.wait_ge(y_done[0], j * 2 + 2)
                pe.sem_inc(t_ready[1], 4)
                pe.sem_inc(a_ready, NC)

            pe.wait_ge(ident_landed, 16)
            for g in range(2):
                for half in range(2):
                    if g == 0:
                        pe.wait_ge(x_landed[half], 16)
                    else:
                        pe.wait_ge(t_lo[half], 1)
                    transpose_x(half, g)
            n = job_count(pe)
            with pe.Fori(0, n) as j:
                both = job_value(pe, 2, j, 1)
                with pe.If(both > 0):
                    body(j, (0, 1))
                with pe.Else():
                    body(j, (0,))


def combine(nc, gates, h2_dram, y_dram, out):
    with ExitStack() as ctx:
        sb = lambda n, s, d=F32: ctx.enter_context(nc.sbuf_tensor(n, s, d))
        sem = lambda n: ctx.enter_context(nc.semaphore(n))
        yk = sb("yk", [P, 2, TOP_K * D])
        h2 = sb("h2_in", [P, 2, D])
        y_sem = [sem(f"yk_landed{i}") for i in range(2)]
        o_sem = [sem(f"out_stored{i}") for i in range(2)]
        added = sem("added")
        block = ctx.enter_context(nc.Block())

        @block.sync
        def _(sp):
            for t in range(NT):
                b = t % 2
                if t >= 2:
                    sp.wait_ge(added, TOP_K * (t - 1))
                    sp.wait_ge(o_sem[b], 16 * (t // 2))
                sp.dma_start(yk[:, b, :], y_dram[t * P * TOP_K:(t + 1) * P * TOP_K, :].rearrange("(p k) d -> p (k d)", k=TOP_K)
                             ).then_inc(y_sem[b], 16)
                sp.dma_start(h2[:, b, :], h2_dram[t * P:(t + 1) * P, :]).then_inc(y_sem[b], 16)

        @block.scalar
        def _(act):
            for t in range(NT):
                act.wait_ge(added, TOP_K * (t + 1))
                act.dma_start(out[0, t * P:(t + 1) * P, :], h2[:, t % 2, :]).then_inc(o_sem[t % 2], 16)
            for b in range(2):
                act.wait_ge(o_sem[b], 16 * (NT // 2))

        @block.vector
        def _(dve):
            for t in range(NT):
                b = t % 2
                dve.wait_ge(y_sem[b], 32 * (t // 2 + 1))
                for k in range(TOP_K):
                    if k:
                        dve.wait_ge(added, TOP_K * t + k)
                    dve.scalar_tensor_tensor(out=h2[:, b, :], in0=yk[:, b, k * D:(k + 1) * D], scalar=gates[:, t, k:k + 1],
                                             in1=h2[:, b, :], op0=ALU.mult, op1=ALU.add).then_inc(added, 1)


def build(nc, a, out):
    dram = lambda n, s, d=F32: nc.dram_tensor(n, s, d, kind="Internal").ap()
    qk_dram = dram("qk_dram", [2, R_W, KEYS])
    h2_dram, v_dram = dram("h2_dram", [SEQ, D]), dram("v_dram", [SEQ, D])
    y_dram = dram("y_dram", [SEQ * TOP_K, D])
    slot_dram = dram("slot_dram", [N_EXP * CAP, 2], U32)
    with nc.sbuf_tensor("gates", [P, NT, TOP_K], F32) as gates, nc.sbuf_tensor("jobs", [1, 4, NJ], I32) as jobs:
        with nc.sbuf_tensor("v_all", [P, NT + 1, 640], F32) as v_all:
            project(nc, a, v_all, qk_dram)
            with nc.sbuf_tensor("mixed", [P, NT, D], F32) as mixed:
                attend_window(nc, a, v_all, mixed, qk_dram)
                attend_diff(nc, a, v_all, mixed, qk_dram)
                route(nc, a, mixed, gates, jobs, h2_dram, v_dram, slot_dram)
        experts(nc, a, jobs, v_dram, slot_dram, y_dram)
        combine(nc, gates, h2_dram, y_dram, out)


def rope_table():
    pos = np.concatenate([np.arange(N_META, KEYS), np.arange(N_META)]).astype(np.float32)
    cols = []
    for d in (DH, DQ):
        inv = (np.float32(10000.0) ** (-np.arange(0, d, 2, dtype=np.float32) / np.float32(d))).astype(np.float32)
        ang = pos[:, None] * inv[None, :]
        cols += [np.cos(ang), np.sin(ang)]
    return np.concatenate(cols, 1).astype(np.float32)


def band_masks():
    q, k = np.arange(P)[:, None], np.arange(P)[None, :]
    prev, nxt = np.where(k >= q, 0.0, NEG), np.where(k <= q, 0.0, NEG)
    m = np.zeros((P, 3, 3 * P + N_META), np.float32)
    m[:, 0, P:2 * P] = nxt
    m[:, 1, 0:P], m[:, 1, 2 * P:3 * P] = prev, nxt
    m[:, 2, 0:P] = prev
    return m


def constants():
    c = np.zeros((P, C_W), np.float32)
    i = np.arange(P)
    c[:, C_ID:C_ID + P] = np.eye(P)
    c[:, C_TRI:C_TRI + P] = i[:, None] < i[None, :]
    c[:, C_EXP:C_EXP + N_EXP] = np.arange(N_EXP)
    c[:, C_BASE:C_BASE + N_EXP] = np.arange(N_EXP) * CAP
    c[:, C_JOB:C_JOB + NJ] = np.arange(NJ)
    c[:, C_STEP:C_STEP + 4] = np.arange(4) * JOB
    return c


_INS = ["x", "meta_tokens", "g_attn", "w_in", "g_q_swa", "g_k_swa", "g_q_diff", "g_k_diff", "sink_swa",
        "lambda_q1", "lambda_k1", "lambda_q2", "lambda_k2", "g_diff_head", "w_out", "g_ffn",
        "w_router", "b_router", "w_mlp1", "b_mlp1", "w_mlp2", "b_mlp2"]


def kernel(**inputs):
    import concourse.bacc as bacc
    from concourse.bass_utils import run_bass_kernel_spmd

    nc = bacc.Bacc("TRN2", target_bir_lowering=False, num_devices=1)
    arrays = {f"in_{n}": np.ascontiguousarray(inputs[n]) for n in _INS}
    arrays |= {"in_rope": rope_table(), "in_masks": band_masks(), "in_consts": constants(),
               "in_ones": np.ones((P, P), np.float32)}
    aps = {n[3:]: nc.dram_tensor(n, v.shape, mybir.dt.from_np(v.dtype), kind="ExternalInput").ap()
           for n, v in arrays.items()}
    out = nc.dram_tensor("out_h", (1, SEQ, D), F32, kind="ExternalOutput").ap()
    build(nc, aps, out)
    r = run_bass_kernel_spmd(nc, [arrays], core_ids=[0])
    return r.results[0]["out_h"]
```

```python
import math
from contextlib import ExitStack

import numpy as np

import concourse.bass as bass
from concourse import mybir

F32 = mybir.dt.float32
F32R = mybir.dt.float32r
I32 = mybir.dt.int32
U32 = mybir.dt.uint32
ALU = mybir.AluOpType
ACT = mybir.ActivationFunctionType
AX = mybir.AxisListType

P = 128
D = 1024
KC = D // P
SEQ = 1024
NT = SEQ // P
N_META = 16
KEYS = SEQ + N_META
EPS = 1e-6
EPS_HEAD = 1e-5
HQ, HKV, DH = 8, 2, 64
G = HQ // HKV
HD, DQ, DV = 8, 32, 64
LAMBDA_INIT = 0.8 - 0.6 * math.exp(0.0)
QA, KA, VA, QD, KD, VD, IN_W = 0, 512, 640, 768, 1280, 1792, 2304
R_KA, R_QD, R_KD, R_W = 512, 640, 1152, 1664
RC = R_W // P
N_EXP, TOP_K = 32, 4
LIMIT, ALPHA = 7.0, 1.702
GLU_LIMIT = LIMIT / (1.0 + math.exp(-ALPHA * LIMIT))
CAP = SEQ
JOB = 2 * P
FEW = P // 2
MAX_JOBS = N_EXP + SEQ * TOP_K // JOB - 1
NJ = 64
NEG = -1e30


def chained(eng, sem):
    n = [0]

    def step(ins):
        n[0] += 1
        ins.then_inc(sem, 1)
        eng.wait_ge(sem, n[0])
    return step


def project(nc, a, v_all, qk_dram):
    with ExitStack() as ctx:
        sb = lambda n, s, d=F32: ctx.enter_context(nc.sbuf_tensor(n, s, d))
        sem = lambda n: ctx.enter_context(nc.semaphore(n))
        w_sb = sb("w_in_sb", [P, KC, IN_W])
        xs = sb("xs", [P, 2, D])
        us = sb("us", [P, 2, D])
        ut = sb("ut", [P, 2, KC, P])
        g_sb = sb("g_attn_sb", [P, D])
        rope = sb("rope_sb", [P, NT + 1, 96])
        gains = sb("gains_sb", [P, 2, DH])
        gaind = sb("gaind_sb", [P, 2, DQ])
        ident = sb("ident1", [P, P])
        pr = sb("pr", [P, 2, IN_W])
        qn = sb("qn", [P, R_W])
        t1 = sb("t1", [P, R_W])
        t2 = sb("t2", [P, R_W])
        ro = sb("ro", [P, 2, R_W])
        hi = sb("qk_hi", [P, 2, RC, P], F32R)
        lo = sb("qk_lo", [P, 2, RC, P], F32R)
        ss = sb("ss1", [P, NT + 1])
        rs = sb("rs1", [P, NT + 1])
        hs = sb("hs", [P, 42])
        hr = sb("hr", [P, 42])
        eps = sb("eps1", [P, 1])
        ptu = ctx.enter_context(nc.psum_tensor("ptu", [P, 2, 512], F32))
        ptq = ctx.enter_context(nc.psum_tensor("ptq", [P, 2, 512], F32))
        pp = ctx.enter_context(nc.psum_tensor("pp", [P, 4, 512], F32))

        w_in_sem = [sem(f"w_landed{k}") for k in range(KC)]
        x_sem = [sem(f"x_landed{i}") for i in range(2)]
        const_landed, consts_set = sem("const_landed"), sem("consts_set")
        ss_done, std_done, rs_done, u_done = sem("ss_done"), sem("std_done"), sem("rs_done"), sem("u_done")
        ut_ps, ut_a, ut_v = sem("u_transposed"), sem("ut_copied_act"), sem("ut_copied_dve")
        proj_ps, proj_out = sem("proj_ready"), sem("proj_copied")
        sq_done, hs_done, hstd_done = sem("head_squares"), sem("head_sums"), sem("head_std")
        qn_done, gain_done, t1_done, t2_done, ro_done = (sem("qn_done"), sem("gain_done"), sem("t1_done"),
                                                        sem("t2_done"), sem("rotated"))
        qk_ps, hi_done, lo_done = sem("qk_transposed"), sem("hi_done"), sem("lo_done")
        qk_stored = [sem(f"qk_stored{i}") for i in range(2)]
        dve_chain = sem("dve_chain1")

        T = NT + 1
        rows = [P] * NT + [N_META]
        colgroups = [[(0, 512), (512, 1024), (1024, 1536), (1536, 2048), (2048, 2304)]] * NT + \
                    [[(512, 768), (1280, 1792), (1792, 2304)]]
        chunks = [list(range(RC))] * NT + [[4, 9, 10, 11, 12]]
        tgroups = [[c[i:i + 4] for i in range(0, len(c), 4)] for c in chunks]
        ngroups_before = [sum(len(x) for x in colgroups[:t]) for t in range(T + 1)]
        ntg_before = [sum(len(x) for x in tgroups[:t]) for t in range(T + 1)]
        turned_after = [{}] + [{2: (0, 1), 3: (2, 3)}] * (NT - 1) + [{2: (0, 1, 2, 3)}]
        heads_a = [(0, 10)] * NT + [(8, 10)]
        heads_d = [(0, 32)] * NT + [(16, 32)]
        gain_ops = [4] * NT + [2]

        def view_a(ap, t):
            h0, h1 = heads_a[t]
            return ap[:, h0 * DH:h1 * DH].rearrange("p (h d) -> p h d", d=DH)

        def view_d(ap, t, base):
            h0, h1 = heads_d[t]
            return ap[:, base + h0 * DQ:base + h1 * DQ].rearrange("p (h d) -> p h d", d=DQ)

        def halves(ap, t, base):
            r = rows[t]
            va = view_a(ap[0:r], t).rearrange("p h (s d) -> p h s d", s=2)
            vd = view_d(ap[0:r], t, base).rearrange("p h (s d) -> p h s d", s=2)
            return va, vd

        block = ctx.enter_context(nc.Block())

        @block.sync
        def _(sp):
            def load_x(t):
                if t >= 2:
                    sp.wait_ge(u_done, t - 1)
                src = a["x"][0, t * P:(t + 1) * P, :] if t < NT else a["meta_tokens"][:, :]
                sp.dma_start(xs[0:rows[t], t % 2, :], src).then_inc(x_sem[t % 2], 16)
            load_x(0)
            sp.dma_start(g_sb[:, :], a["g_attn"][0, :].partition_broadcast(P)).then_inc(const_landed, 16)
            sp.dma_start(ident[:, :], a["consts"][:, 0:P]).then_inc(const_landed, 16)
            load_x(1)
            for k in range(KC):
                sp.dma_start(w_sb[:, k, :], a["w_in"][0, k * P:(k + 1) * P, :]).then_inc(w_in_sem[k], 16)
                if k == 0:
                    sp.dma_start(rope[:, 0:NT, :], a["rope"][0:SEQ, :].rearrange("(t p) n -> p t n", p=P)
                                 ).then_inc(const_landed, 16)
                    sp.dma_start(rope[0:N_META, NT, :], a["rope"][SEQ:KEYS, :]).then_inc(const_landed, 16)
                    for i, n in enumerate(("g_q_swa", "g_k_swa")):
                        sp.dma_start(gains[:, i, :], a[n][0, :].partition_broadcast(P)).then_inc(const_landed, 16)
                    for i, n in enumerate(("g_q_diff", "g_k_diff")):
                        sp.dma_start(gaind[:, i, :], a[n][0, :].partition_broadcast(P)).then_inc(const_landed, 16)
            load_x(2)
            stored = [0, 0]
            for t in range(T):
                r = rows[t]
                if t + 3 < T:
                    load_x(t + 3)
                sp.wait_ge(hi_done, ntg_before[t + 1])
                sp.wait_ge(lo_done, ntg_before[t + 1])
                c0 = t * P
                for part, buf in ((0, hi), (1, lo)):
                    dst = qk_dram[part].rearrange("(c p) n -> p c n", p=P)[:, :, c0:c0 + r]
                    for x0, x1 in ([(0, RC)] if t < NT else [(4, 5), (9, 13)]):
                        sp.dma_start(dst[:, x0:x1, :], buf[:, t % 2, x0:x1, 0:r].bitcast(F32)).then_inc(qk_stored[t % 2], 16)
                        stored[t % 2] += 16
            for i in range(2):
                sp.wait_ge(qk_stored[i], stored[i])

        stored_before = [0 if t < 2 else 32 * (t // 2) for t in range(T)]

        @block.scalar
        def _(act):
            def norm(t):
                r = rows[t]
                act.wait_ge(x_sem[t % 2], 16 * (t // 2 + 1))
                if t >= 2:
                    act.wait_ge(ut_ps, 2 * (t - 1))
                act.activation(us[0:r, t % 2, :], xs[0:r, t % 2, :], ACT.Square, accum_out=ss[0:r, t:t + 1]).then_inc(ss_done, 1)
                act.wait_ge(ss_done, t + 1)
                act.wait_ge(consts_set, 1)
                act.activation(rs[0:r, t:t + 1], ss[0:r, t:t + 1], ACT.Sqrt, bias=eps[0:r], scale=1.0 / D
                               ).then_inc(std_done, 1)

            def copy_ut(t):
                r = rows[t]
                act.wait_ge(ut_ps, 2 * t + 1)
                if t >= 2:
                    act.wait_ge(proj_ps, ngroups_before[t - 1])
                act.copy(ut[:, t % 2, 0:4, 0:r], ptu[:, 0, :].rearrange("p (c n) -> p c n", n=P)[:, :, 0:r]
                         ).then_inc(ut_a, 1)

            def copy_hi(t, groups):
                r = rows[t]
                if t >= 2:
                    act.wait_ge(qk_stored[t % 2], stored_before[t])
                for i in groups:
                    cs = tgroups[t][i]
                    n = ntg_before[t] + i
                    act.wait_ge(qk_ps, n + 1)
                    runs = [cs] if cs[-1] - cs[0] == len(cs) - 1 else [cs[:1], cs[1:]]
                    at = 0
                    for run in runs:
                        ins = act.copy(hi[:, t % 2, run[0]:run[-1] + 1, 0:r],
                                       ptq[:, n % 2, at * P:(at + len(run)) * P].rearrange("p (c n) -> p c n", n=P)[:, :, 0:r])
                        at += len(run)
                    ins.then_inc(hi_done, 1)

            norm(0)
            copy_ut(0)
            norm(1)
            for t in range(T):
                r = rows[t]
                if t >= 2:
                    act.wait_ge(ro_done, 4 * (t - 1))
                for i, (c0, c1) in enumerate(colgroups[t]):
                    n = ngroups_before[t] + i
                    act.wait_ge(proj_ps, n + 1)
                    act.copy(pr[0:r, t % 2, c0:c1], pp[0:r, n % 4, 0:c1 - c0]).then_inc(proj_out, 1)
                    if i == 0 and t + 1 < T:
                        copy_ut(t + 1)
                    if i == 0 and t + 2 < T:
                        norm(t + 2)
                    if i in turned_after[t]:
                        copy_hi(t - 1, turned_after[t][i])
                act.wait_ge(hs_done, t + 1)
                act.activation(hr[0:r, :], hs[0:r, :], ACT.Sqrt, bias=eps[0:r]).then_inc(hstd_done, 1)
            copy_hi(T - 1, range(len(tgroups[T - 1])))

        @block.vector
        def _(dve):
            step = chained(dve, dve_chain)
            dve.memset(hs[:, :], 1.0)
            dve.memset(eps[:, :], EPS).then_inc(consts_set, 1)
            dve.wait_ge(const_landed, 16 * 8)
            step(dve.tensor_scalar(gains[:, 0, :], gains[:, 0, :], DH ** -0.5, None, ALU.mult))
            step(dve.tensor_scalar(gaind[:, 0, :], gaind[:, 0, :], DQ ** -0.5, None, ALU.mult))

            def norm(t):
                r = rows[t]
                dve.wait_ge(std_done, t + 1)
                dve.reciprocal(rs[0:r, t:t + 1], rs[0:r, t:t + 1]).then_inc(rs_done, 1)
                dve.wait_ge(rs_done, t + 1)
                if t >= 2:
                    dve.wait_ge(ut_ps, 2 * (t - 1))
                dve.scalar_tensor_tensor(out=us[0:r, t % 2, :], in0=xs[0:r, t % 2, :], scalar=rs[0:r, t:t + 1],
                                         in1=g_sb[0:r, :], op0=ALU.mult, op1=ALU.mult).then_inc(u_done, 1)

            def copy_ut(t):
                r = rows[t]
                dve.wait_ge(ut_ps, 2 * t + 2)
                if t >= 2:
                    dve.wait_ge(proj_ps, ngroups_before[t - 1])
                dve.tensor_copy(ut[:, t % 2, 4:8, 0:r], ptu[:, 1, :].rearrange("p (c n) -> p c n", n=P)[:, :, 0:r]
                                ).then_inc(ut_v, 1)

            def head_sums(t):
                r = rows[t]
                (a0, a1), (d0, d1) = heads_a[t], heads_d[t]
                dve.wait_ge(sq_done, 2 * (t + 1))
                step(dve.tensor_reduce(hs[0:r, a0:a1], view_a(t1[0:r], t), AX.X, ALU.add))
                step(dve.tensor_reduce(hs[0:r, 10 + d0:10 + d1], view_d(t1[0:r], t, R_QD), AX.X, ALU.add))
                step(dve.tensor_scalar(hs[0:r, a0:a1], hs[0:r, a0:a1], 1.0 / DH, None, ALU.mult))
                dve.tensor_scalar(hs[0:r, 10 + d0:10 + d1], hs[0:r, 10 + d0:10 + d1], 1.0 / DQ, None,
                                  ALU.mult).then_inc(hs_done, 1)

            def rotate(t):
                r = rows[t]
                (a0, a1), (d0, d1) = heads_a[t], heads_d[t]
                dve.wait_ge(hstd_done, t + 1)
                step(dve.reciprocal(hr[0:r, :], hr[0:r, :]))
                if t >= 1:
                    dve.wait_ge(t1_done, 2 * t)
                    dve.wait_ge(t2_done, 4 * t)
                dve.tensor_tensor(view_a(qn[0:r], t), view_a(pr[0:r, t % 2], t),
                                  hr[0:r, a0:a1].unsqueeze(2).broadcast_to((r, a1 - a0, DH)), ALU.mult).then_inc(qn_done, 1)
                dve.tensor_tensor(view_d(qn[0:r], t, R_QD), view_d(pr[0:r, t % 2], t, QD),
                                  hr[0:r, 10 + d0:10 + d1].unsqueeze(2).broadcast_to((r, d1 - d0, DQ)), ALU.mult).then_inc(qn_done, 1)
                dve.wait_ge(gain_done, sum(gain_ops[:t + 1]))
                qa, qd = halves(qn, t, R_QD)
                ta, td = halves(t1, t, R_QD)
                sa, sd = halves(t2, t, R_QD)
                oa, od = halves(ro[:, t % 2], t, R_QD)
                for q, o, h, c, n in ((qa, ta, a1 - a0, 0, 32), (qd, td, d1 - d0, 64, 16)):
                    cos = rope[0:r, t, c:c + n].unsqueeze(1).broadcast_to((r, h, n))
                    for s in range(2):
                        ins = dve.tensor_tensor(o[:, :, s, :], q[:, :, s, :], cos, ALU.mult)
                    ins.then_inc(t1_done, 1)
                dve.wait_ge(t1_done, 2 * (t + 1))
                dve.wait_ge(t2_done, 4 * (t + 1))
                if t >= 2:
                    dve.wait_ge(qk_ps, ntg_before[t - 1])
                for o, x, y in ((oa, ta, sa), (od, td, sd)):
                    dve.tensor_tensor(o[:, :, 0, :], x[:, :, 0, :], y[:, :, 0, :], ALU.subtract).then_inc(ro_done, 1)
                    dve.tensor_tensor(o[:, :, 1, :], x[:, :, 1, :], y[:, :, 1, :], ALU.add).then_inc(ro_done, 1)

            def low(t):
                r = rows[t]
                if t >= 2:
                    dve.wait_ge(qk_stored[t % 2], stored_before[t])
                for i, cs in enumerate(tgroups[t]):
                    n = ntg_before[t] + i
                    dve.wait_ge(hi_done, n + 1)
                    runs = [cs] if cs[-1] - cs[0] == len(cs) - 1 else [cs[:1], cs[1:]]
                    at = 0
                    for run in runs:
                        k = slice(run[0], run[-1] + 1)
                        ins = dve.tensor_tensor(lo[:, t % 2, k, 0:r],
                                                ptq[:, n % 2, at * P:(at + len(run)) * P].rearrange("p (c n) -> p c n", n=P)[:, :, 0:r],
                                                hi[:, t % 2, k, 0:r].bitcast(F32), ALU.subtract)
                        at += len(run)
                    ins.then_inc(lo_done, 1)

            norm(0)
            copy_ut(0)
            norm(1)
            for t in range(T):
                if t + 1 < T:
                    copy_ut(t + 1)
                if t + 2 < T:
                    norm(t + 2)
                if t >= 1:
                    low(t - 1)
                head_sums(t)
                rotate(t)
            low(T - 1)

        @block.gpsimd
        def _(pool):
            pool.wait_ge(const_landed, 16 * 8)
            for t in range(T):
                r = rows[t]
                (a0, a1), (d0, d1) = heads_a[t], heads_d[t]
                pool.wait_ge(proj_out, ngroups_before[t + 1])
                if t >= 1:
                    pool.wait_ge(ro_done, 4 * t)
                pool.tensor_tensor(view_a(t1[0:r], t), view_a(pr[0:r, t % 2], t), view_a(pr[0:r, t % 2], t),
                                   ALU.mult).then_inc(sq_done, 1)
                pool.tensor_tensor(view_d(t1[0:r], t, R_QD), view_d(pr[0:r, t % 2], t, QD),
                                   view_d(pr[0:r, t % 2], t, QD), ALU.mult).then_inc(sq_done, 1)
                vw = v_all[0:r, t, :]
                pool.tensor_copy(vw[:, 0:128], pr[0:r, t % 2, VA:VA + 128])
                pool.tensor_copy(vw[:, 128:640], pr[0:r, t % 2, VD:VD + 512])
                pool.wait_ge(qn_done, 2 * (t + 1))
                for h0, h1, g in ((0, 8, 0), (8, 10, 1)):
                    if h0 >= a0:
                        v = qn[0:r, h0 * DH:h1 * DH].rearrange("p (h d) -> p h d", d=DH)
                        pool.tensor_tensor(v, v, gains[0:r, g, :].unsqueeze(1).broadcast_to((r, h1 - h0, DH)),
                                           ALU.mult).then_inc(gain_done, 1)
                for h0, h1, g in ((0, 16, 0), (16, 32, 1)):
                    if h0 >= d0:
                        v = qn[0:r, R_QD + h0 * DQ:R_QD + h1 * DQ].rearrange("p (h d) -> p h d", d=DQ)
                        pool.tensor_tensor(v, v, gaind[0:r, g, :].unsqueeze(1).broadcast_to((r, h1 - h0, DQ)),
                                           ALU.mult).then_inc(gain_done, 1)
                pool.wait_ge(gain_done, sum(gain_ops[:t + 1]))
                if t >= 1:
                    pool.wait_ge(ro_done, 4 * t)
                qa, qd = halves(qn, t, R_QD)
                sa, sd = halves(t2, t, R_QD)
                for q, o, h, c, n in ((qa, sa, a1 - a0, 32, 32), (qd, sd, d1 - d0, 80, 16)):
                    sin = rope[0:r, t, c:c + n].unsqueeze(1).broadcast_to((r, h, n))
                    for s in range(2):
                        pool.tensor_tensor(o[:, :, s, :], q[:, :, 1 - s, :], sin, ALU.mult).then_inc(t2_done, 1)

        @block.tensor
        def _(pe):
            def transpose_u(t):
                r = rows[t]
                pe.wait_ge(u_done, t + 1)
                for b in range(2):
                    if t >= 1:
                        pe.wait_ge((ut_a, ut_v)[b], t)
                    for c in range(4):
                        k = 4 * b + c
                        ins = pe.transpose(ptu[:, b, c * P:c * P + r], us[0:r, t % 2, k * P:(k + 1) * P], ident[0:r, 0:r])
                    ins.then_inc(ut_ps, 1)

            def transpose_qk(t, groups):
                r = rows[t]
                pe.wait_ge(ro_done, 4 * (t + 1))
                for i in groups:
                    n = ntg_before[t] + i
                    if n >= 2:
                        pe.wait_ge(lo_done, n - 1)
                    for j, c in enumerate(tgroups[t][i]):
                        ins = pe.transpose(ptq[:, n % 2, j * P:j * P + r], ro[0:r, t % 2, c * P:(c + 1) * P], ident[0:r, 0:r])
                    ins.then_inc(qk_ps, 1)

            def product(t, i, k):
                r, (c0, c1), n = rows[t], colgroups[t][i], ngroups_before[t] + i
                ins = pe.matmul(pp[0:r, n % 4, 0:c1 - c0], ut[:, t % 2, k, 0:r], w_sb[:, k, c0:c1],
                                start=(k == 0), stop=(k == KC - 1))
                if k == KC - 1:
                    ins.then_inc(proj_ps, 1)

            pe.wait_ge(const_landed, 16 * 8)
            transpose_u(0)
            pe.wait_ge(ut_a, 1)
            pe.wait_ge(ut_v, 1)
            for k in range(KC):
                pe.wait_ge(w_in_sem[k], 16)
                for i in range(4):
                    product(0, i, k)
            for t in range(T):
                pe.wait_ge(ut_a, t + 1)
                pe.wait_ge(ut_v, t + 1)
                for i in range(len(colgroups[t])):
                    n = ngroups_before[t] + i
                    if n >= 4:
                        pe.wait_ge(proj_out, n - 3)
                        for k in range(KC):
                            product(t, i, k)
                    if i == 0 and t + 1 < T:
                        transpose_u(t + 1)
                    if i in turned_after[t]:
                        transpose_qk(t - 1, turned_after[t][i])
            transpose_qk(T - 1, range(len(tgroups[T - 1])))


C_ID, C_TRI, C_EXP, C_BASE, C_JOB, C_STEP, C_W = 0, 128, 256, 288, 320, 384, 388


class RouteWeights:
    LOADS = 8

    def __init__(self, nc, ctx):
        sb = lambda n, s, d=F32: ctx.enter_context(nc.sbuf_tensor(n, s, d))
        self.nc = nc
        self.w_sb = sb("w_out_sb", [P, KC, D])
        self.wr = sb("w_router_sb", [P, KC, N_EXP])
        self.br = sb("b_router_sb", [P, N_EXP])
        self.gd = sb("g_head_sb", [P, DV])
        self.gf = sb("g_ffn_sb", [P, D])
        self.cst = sb("cst", [P, C_W])
        self.ones = sb("ones", [P, P])
        self.landed = ctx.enter_context(nc.semaphore("route_landed"))

    def load(self, sp, a):
        landed = self.landed
        sp.dma_start(self.cst[:, :], a["consts"][:, :]).then_inc(landed, 16)
        sp.dma_start(self.gd[:, :], a["g_diff_head"][0, :].partition_broadcast(P)).then_inc(landed, 16)
        for c in range(2):
            sp.dma_start(self.w_sb[:, 4 * c:4 * c + 4, :],
                         a["w_out"][0, 512 * c:512 * c + 512, :].rearrange("(k p) n -> p k n", p=P)).then_inc(landed, 16)
        sp.dma_start(self.gf[:, :], a["g_ffn"][0, :].partition_broadcast(P)).then_inc(landed, 16)
        sp.dma_start(self.br[:, :], a["b_router"][0, :].partition_broadcast(P)).then_inc(landed, 16)
        with self.nc.allow_non_contiguous_dma("128 byte rows, once"):
            sp.dma_start(self.wr[:, :, :], a["w_router"][0].rearrange("(k p) n -> p k n", p=P)).then_inc(landed, 16)
        sp.dma_start(self.ones[:, :], a["ones"][:, :]).then_inc(landed, 16)


class DiffStacks:
    def __init__(self, nc, ctx):
        sb = lambda n, s, d=F32: ctx.enter_context(nc.sbuf_tensor(n, s, d))
        sem = lambda n: ctx.enter_context(nc.semaphore(n))
        self.q_st = sb("q_st", [P, 2, 2, SEQ], F32R)
        self.k_st = sb("k_st", [P, 2, 2, KEYS], F32R)
        self.ident = sb("ident2", [P, P])
        self.lam = sb("lam", [P, 4, DQ])
        self.const_landed = sem("const_landed2")
        self.st_sem = [sem(f"stack_landed{i}") for i in range(2)]

    def load_small(self, sp, a):
        sp.dma_start(self.ident[:, :], a["consts"][:, 0:P]).then_inc(self.const_landed, 16)
        for i, n in enumerate(("lambda_q1", "lambda_k1", "lambda_q2", "lambda_k2")):
            sp.dma_start(self.lam[:, i, :], a[n][0, :].partition_broadcast(P)).then_inc(self.const_landed, 16)

    def load_head(self, sp, qk_dram, h):
        for j in range(4):
            rows = slice(32 * j, 32 * j + 32)
            for buf, at, part, n in ((self.q_st, R_QD, j % 2, SEQ), (self.k_st, R_KD, j // 2, KEYS)):
                src = qk_dram[part, at + h * 64:at + h * 64 + 64, 0:n].rearrange("(s d) n -> d s n", s=2)
                sp.dma_start(buf[rows, h % 2, :, 0:n].bitcast(F32), src).then_inc(self.st_sem[h % 2], 16)


def attend_diff(nc, a, v_all, mixed, qk_dram, stacks, weights):
    with ExitStack() as ctx:
        sb = lambda n, s, d=F32: ctx.enter_context(nc.sbuf_tensor(n, s, d))
        sem = lambda n: ctx.enter_context(nc.semaphore(n))
        ps = lambda n, s: ctx.enter_context(nc.psum_tensor(n, s, F32))
        q_st, k_st, ident, lam = stacks.q_st, stacks.k_st, stacks.ident, stacks.lam
        const_landed, st_sem = stacks.const_landed, stacks.st_sem
        e = sb("e", [P, 2, 2, KEYS])
        dsb = sb("dsb", [P, 2, KEYS])
        pt = sb("pt", [P, 2, 9, 512])
        ot = sb("ot", [DV, 512])
        lw = sb("lw", [P, 8])
        meta_s = sb("meta_s", [P, 2, 2 * NT, N_META])
        meta_nm = sb("meta_nm", [P, 2, 2 * NT])
        seq_nm = sb("seq_nm", [P, 4])
        nm = sb("nm", [P, 4])
        ls = sb("ls", [P, 2, 2, 2])
        total = sb("total", [P, 16, 2])
        inverse = sb("inverse", [P, 16, 2])
        ratio = sb("ratio", [P, 2])
        s_ps = [ps("s_ps0", [P, 2, 512]), ps("s_ps1", [P, 2, 512])]
        t_ps = ps("t_ps", [P, 2, 512])
        x_ps = ps("x_ps", [P, 512])
        o_ps = ps("o_ps", [P, 512])
        S = lambda i: s_ps[i][:, :, :].rearrange("p b n -> p (b n)")

        lam_dots, lam_exp, lam_done = sem("lam_dots"), sem("lam_exp"), sem("lam_done")
        scores_ready, max_ready, exp_done = sem("scores_ready"), sem("max_ready"), sem("exp_done")
        nm_ready, s_used = sem("nm_ready"), sem("scores_used")
        inverted = sem("inverted")
        total_done, ratio_done, combined = sem("total_done"), sem("ratio_done"), sem("combined")
        t_ready, t_copied = sem("p_transposed"), sem("pt_copied")
        x_ready, x_copied, meta_max = sem("x_ready"), sem("x_copied"), sem("meta_max")
        o_ready, ot_done = sem("o_ready"), sem("ot_copied")
        dve_chain = sem("dve_chain2")

        U = HD * NT
        NG = U // 4
        STEPS = U + 8
        block = ctx.enter_context(nc.Block())

        copied_in = lambda n: (n - 9) // 4 if n >= 9 and (n - 9) % 4 == 0 and (n - 9) // 4 < NG else None
        back_in = lambda n: copied_in(n - 1)
        order = [("scores", 0)]
        for n in range(STEPS):
            if 2 <= n <= U + 1:
                order.append(("meta", n - 2))
            if back_in(n) is not None:
                order.append(("back", back_in(n)))
            if n % NT == NT - 1 and n + 1 < U:
                order.append(("scores", (n + 1) // NT))
        use_of = {what: k for k, what in enumerate(order)}

        @block.sync
        def _(sp):
            weights.load(sp, a)
            for h in range(2, HD):
                sp.wait_ge(scores_ready, 2 * NT * (h - 1))
                stacks.load_head(sp, qk_dram, h)

        @block.scalar
        def _(act):
            def copy_part(u, g):
                act.wait_ge(t_ready, 2 * u + g + 1)
                if g == 0 and u % 4 == 0 and u >= 8:
                    act.wait_ge(o_ready, u // 4 - 1)
                act.copy(pt[:, (u // 4) % 2, 4 * g:4 * g + 4, (u % 4) * P:(u % 4 + 1) * P],
                         t_ps[:, g, :].rearrange("p (c n) -> p c n", n=P)).then_inc(t_copied, 1)

            act.wait_ge(lam_dots, 2)
            act.activation(lw[:, 2:4], lw[:, 0:2], ACT.Exp).then_inc(lam_exp, 1)
            for n in range(STEPS):
                for i in range(2):
                    if n < U:
                        act.wait_ge(nm_ready, 2 * n + i + 1)
                        if n >= 2 and i == 0:
                            act.wait_ge(combined, n - 1)
                            act.wait_ge(total_done, n - 1)
                        k = (2 * n + i) % 4
                        act.activation(e[:, n % 2, i, 0:SEQ], S(i), ACT.Exp, bias=nm[:, k:k + 1],
                                       accum_out=ls[:, n % 2, 0, i:i + 1]).then_inc(s_used, 1)
                        act.activation(e[:, n % 2, i, SEQ:KEYS], meta_s[:, (n // NT) % 2, 2 * (n % NT) + i, :], ACT.Exp,
                                       bias=nm[:, k:k + 1], accum_out=ls[:, n % 2, 1, i:i + 1]).then_inc(exp_done, 1)
                    if i == 0 and 2 <= n <= U + 1:
                        copy_part(n - 2, 0)
                        copy_part(n - 2, 1)
                g = copied_in(n)
                if g is not None:
                    act.wait_ge(o_ready, g + 1)
                    if g >= 1:
                        act.wait_ge(x_ready, use_of[("back", g - 1)] + 1)
                    act.copy(ot[:, :], o_ps[0:DV, :]).then_inc(ot_done, 1)

        @block.vector
        def _(dve):
            step = chained(dve, dve_chain)
            dve.wait_ge(const_landed, 16 * 5)
            for i in range(2):
                dve.tensor_tensor_reduce(lam[:, 2 * i, :], lam[:, 2 * i, :], lam[:, 2 * i + 1, :], 1.0, 0.0,
                                         ALU.mult, ALU.add, lw[:, i:i + 1]).then_inc(lam_dots, 1)
            dve.wait_ge(lam_exp, 1)
            step(dve.tensor_tensor(lw[:, 4:5], lw[:, 3:4], lw[:, 2:3], ALU.subtract))
            dve.tensor_scalar(lw[:, 5:6], lw[:, 4:5], -LAMBDA_INIT, None, ALU.add).then_inc(lam_done, 1)
            dve.wait_ge(lam_done, 1)

            def meta_scores(h):
                dve.wait_ge(x_ready, use_of[("scores", h)] + 1)
                if h >= 2:
                    dve.wait_ge(exp_done, 2 * NT * (h - 1))
                x = x_ps[:, 0:2 * NT * N_META].rearrange("p (u m) -> p u m", m=N_META)
                dve.tensor_reduce(meta_nm[:, h % 2, :], x, AX.X, ALU.max, negate=True).then_inc(meta_max, 1)
                dve.tensor_copy(meta_s[:, h % 2, :, :], x).then_inc(x_copied, 1)

            def maximum(n, i):
                k = (2 * n + i) % 4
                dve.wait_ge(scores_ready, 2 * n + i + 1)
                if n >= 2:
                    dve.wait_ge(nm_ready, 2 * n + i - 3)
                dve.tensor_reduce(seq_nm[:, k:k + 1], S(i), AX.X, ALU.max, negate=True).then_inc(max_ready, 1)
                if n % NT == 0 and i == 0:
                    dve.wait_ge(meta_max, n // NT + 1)
                if n >= 2:
                    dve.wait_ge(exp_done, 2 * n + i - 3)
                dve.wait_ge(max_ready, 2 * n + i + 1)
                at = 2 * (n % NT) + i
                dve.tensor_tensor(nm[:, k:k + 1], seq_nm[:, k:k + 1], meta_nm[:, (n // NT) % 2, at:at + 1],
                                  ALU.min).then_inc(nm_ready, 1)

            def invert(u):
                dve.wait_ge(total_done, u + 1)
                dve.reciprocal(inverse[:, u % 16, :], total[:, u % 16, :]).then_inc(inverted, 1)

            def combine_halves(u):
                b = u % 2
                dve.wait_ge(s_used, 2 * u + 2)
                dve.wait_ge(exp_done, 2 * u + 2)
                if u >= 2:
                    dve.wait_ge(t_ready, 2 * u - 2)
                    dve.wait_ge(x_ready, use_of[("meta", u - 2)] + 1)
                dve.wait_ge(ratio_done, u + 1)
                dve.scalar_tensor_tensor(out=dsb[:, b, :], in0=e[:, b, 1, :], scalar=ratio[:, b:b + 1],
                                         in1=e[:, b, 0, :], op0=ALU.mult, op1=ALU.add).then_inc(combined, 1)

            def copy_meta(u):
                dve.wait_ge(x_ready, use_of[("meta", u)] + 1)
                if u % 4 == 0 and u >= 8:
                    dve.wait_ge(o_ready, u // 4 - 1)
                dve.tensor_copy(pt[0:N_META, (u // 4) % 2, 8, (u % 4) * P:(u % 4 + 1) * P],
                                x_ps[0:N_META, 0:P]).then_inc(x_copied, 1)

            def store_out(g):
                h, t0 = g // 2, 4 * (g % 2)
                dve.wait_ge(x_ready, use_of[("back", g)] + 1)
                dve.wait_ge(inverted, 4 * g + 4)
                for j in range(4):
                    ins = dve.tensor_scalar(mixed[:, t0 + j, 512 + h * DV:512 + (h + 1) * DV],
                                            x_ps[:, j * DV:(j + 1) * DV], inverse[:, (4 * g + j) % 16, 0:1],
                                            None, ALU.mult)
                ins.then_inc(x_copied, 1)

            meta_scores(0)
            for n in range(STEPS):
                if n < U:
                    maximum(n, 0)
                if 1 <= n <= U:
                    invert(n - 1)
                if 2 <= n <= U + 1:
                    copy_meta(n - 2)
                if n < U:
                    maximum(n, 1)
                if 1 <= n <= U:
                    combine_halves(n - 1)
                if back_in(n) is not None:
                    store_out(back_in(n))
                if n % NT == NT - 1 and n + 1 < U:
                    meta_scores((n + 1) // NT)

        @block.gpsimd
        def _(pool):
            pool.wait_ge(lam_done, 1)
            for u in range(U):
                pool.wait_ge(s_used, 2 * u + 2)
                pool.wait_ge(exp_done, 2 * u + 2)
                if u >= 16:
                    pool.wait_ge(x_copied, use_of[("back", u // 4 - 4)] + 1)
                pool.tensor_tensor(total[:, u % 16, :], ls[:, u % 2, 0, :], ls[:, u % 2, 1, :], ALU.add).then_inc(total_done, 1)
                if u >= 2:
                    pool.wait_ge(combined, u - 1)
                pool.wait_ge(inverted, u + 1)
                pool.tensor_scalar(ratio[:, u % 2:u % 2 + 1], total[:, u % 16, 0:1], inverse[:, u % 16, 1:2], lw[:, 5:6],
                                   ALU.mult, ALU.mult).then_inc(ratio_done, 1)

        @block.tensor
        def _(pe):
            def scores(n, i):
                h, t = n // NT, n % NT
                if n >= 1:
                    pe.wait_ge(s_used, 2 * n + i - 1)
                for c in range(2):
                    ins = pe.matmul(s_ps[i][:, c, :], q_st[:, h % 2, i, t * P:(t + 1) * P],
                                    k_st[:, h % 2, i, c * 512:(c + 1) * 512], start=True, stop=True)
                ins.then_inc(scores_ready, 1)

            def free_x(what):
                if use_of[what] >= 1:
                    pe.wait_ge(x_copied, use_of[what])

            def meta_scores(h):
                pe.wait_ge(st_sem[h % 2], 16 * 8 * (h // 2 + 1))
                free_x(("scores", h))
                for t in range(NT):
                    for i in range(2):
                        k = 2 * t + i
                        ins = pe.matmul(x_ps[:, k * N_META:(k + 1) * N_META], q_st[:, h % 2, i, t * P:(t + 1) * P],
                                        k_st[:, h % 2, i, SEQ:KEYS], start=True, stop=True)
                ins.then_inc(x_ready, 1)

            def transpose_part(u, g):
                if u >= 1:
                    pe.wait_ge(t_copied, 2 * u + g - 1)
                for c in range(4 * g, 4 * g + 4):
                    ins = pe.transpose(t_ps[:, g, (c % 4) * P:(c % 4 + 1) * P], dsb[:, u % 2, c * P:(c + 1) * P], ident[:, :])
                ins.then_inc(t_ready, 1)

            def transpose_meta(u):
                free_x(("meta", u))
                pe.transpose(x_ps[0:N_META, 0:P], dsb[:, u % 2, SEQ:KEYS], ident[:, :]).then_inc(x_ready, 1)

            def values(m0, m1):
                for m in range(m0, m1):
                    g, c = divmod(m, 9)
                    h = g // 2
                    r = P if c < 8 else N_META
                    if c == 0:
                        pe.wait_ge(t_copied, 2 * (4 * g + 4))
                        pe.wait_ge(x_copied, use_of[("meta", 4 * g + 3)] + 1)
                        if g >= 1:
                            pe.wait_ge(ot_done, g)
                    vt = v_all[0:r, c, 128 + h * DV:128 + (h + 1) * DV]
                    ins = pe.matmul(o_ps[0:DV, :], vt, pt[0:r, g % 2, c, :], start=(c == 0), stop=(c == 8))
                    if c == 8:
                        ins.then_inc(o_ready, 1)

            pe.wait_ge(const_landed, 16 * 5)
            meta_scores(0)
            for n in range(STEPS):
                weighing = 6 <= n < U + 6
                m = 9 * ((n - 6) // 4) + 2 * ((n - 6) % 4)
                if n < U:
                    scores(n, 0)
                if weighing and (n - 6) % 4 == 3:
                    values(m, m + 1)
                    m += 1
                if 2 <= n <= U + 1:
                    pe.wait_ge(combined, n - 1)
                    transpose_part(n - 2, 0)
                    transpose_part(n - 2, 1)
                    transpose_meta(n - 2)
                if n < U:
                    scores(n, 1)
                if weighing:
                    values(m, m + 2)
                g = back_in(n)
                if g is not None:
                    pe.wait_ge(ot_done, g + 1)
                    free_x(("back", g))
                    for j in range(4):
                        ins = pe.transpose(x_ps[:, j * DV:(j + 1) * DV], ot[:, j * P:(j + 1) * P], ident[0:DV, 0:DV])
                    ins.then_inc(x_ready, 1)
                if n % NT == NT - 1 and n + 1 < U:
                    meta_scores((n + 1) // NT)


def attend_window(nc, a, v_all, mixed, qk_dram, stacks):
    with ExitStack() as ctx:
        sb = lambda n, s, d=F32: ctx.enter_context(nc.sbuf_tensor(n, s, d))
        sem = lambda n: ctx.enter_context(nc.semaphore(n))
        ps = lambda n, s: ctx.enter_context(nc.psum_tensor(n, s, F32))
        BW = 3 * P + N_META
        q_st = sb("qa_st", [P, HQ, SEQ], F32R)
        k_st = sb("ka_st", [P, 2, HKV, KEYS], F32R)
        masks = sb("masks", [P, 3, BW])
        sink = sb("sink", [P, HQ])
        sm = sb("sm", [P, 2, G, BW])
        pt = sb("pta", [P, 2, 4, 512])
        ot = sb("ota", [DV, 2, 512])
        ident = sb("ident3", [P, P])
        mx = sb("mx", [P, 2, G])
        nm = sb("nma", [P, 2, G])
        ls = sb("lsa", [P, 2, G])
        xs = sb("xsink", [P, 2, G])
        rl = sb("rla", [P, 4, G])
        s_ps = ps("sa_ps", [P, 4, 512])
        t_ps = ps("ta_ps", [P, 2, 512])
        o_ps = ps("oa_ps", [P, 512])
        ob_ps = ps("ob_ps", [P, 512])

        landed = sem("window_landed")
        pieces = [((0, 2 * P), [(0, 3 * P), (SEQ, KEYS)]), ((2 * P, 4 * P), [(3 * P, 5 * P)]),
                  ((4 * P, NT * P), [(5 * P, NT * P)])]
        piece_landed = [sem(f"window_piece{i}") for i in range(3)]
        s_ready, masked, mx_done, nm_done, exp_done = (sem("sa_ready"), sem("masked"), sem("maxa"), sem("nm_done"),
                                                       sem("expa_done"))
        sink_in, sink_exp, rl_done = sem("sink_in"), sem("sink_exp"), sem("rl_done")
        t_ready, t_copied = sem("ta_ready"), sem("ta_copied")
        o_ready, ot_done, ob_ready, ob_done = sem("oa_ready"), sem("ota_done"), sem("ob_ready"), sem("ob_done")
        dve_chain = sem("dve_chain3")
        U = NT * HKV
        bands = [[t + d for d in (-1, 0, 1) if 0 <= t + d < NT] for t in range(NT)]
        which = [0 if t == 0 else 2 if t == NT - 1 else 1 for t in range(NT)]
        nchunk = [len(bands[u // HKV]) + 1 for u in range(U)]
        before = [sum(nchunk[:u]) for u in range(U + 1)]
        width = lambda u: P * (nchunk[u] - 1) + N_META
        block = ctx.enter_context(nc.Block())

        @block.sync
        def _(sp):
            def load_piece(i):
                (q0, q1), cols = pieces[i]
                for part in range(2):
                    rows = slice(64 * part, 64 * part + 64)
                    src = qk_dram[part, 0:HQ * DH, q0:q1].rearrange("(h d) n -> d h n", d=DH)
                    sp.dma_start(q_st[rows, :, q0:q1].bitcast(F32), src).then_inc(piece_landed[i], 16)
                    for twice in range(2):
                        for k0, k1 in cols:
                            src = qk_dram[part, R_KA:R_KA + HKV * DH, k0:k1].rearrange("(h d) n -> d h n", d=DH)
                            dst = k_st[64 * twice:64 * twice + 64, part, :, k0:k1]
                            with nc.allow_non_contiguous_dma("64 byte rows of the meta keys, once"):
                                sp.dma_start(dst.bitcast(F32), src).then_inc(piece_landed[i], 16)

            load_piece(0)
            sp.dma_start(masks[:, :, :], a["masks"][:, :, :]).then_inc(landed, 16)
            sp.dma_start(sink[:, :], a["sink_swa"][0, :].partition_broadcast(P)).then_inc(landed, 16)
            sp.dma_start(ident[:, :], a["consts"][:, 0:P]).then_inc(landed, 16)
            load_piece(1)
            load_piece(2)
            stacks.load_small(sp, a)
            for h in range(2):
                stacks.load_head(sp, qk_dram, h)

        @block.tensor
        def _(pe):
            pe.wait_ge(landed, 16 * 3)

            def scores(u):
                t, g = u // HKV, u % HKV
                for i, ((q0, q1), cols) in enumerate(pieces):
                    if g == 0 and t * P == q0:
                        pe.wait_ge(piece_landed[i], 16 * (2 + 4 * len(cols)))
                k0, nb = bands[t][0] * P, (nchunk[u] - 1) * P
                for j in range(G):
                    if u >= 1:
                        pe.wait_ge(masked, G * (u - 1) + j + 1)
                    q = q_st[:, g * G + j, t * P:(t + 1) * P]
                    for part in range(2):
                        pe.matmul(s_ps[:, j, 0:nb], q, k_st[:, part, g, k0:k0 + nb], start=(part == 0), stop=(part == 1))
                    for part in range(2):
                        ins = pe.matmul(s_ps[:, j, nb:nb + N_META], q, k_st[:, part, g, SEQ:KEYS],
                                        start=(part == 0), stop=(part == 1))
                    ins.then_inc(s_ready, 1)

            def weigh(u, chunks):
                t, g = u // HKV, u % HKV
                pe.wait_ge(exp_done, G * (u + 1))
                for c in chunks:
                    n = before[u] + c
                    w = P if c < nchunk[u] - 1 else N_META
                    if n >= 2:
                        pe.wait_ge(t_copied, n - 1)
                    for j in range(G):
                        ins = pe.transpose(t_ps[0:w, n % 2, j * P:(j + 1) * P], sm[:, u % 2, j, c * P:c * P + w], ident[:, :])
                    ins.then_inc(t_ready, 1)

            def values(u):
                t, g = u // HKV, u % HKV
                for c in range(nchunk[u]):
                    w = P if c < nchunk[u] - 1 else N_META
                    tile = bands[t][c] if w == P else NT
                    pe.wait_ge(t_copied, before[u] + c + 1)
                    if c == 0 and u >= 1:
                        pe.wait_ge(ot_done, u)
                    ins = pe.matmul(o_ps[0:DV, :], v_all[0:w, tile, g * DH:(g + 1) * DH], pt[0:w, u % 2, c, :],
                                    start=(c == 0), stop=(c == nchunk[u] - 1))
                ins.then_inc(o_ready, 1)

            def back(u):
                pe.wait_ge(ot_done, u + 1)
                if u >= 1:
                    pe.wait_ge(ob_done, u)
                for j in range(G):
                    ins = pe.transpose(ob_ps[:, j * DV:(j + 1) * DV], ot[:, u % 2, j * P:(j + 1) * P], ident[0:DV, 0:DV])
                ins.then_inc(ob_ready, 1)

            for n in range(U + 3):
                if n < U:
                    scores(n)
                if 1 <= n <= U:
                    weigh(n - 1, (0, 1))
                if 2 <= n <= U + 1:
                    values(n - 2)
                if 1 <= n <= U:
                    weigh(n - 1, range(2, nchunk[n - 1]))
                if n >= 3:
                    back(n - 3)

        def copy_chunk(op, eng, u, c):
            n = before[u] + c
            w = P if c < nchunk[u] - 1 else N_META
            eng.wait_ge(t_ready, n + 1)
            if n >= 1:
                eng.wait_ge(t_copied, n)
            if u >= 2 and c < 2:
                eng.wait_ge(o_ready, u - 1)
            op(pt[0:w, u % 2, c, :], t_ps[0:w, n % 2, :]).then_inc(t_copied, 1)

        @block.vector
        def _(dve):
            step = chained(dve, dve_chain)
            dve.wait_ge(landed, 16 * 3)
            for n in range(U + 3):
                if n < U:
                    t, g, b, w = n // HKV, n % HKV, n % 2, width(n)
                    if n >= 2:
                        dve.wait_ge(t_ready, before[n - 1])
                    for j in range(G):
                        dve.wait_ge(s_ready, G * n + j + 1)
                        dve.tensor_tensor_reduce(sm[:, b, j, 0:w], s_ps[:, j, 0:w], masks[:, which[t], 0:w], 1.0, NEG,
                                                 ALU.add, ALU.max, mx[:, b, j:j + 1]).then_inc(masked, 1)
                    dve.wait_ge(masked, G * (n + 1))
                    step(dve.tensor_tensor(mx[:, b, :], mx[:, b, :], sink[:, g * G:(g + 1) * G], ALU.max))
                    dve.tensor_scalar(nm[:, b, :], mx[:, b, :], -1.0, None, ALU.mult).then_inc(nm_done, 1)
                    dve.tensor_tensor(xs[:, b, :], sink[:, g * G:(g + 1) * G], mx[:, b, :], ALU.subtract).then_inc(sink_in, 1)
                if 1 <= n <= U:
                    u = n - 1
                    dve.wait_ge(sink_exp, u + 1)
                    dve.wait_ge(exp_done, G * (u + 1))
                    step(dve.tensor_tensor(ls[:, u % 2, :], ls[:, u % 2, :], xs[:, u % 2, :], ALU.add))
                    dve.reciprocal(rl[:, u % 4, :], ls[:, u % 2, :]).then_inc(rl_done, 1)
                    for c in range(2, nchunk[u]):
                        copy_chunk(dve.tensor_copy, dve, u, c)
                if n >= 3:
                    u = n - 3
                    t, g = u // HKV, u % HKV
                    dve.wait_ge(ob_ready, u + 1)
                    dve.wait_ge(rl_done, u + 1)
                    for j in range(G):
                        hcol = (g * G + j) * DH
                        ins = dve.tensor_scalar(mixed[:, t, hcol:hcol + DH], ob_ps[:, j * DV:(j + 1) * DV],
                                                rl[:, u % 4, j:j + 1], None, ALU.mult)
                    ins.then_inc(ob_done, 1)

        @block.scalar
        def _(act):
            for n in range(U + 2):
                if 1 <= n <= U:
                    for c in range(2):
                        copy_chunk(act.copy, act, n - 1, c)
                if n < U:
                    b, w = n % 2, width(n)
                    act.wait_ge(nm_done, n + 1)
                    if n >= 2:
                        act.wait_ge(rl_done, n - 1)
                    for j in range(G):
                        act.activation(sm[:, b, j, 0:w], sm[:, b, j, 0:w], ACT.Exp, bias=nm[:, b, j:j + 1],
                                       accum_out=ls[:, b, j:j + 1]).then_inc(exp_done, 1)
                    act.wait_ge(sink_in, n + 1)
                    act.activation(xs[:, b, :], xs[:, b, :], ACT.Exp).then_inc(sink_exp, 1)
                if n >= 2:
                    u = n - 2
                    act.wait_ge(o_ready, u + 1)
                    if u >= 2:
                        act.wait_ge(ob_ready, u - 1)
                    act.copy(ot[:, u % 2, :], o_ps[0:DV, :]).then_inc(ot_done, 1)


def route(nc, a, mixed, gates, jobs, h2_dram, v_dram, slot_dram, weights):
    with ExitStack() as ctx:
        sb = lambda n, s, d=F32: ctx.enter_context(nc.sbuf_tensor(n, s, d))
        sem = lambda n: ctx.enter_context(nc.semaphore(n))
        ps = lambda n, s: ctx.enter_context(nc.psum_tensor(n, s, F32))
        w_sb, wr, br, gd, gf = weights.w_sb, weights.wr, weights.br, weights.gd, weights.gf
        cst, ones, landed = weights.cst, weights.ones, weights.landed
        xs = sb("xs4", [P, 2, D])
        hsq = sb("hsq", [P, HD * DV])
        hs = sb("hs4", [P, HD])
        hr = sb("hr4", [P, HD])
        mt = sb("mt", [P, 2, KC, P])
        h2 = sb("h2", [P, 2, D])
        vs = sb("vs", [P, 2, D])
        vt = sb("vt", [P, KC, P])
        ss = sb("ss4", [P, NT])
        rs = sb("rs4", [P, NT])
        eps = sb("eps4", [P, 2])
        lg = sb("lg", [P, N_EXP])
        top = sb("top", [P, NT, 8])
        idx = sb("idx", [P, 8], U32)
        idf = sb("idf", [P, 8])
        oh = sb("oh", [P, TOP_K, N_EXP])
        sel = sb("sel", [P, N_EXP])
        acc = sb("acc", [P, N_EXP])
        pos = sb("pos", [P, N_EXP])
        junk = sb("junk", [P, N_EXP])
        dst = sb("dst", [P, NT, TOP_K])
        dsti = sb("dsti", [P, NT, TOP_K], U32)
        code = sb("code", [P, NT, TOP_K, 2], U32)
        none = sb("none", [P, N_EXP * CAP * 2 // P], U32)
        gsum = sb("gsum", [P, NT])
        ec = sb("ec", [N_EXP, 8])
        ej = sb("ej", [N_EXP, 3, NJ])
        jf = sb("jf", [1, 6, NJ])
        tm_ps, tv_ps = ps("tm_ps", [P, 2, 512]), ps("tv_ps", [P, 512])
        o_ps, r_ps = ps("o4_ps", [P, 4, 512]), ps("r_ps", [P, 512])

        x_sem = [sem(f"x4_landed{i}") for i in range(2)]
        h2_sem = [sem(f"h2_stored{i}") for i in range(2)]
        v_sem = [sem(f"v_stored{i}") for i in range(2)]
        cleared, scattered = sem("slots_cleared"), sem("slots_written")
        ready, ones_set, codes_set = sem("consts4_set"), sem("ones_set"), sem("codes_set")
        hs_done, hstd_done, head_done = sem("hs4_done"), sem("hstd4_done"), sem("head_done")
        tm_ready, mt_a, mt_v = sem("tm_ready"), sem("mt_act"), sem("mt_dve")
        o_ready, h2_done = sem("o4_ready"), sem("h2_done")
        ss_done, std_done, v_done = sem("ss4_done"), sem("std4_done"), sem("v_done")
        tv_ready, vt_done = sem("tv_ready"), sem("vt_done")
        r_ready, lg_done, sel_done, rank_ready, dst_done = (sem("r_ready"), sem("lg_done"), sem("sel_done"),
                                                            sem("rank_ready"), sem("dst_done"))
        gates_in, gates_exp = sem("gates_in"), sem("gates_exp")
        cnt_ready, jobs_step, jobs_in = sem("cnt_ready"), sem("jobs_step"), sem("jobs_in")
        dve_chain = sem("dve_chain4")
        block = ctx.enter_context(nc.Block())
        NL = RouteWeights.LOADS

        @block.sync
        def _(sp):
            def load_x(t):
                if t >= 2:
                    sp.wait_ge(h2_done, 2 * (t - 1))
                sp.dma_start(xs[:, t % 2, :], a["x"][0, t * P:(t + 1) * P, :]).then_inc(x_sem[t % 2], 16)
            load_x(0)
            load_x(1)
            for t in range(NT):
                sp.wait_ge(h2_done, 2 * (t + 1))
                sp.dma_start(h2_dram[t * P:(t + 1) * P, :], h2[:, t % 2, :]).then_inc(h2_sem[t % 2], 16)
                if t + 2 < NT:
                    load_x(t + 2)
                sp.wait_ge(v_done, t + 1)
                sp.dma_start(v_dram[t * P:(t + 1) * P, :], vs[:, t % 2, :]).then_inc(v_sem[t % 2], 16)
            for i in range(2):
                sp.wait_ge(h2_sem[i], 16 * (NT // 2))
                sp.wait_ge(v_sem[i], 16 * (NT // 2))

        @block.gpsimd
        def _(pool):
            pool.memset(none[:, :], SEQ * TOP_K).then_inc(ready, 1)
            pool.iota(code[:, :, :, 0], pattern=[[P * TOP_K, NT], [1, TOP_K]], base=0, channel_multiplier=TOP_K
                      ).then_inc(codes_set, 1)
            pool.iota(code[:, :, :, 1], pattern=[[P, NT], [0, TOP_K]], base=0, channel_multiplier=1
                      ).then_inc(codes_set, 1)
            pool.wait_ge(ready, 1)
            pool.dma_start(slot_dram.rearrange("(p n) c -> p (n c)", p=P), none[:, :]).then_inc(cleared, 16)
            pool.wait_ge(cleared, 16)
            pool.wait_ge(codes_set, 2)
            for t in range(NT):
                pool.wait_ge(dst_done, t + 1)
                for k in range(TOP_K):
                    pool.indirect_dma_start(out=slot_dram[:, :],
                                            out_offset=bass.IndirectOffsetOnAxis(ap=dsti[:, t, k:k + 1], axis=0),
                                            in_=code[:, t, k, :], in_offset=None).then_inc(scattered, 16)
            pool.wait_ge(scattered, 16 * NT * TOP_K)

        @block.scalar
        def _(act):
            act.wait_ge(ones_set, 1)

            def head_std(t):
                act.wait_ge(hs_done, t + 1)
                act.activation(hr[:, :], hs[:, :], ACT.Sqrt, bias=eps[:, 1:2], scale=1.0 / DV).then_inc(hstd_done, 1)

            def copy_mt(t):
                act.wait_ge(tm_ready, 2 * t + 1)
                if t >= 2:
                    act.wait_ge(o_ready, 2 * (t - 1))
                act.copy(mt[:, t % 2, 0:4, :], tm_ps[:, 0, :].rearrange("p (c n) -> p c n", n=P)).then_inc(mt_a, 1)

            head_std(0)
            copy_mt(0)
            head_std(1)
            for t in range(NT + 1):
                if t + 1 < NT:
                    copy_mt(t + 1)
                if t >= 1:
                    u = t - 1
                    for b in range(2):
                        act.wait_ge(tv_ready, 2 * u + b + 1)
                        if b == 0 and u >= 1:
                            act.wait_ge(r_ready, u)
                        act.copy(vt[:, 4 * b:4 * b + 4, :], tv_ps[:, :].rearrange("p (c n) -> p c n", n=P)).then_inc(vt_done, 1)
                if t + 2 < NT:
                    head_std(t + 2)
                if t < NT:
                    act.wait_ge(h2_done, 2 * (t + 1))
                    if t >= 2:
                        act.wait_ge(tv_ready, 2 * (t - 1))
                        act.wait_ge(v_sem[t % 2], 16 * (t // 2))
                    act.activation(vs[:, t % 2, :], h2[:, t % 2, :], ACT.Square, accum_out=ss[:, t:t + 1]).then_inc(ss_done, 1)
                    act.wait_ge(ss_done, t + 1)
                    act.activation(rs[:, t:t + 1], ss[:, t:t + 1], ACT.Sqrt, bias=eps[:, 0:1], scale=1.0 / D).then_inc(std_done, 1)
            act.wait_ge(gates_in, 1)
            act.activation(gates[:, :, :], gates[:, :, :], ACT.Exp).then_inc(gates_exp, 1)

        @block.vector
        def _(dve):
            step = chained(dve, dve_chain)
            dve.memset(acc[:, :], 0.0)
            dve.memset(eps[:, 0:1], EPS)
            step(dve.memset(eps[:, 1:2], EPS_HEAD))
            dve.wait_ge(landed, 16 * NL)
            dve.tensor_scalar(gd[:, :], gd[:, :], 1.0 - LAMBDA_INIT, None, ALU.mult).then_inc(ones_set, 1)
            dve.wait_ge(ones_set, 1)

            def heads(t):
                m = mixed[:, t, 512:1024]
                v = m.rearrange("p (h d) -> p h d", d=DV)
                step(dve.tensor_tensor(hsq[:, :], m, m, ALU.mult))
                if t >= 1:
                    dve.wait_ge(head_done, t)
                dve.tensor_reduce(hs[:, :], hsq[:, :].rearrange("p (h d) -> p h d", d=DV), AX.X, ALU.add).then_inc(hs_done, 1)
                dve.wait_ge(hstd_done, t + 1)
                step(dve.reciprocal(hr[:, :], hr[:, :]))
                step(dve.tensor_tensor(v, v, hr[:, :].unsqueeze(2).broadcast_to((P, HD, DV)), ALU.mult))
                dve.tensor_tensor(v, v, gd[:, :].unsqueeze(1).broadcast_to((P, HD, DV)), ALU.mult).then_inc(head_done, 1)

            def copy_mt(t):
                dve.wait_ge(tm_ready, 2 * t + 2)
                if t >= 2:
                    dve.wait_ge(o_ready, 2 * (t - 1))
                dve.tensor_copy(mt[:, t % 2, 4:8, :], tm_ps[:, 1, :].rearrange("p (c n) -> p c n", n=P)).then_inc(mt_v, 1)

            def residual(t, b):
                dve.wait_ge(x_sem[t % 2], 16 * (t // 2 + 1))
                if t >= 2:
                    dve.wait_ge(v_done, t - 1)
                    dve.wait_ge(h2_sem[t % 2], 16 * (t // 2))
                dve.wait_ge(o_ready, 2 * t + b + 1)
                dve.tensor_tensor(h2[:, t % 2, 512 * b:512 * b + 512], o_ps[:, 2 * (t % 2) + b, :],
                                  xs[:, t % 2, 512 * b:512 * b + 512], ALU.add).then_inc(h2_done, 1)

            def normalise(t):
                dve.wait_ge(std_done, t + 1)
                step(dve.reciprocal(rs[:, t:t + 1], rs[:, t:t + 1]))
                dve.scalar_tensor_tensor(out=vs[:, t % 2, :], in0=h2[:, t % 2, :], scalar=rs[:, t:t + 1], in1=gf[:, :],
                                         op0=ALU.mult, op1=ALU.mult).then_inc(v_done, 1)

            def choose(u):
                dve.wait_ge(r_ready, u + 1)
                step(dve.tensor_tensor(lg[:, :], r_ps[:, 0:N_EXP], br[:, :], ALU.add))
                step(dve.max(top[:, u, :], lg[:, :]))
                step(dve.max_index(idx[:, :], top[:, u, :], lg[:, :]))
                step(dve.tensor_copy(idf[:, :], idx[:, :]))
                for k in range(TOP_K):
                    ins = dve.tensor_scalar(oh[:, k, :], cst[:, C_EXP:C_EXP + N_EXP], idf[:, k:k + 1], None, ALU.is_equal)
                step(ins)
                dve.tensor_reduce(sel[:, :], oh[:, :, :].rearrange("p k e -> p e k"), AX.X, ALU.add).then_inc(sel_done, 1)

            def place(u):
                dve.wait_ge(rank_ready, u + 1)
                step(dve.tensor_tensor(pos[:, :], r_ps[:, 32:64], cst[:, C_BASE:C_BASE + N_EXP], ALU.add))
                for k in range(TOP_K):
                    step(dve.tensor_tensor_reduce(junk[:, :], oh[:, k, :], pos[:, :], 1.0, 0.0, ALU.mult, ALU.add,
                                                  dst[:, u, k:k + 1]))
                step(dve.tensor_tensor(acc[:, :], acc[:, :], sel[:, :], ALU.add))
                dve.tensor_copy(dsti[:, u, :], dst[:, u, :]).then_inc(dst_done, 1)

            heads(0)
            copy_mt(0)
            heads(1)
            for t in range(NT + 2):
                if t < NT:
                    residual(t, 0)
                if t + 1 < NT:
                    copy_mt(t + 1)
                if t >= 2:
                    place(t - 2)
                if t + 2 < NT:
                    heads(t + 2)
                if t < NT:
                    residual(t, 1)
                    normalise(t)
                if 1 <= t <= NT:
                    choose(t - 1)
            dve.tensor_tensor(gates[:, :, :], top[:, :, 0:TOP_K], top[:, :, 0:1].broadcast_to((P, NT, TOP_K)),
                              ALU.subtract).then_inc(gates_in, 1)
            dve.wait_ge(gates_exp, 1)
            step(dve.tensor_reduce(gsum[:, :], gates[:, :, :], AX.X, ALU.add))
            step(dve.reciprocal(gsum[:, :], gsum[:, :]))
            step(dve.tensor_tensor(gates[:, :, :], gates[:, :, :], gsum[:, :].unsqueeze(2).broadcast_to((P, NT, TOP_K)), ALU.mult))
            step(dve.memset(ec[:, :], 1.0))
            dve.wait_ge(cnt_ready, 1)
            step(dve.tensor_copy(ec[:, 2:3], r_ps[0:N_EXP, 64:65]))
            step(dve.tensor_scalar(ej[:, 0, 0:4], cst[0:N_EXP, C_STEP:C_STEP + 4], ec[:, 2:3], None, ALU.is_lt))
            dve.tensor_reduce(ec[:, 1:2], ej[:, 0, 0:4], AX.X, ALU.add).then_inc(jobs_step, 1)
            dve.wait_ge(jobs_step, 1)
            dve.wait_ge(cnt_ready, 2)
            step(dve.tensor_copy(ec[:, 4:5], r_ps[0:N_EXP, 65:66]))
            step(dve.tensor_tensor(ec[:, 3:4], ec[:, 4:5], ec[:, 1:2], ALU.add))
            step(dve.tensor_scalar(ej[:, 0, :], cst[0:N_EXP, C_JOB:C_JOB + NJ], ec[:, 3:4], None, ALU.is_ge))
            step(dve.tensor_scalar(ej[:, 1, :], cst[0:N_EXP, C_JOB:C_JOB + NJ], ec[:, 4:5], None, ALU.is_ge))
            dve.tensor_tensor(ej[:, 2, :], ej[:, 1, :], ej[:, 0, :], ALU.subtract).then_inc(jobs_step, 1)
            dve.wait_ge(cnt_ready, 3)
            step(dve.tensor_copy(jf[0:1, 0:3, :], r_ps[0:1, 128:128 + 3 * NJ].rearrange("p (r n) -> p r n", n=NJ)))
            step(dve.tensor_tensor(jf[0:1, 3, :], cst[0:1, C_JOB:C_JOB + NJ], jf[0:1, 1, :], ALU.subtract))
            step(dve.scalar_tensor_tensor(out=jf[0:1, 4, :], in0=jf[0:1, 3, :], scalar=-float(JOB), in1=jf[0:1, 2, :],
                                          op0=ALU.mult, op1=ALU.add))
            step(dve.tensor_scalar(jf[0:1, 5, :], jf[0:1, 4, :], float(P), None, ALU.is_gt))
            step(dve.tensor_scalar(jf[0:1, 2, :], jf[0:1, 4, :], float(P + FEW), None, ALU.is_gt))
            step(dve.tensor_tensor(jf[0:1, 5, :], jf[0:1, 5, :], jf[0:1, 2, :], ALU.add))
            step(dve.tensor_scalar(jf[0:1, 0, :], jf[0:1, 0, :], float(N_EXP - 1), None, ALU.min))
            step(dve.tensor_scalar(jf[0:1, 3, :], jf[0:1, 3, :], 3.0, None, ALU.min))
            step(dve.tensor_scalar(jf[0:1, 3, :], jf[0:1, 3, :], float(JOB), None, ALU.mult))
            step(dve.scalar_tensor_tensor(out=jf[0:1, 4, :], in0=jf[0:1, 0, :], scalar=float(CAP), in1=jf[0:1, 3, :],
                                          op0=ALU.mult, op1=ALU.add))
            step(dve.tensor_copy(jobs[0:1, 0, :], jf[0:1, 0, :]))
            step(dve.tensor_copy(jobs[0:1, 1, :], jf[0:1, 4, :]))
            step(dve.tensor_copy(jobs[0:1, 2, :], jf[0:1, 5, :]))
            step(dve.tensor_copy(jobs[0:1, 3, 0:1], r_ps[0:1, 127:128]))

        @block.tensor
        def _(pe):
            ident = cst[:, C_ID:C_ID + P]
            pe.wait_ge(landed, 16 * NL)
            pe.wait_ge(ones_set, 1)

            def transpose_mixed(t):
                pe.wait_ge(head_done, t + 1)
                for b in range(2):
                    if t >= 1:
                        pe.wait_ge((mt_a, mt_v)[b], t)
                    for c in range(4):
                        k = 4 * b + c
                        ins = pe.transpose(tm_ps[:, b, c * P:(c + 1) * P], mixed[:, t, k * P:(k + 1) * P], ident)
                    ins.then_inc(tm_ready, 1)

            def project_out(t, b, k0, k1):
                if b == 0:
                    pe.wait_ge(mt_a, t + 1)
                    pe.wait_ge(mt_v, t + 1)
                    if t >= 2:
                        pe.wait_ge(h2_done, 2 * (t - 1))
                for k in range(k0, k1):
                    ins = pe.matmul(o_ps[:, 2 * (t % 2) + b, :], mt[:, t % 2, k, :], w_sb[:, k, 512 * b:512 * b + 512],
                                    start=(k == 0), stop=(k == KC - 1))
                if k1 == KC:
                    ins.then_inc(o_ready, 1)

            def transpose_v(t, b):
                pe.wait_ge(v_done, t + 1)
                if 2 * t + b >= 1:
                    pe.wait_ge(vt_done, 2 * t + b)
                for c in range(4):
                    k = 4 * b + c
                    ins = pe.transpose(tv_ps[:, c * P:(c + 1) * P], vs[:, t % 2, k * P:(k + 1) * P], ident)
                ins.then_inc(tv_ready, 1)

            def logits(t):
                pe.wait_ge(vt_done, 2 * t + 2)
                if t >= 1:
                    pe.wait_ge(dst_done, t)
                for k in range(KC):
                    ins = pe.matmul(r_ps[:, 0:N_EXP], vt[:, k, :], wr[:, k, :], start=(k == 0), stop=(k == KC - 1))
                ins.then_inc(r_ready, 1)

            def ranks(t):
                pe.wait_ge(sel_done, t + 1)
                pe.matmul(r_ps[:, 32:64], ones[:, :], acc[:, :], start=True, stop=False)
                pe.matmul(r_ps[:, 32:64], cst[:, C_TRI:C_TRI + P], sel[:, :], start=False, stop=True).then_inc(rank_ready, 1)

            transpose_mixed(0)
            for t in range(NT + 2):
                if t < NT:
                    project_out(t, 0, 0, KC)
                if t + 1 < NT:
                    transpose_mixed(t + 1)
                if t >= 2:
                    ranks(t - 2)
                if 1 <= t <= NT:
                    transpose_v(t - 1, 0)
                if t < NT:
                    project_out(t, 1, 0, KC // 2)
                if 1 <= t <= NT:
                    transpose_v(t - 1, 1)
                if t < NT:
                    project_out(t, 1, KC // 2, KC)
                if 1 <= t <= NT:
                    logits(t - 1)
            pe.wait_ge(dst_done, NT)
            pe.matmul(r_ps[0:N_EXP, 64:65], acc[:, :], ones[:, 0:1], start=True, stop=True).then_inc(cnt_ready, 1)
            pe.wait_ge(jobs_step, 1)
            pe.matmul(r_ps[0:1, 127:128], ec[:, 1:2], ones[0:N_EXP, 0:1], start=True, stop=True)
            pe.matmul(r_ps[0:N_EXP, 65:66], cst[0:N_EXP, C_TRI:C_TRI + N_EXP], ec[:, 1:2], start=True, stop=True
                      ).then_inc(cnt_ready, 1)
            pe.wait_ge(jobs_step, 2)
            pe.matmul(r_ps[0:1, 128:128 + NJ], ones[0:N_EXP, 0:1], ej[:, 0, :], start=True, stop=True)
            pe.matmul(r_ps[0:1, 128 + NJ:128 + 2 * NJ], ec[:, 1:2], ej[:, 0, :], start=True, stop=True)
            pe.matmul(r_ps[0:1, 128 + 2 * NJ:128 + 3 * NJ], ec[:, 2:3], ej[:, 2, :], start=True, stop=True).then_inc(cnt_ready, 1)


def experts(nc, a, jobs, v_dram, slot_dram, y_dram):
    with ExitStack() as ctx:
        sb = lambda n, s, d=F32: ctx.enter_context(nc.sbuf_tensor(n, s, d))
        sem = lambda n: ctx.enter_context(nc.semaphore(n))
        ps = lambda n, s: ctx.enter_context(nc.psum_tensor(n, s, F32))
        NC, NP = 6, 12
        RAW, SPL, AHEAD = 3, 4, 3
        PK = KC // 2
        raw = sb("raw", [P, RAW, KC, 512])
        whi = sb("whi", [P, SPL, PK, 512], F32R)
        wlo = sb("wlo", [P, SPL, PK, 512], F32R)
        xg = sb("xg", [P, 2, D])
        xt_hi = sb("xt_hi", [P, 2, KC, P], F32R)
        xt_lo = sb("xt_lo", [P, 2, KC, P], F32R)
        ht_hi = sb("ht_hi", [P, 2, KC, P], F32R)
        ht_lo = sb("ht_lo", [P, 2, KC, P], F32R)
        gl = sb("gl", [P, 512])
        sg = sb("sg", [P, 256])
        hh = sb("hh", [P, 2, 2, 256])
        ys = sb("ys", [P, 2, D])
        brow = sb("brow", [1, 3 * D])
        bias = sb("bias", [P, 3 * D])
        idn = sb("idn", [P, 2, 2], U32)
        idc = sb("idc", [P, 2], U32)
        ident = sb("ident5", [P, P])
        m_ps = ps("m_ps", [P, 4, 512])
        y_ps = ps("y_ps", [P, 2, 512])
        t_ps = ps("t5_ps", [P, 2, 512])

        w_sem = [sem(f"w_landed{i}") for i in range(RAW)]
        ident_landed, setup = sem("ident_landed"), sem("setup5")
        hi_done, lo_done, w_used, a_ready = sem("hi_split"), sem("lo_split"), sem("w_used"), sem("a_ready")
        m_read = [sem("m_read_a"), sem("m_read_b")]
        sig_done = [sem("sig_a"), sem("sig_b")]
        h_ready = [sem("h_ready_a"), sem("h_ready_b")]
        t_ready = [sem("t_ready_a"), sem("t_ready_b")]
        t_hi, t_lo = [sem("t_hi_a"), sem("t_hi_b")], [sem("t_lo_a"), sem("t_lo_b")]
        y_done = [sem("y_done_a"), sem("y_done_b")]
        y_stored = [sem("y_stored_a"), sem("y_stored_b")]
        x_landed = [sem("x_gathered_a"), sem("x_gathered_b")]
        idx_landed, idx_kept, brow_landed = sem("idx_landed"), sem("idx_kept"), sem("brow_landed")
        packed, summed = sem("few_packed"), sem("rows_summed")
        bias1, bias2, one_added = sem("bias1_spread"), sem("bias2_spread"), sem("one_added")
        dve_chain = sem("dve_chain5")
        passed = sem("wait_passed")
        block = ctx.enter_context(nc.Block())

        w1 = a["w_mlp1"][0].rearrange("e (k p) (s c n) -> e p k s c n", p=P, s=2, c=4)
        w2 = a["w_mlp2"][0].rearrange("e (c k p) n -> e c p k n", c=2, p=P)
        M_BANK = lambda c, half: 2 * (c % 2) + half
        L = bass.ds

        def piece(k):
            k %= NP
            chunk = raw[:, (k // 2) % RAW, :, :]
            if k < 8:
                return chunk[:, PK * (k % 2):PK * (k % 2) + PK, :]
            return chunk.rearrange("p k n -> p (k n)").rearrange("p (k q n) -> p k q n", k=PK, q=2)[:, :, k % 2, :]

        def job_value(eng, row, j, top):
            return eng.value_load(jobs[0:1, row, L(j, 1)], min_val=0, max_val=top)

        def job_count(eng):
            return eng.value_load(jobs[0:1, 3, 0:1], min_val=1, max_val=MAX_JOBS)

        @block.sync
        def _(sp):
            sp.dma_start(ident[:, :], a["consts"][:, C_ID:C_ID + P]).then_inc(ident_landed, 16)

            def load(c, e):
                s = c % RAW
                if c % NC < 4:
                    for part in range(2):
                        dst = raw[:, s, :, 256 * part:256 * part + 256]
                        sp.dma_start(dst, w1[L(e, 1), :, :, part, c % NC, :].rearrange("o p k n -> (o p) k n")
                                     ).then_inc(w_sem[s], 16)
                else:
                    for part in range(2):
                        sp.dma_start(raw[:, s, :, :].rearrange("p k n -> p (k n)").rearrange("p (k n) -> p k n", k=4)[:, 2 * part:2 * part + 2, :],
                                     w2[L(e, 1), c % NC - 4, :, 2 * part:2 * part + 2, :].rearrange("o p k n -> (o p) k n")
                                     ).then_inc(w_sem[s], 16)
            n = job_count(sp)
            e0 = job_value(sp, 0, 0, N_EXP - 1)
            for half in range(2):
                sp.wait_ge(x_landed[half], 16)
            load(0, e0)
            load(1, e0)
            with sp.Fori(0, n) as j:
                e = job_value(sp, 0, j, N_EXP - 1)
                nxt = job_value(sp, 0, j + 1, N_EXP - 1)
                for c in range(2, NC + 2):
                    sp.wait_ge(hi_done, j * NP + (2 * c + 2))
                    sp.wait_ge(lo_done, j * NP + (2 * c + 2))
                    load(c, e if c < NC else nxt)
            sp.wait_ge(w_sem[0], n * 64 + 32)
            sp.wait_ge(w_sem[1], n * 64 + 32)
            sp.wait_ge(w_sem[2], n * 64)
            sp.sem_inc(passed, 1)

        @block.gpsimd
        def _(pool):
            def load_idx(j):
                base = job_value(pool, 1, j, N_EXP * CAP - JOB)
                src = slot_dram[L(base, JOB), :].rearrange("(h p) c -> p h c", p=P)
                pool.dma_start(idn[:, :, :], src).then_inc(idx_landed, 16)

            def gather():
                for half in range(2):
                    pool.indirect_dma_start(out=xg[:, half, :], out_offset=None, in_=v_dram[:, :],
                                            in_offset=bass.IndirectOffsetOnAxis(ap=idn[:, half, 1:2], axis=0),
                                            bounds_check=SEQ - 1, oob_is_err=False).then_inc(x_landed[half], 16)

            def load_bias(e):
                for s in range(2):
                    pool.dma_start(brow[0:1, 0:2 * D].rearrange("p (c s n) -> p s c n", c=4, s=2)[:, s],
                                   a["b_mlp1"][0][L(e, 1), s * D:(s + 1) * D].rearrange("o (c n) -> o c n", c=4)
                                   ).then_inc(brow_landed, 16)
                pool.dma_start(brow[0:1, 2 * D:3 * D], a["b_mlp2"][0][L(e, 1), :]).then_inc(brow_landed, 16)

            def add_one(ahead):
                v = brow[0:1, 0:2 * D].rearrange("p (c s n) -> p s c n", c=4, s=2)[:, 1]
                pool.tensor_scalar(v, v, 1.0, None, ALU.add).then_inc(one_added, 1)
                pool.wait_ge(one_added, ahead)
                pool.sem_inc(passed, 1)

            load_idx(0)
            pool.memset(xg[:, :, :], 0.0).then_inc(setup, 1)
            pool.wait_ge(setup, 1)
            pool.wait_ge(idx_landed, 16)
            gather()
            pool.memset(ys[:, :, :], 0.0).then_inc(setup, 1)
            pool.wait_ge(setup, 2)
            load_bias(job_value(pool, 0, 0, N_EXP - 1))
            pool.tensor_copy(idc[:, :], idn[:, :, 0]).then_inc(idx_kept, 1)
            pool.wait_ge(brow_landed, 48)
            add_one(1)
            pool.partition_broadcast(bias[:, 0:2 * D], brow[0:1, 0:2 * D]).then_inc(bias1, 1)
            pool.partition_broadcast(bias[:, 2 * D:3 * D], brow[0:1, 2 * D:3 * D]).then_inc(bias2, 1)
            n = job_count(pool)
            with pool.Fori(0, n) as j:
                for half in range(2):
                    pool.wait_ge(x_landed[half], j * 16 + 16)
                pool.wait_ge(idx_kept, j + 1)
                pool.sem_inc(passed, 1)
                load_idx(j + 1)
                pool.wait_ge(idx_landed, j * 16 + 32)
                for half in range(2):
                    pool.wait_ge(t_ready[half], j * 6 + 2)
                pool.sem_inc(passed, 1)
                gather()
                pool.wait_ge(bias1, j + 1)
                pool.wait_ge(bias2, j + 1)
                pool.sem_inc(passed, 1)
                load_bias(job_value(pool, 0, j + 1, N_EXP - 1))
                pool.wait_ge(brow_landed, j * 48 + 96)
                for half in range(2):
                    pool.wait_ge(m_read[half], j * 4 + 6)
                pool.sem_inc(passed, 1)
                add_one(j + 2)
                pool.partition_broadcast(bias[:, 0:2 * D], brow[0:1, 0:2 * D]).then_inc(bias1, 1)
                for half in range(2):
                    pool.wait_ge(y_done[half], j * 2 + 4)
                    pool.sem_inc(passed, 1)
                    pool.indirect_dma_start(out=y_dram[:, :],
                                            out_offset=bass.IndirectOffsetOnAxis(ap=idc[:, half:half + 1], axis=0),
                                            in_=ys[:, half, :], in_offset=None,
                                            bounds_check=SEQ * TOP_K - 1, oob_is_err=False).then_inc(y_stored[half], 16)
                pool.partition_broadcast(bias[:, 2 * D:3 * D], brow[0:1, 2 * D:3 * D]).then_inc(bias2, 1)
                for half in range(2):
                    pool.wait_ge(y_stored[half], j * 16 + 16)
                pool.sem_inc(passed, 1)
                pool.tensor_copy(idc[:, :], idn[:, :, 0]).then_inc(idx_kept, 1)
            for half in range(2):
                pool.wait_ge(x_landed[half], n * 16 + 16)
                pool.wait_ge(idx_landed, n * 16 + 16)
            pool.sem_inc(passed, 1)

        @block.scalar
        def _(act):
            act.sem_inc(hi_done, 2 * RAW)

            def split(j, k):
                s, c = k % SPL, k // 2
                act.wait_ge(w_sem[c % RAW], j * 64 + 32 * (c // RAW + 1))
                act.wait_ge(w_used, j * NP + (k + 1))
                act.copy(whi[:, s, :, :], piece(k)).then_inc(hi_done, 1)

            def keep_hi(half, buf, k0, n, j, g, m=P):
                act.wait_ge(t_ready[half], j * 6 + (g + 3))
                act.copy(buf[:, half, k0:k0 + n, 0:m], t_ps[:, half, 0:n * P].rearrange("p (k m) -> p k m", m=P)[:, :, 0:m]
                         ).then_inc(t_hi[half], 1)

            def body(j, halves, few=False):
                size = (P, FEW if few else P)
                if few:
                    act.wait_ge(t_lo[1], j * 6 + 2)
                    act.copy(xt_hi[:, 1, :, FEW:P], xt_lo[:, 1, :, 0:FEW]).then_inc(packed, 1)
                for k in range(NP):
                    c = k // 2
                    if k == 2 and len(halves) == 1:
                        act.wait_ge(t_hi[1], j * 6 + 2)
                        act.sem_inc(sig_done[1], 4)
                        act.sem_inc(t_hi[1], 4)
                    if k % 2 == 0 and 1 <= c <= 4:
                        for half in halves:
                            if half == halves[-1]:
                                split(j, k + AHEAD)
                            act.wait_ge(m_read[half], j * 4 + (c + 2))
                            r = size[half]
                            act.activation(sg[0:r, :], gl[0:r, 0:256], ACT.Gelu_apprx_sigmoid).then_inc(sig_done[half], 1)
                    if k % 2 == 1 and 1 <= c <= 4:
                        for half in halves:
                            keep_hi(half, ht_hi, 2 * (c - 1), 2, j, c - 1, size[half])
                    if k >= 10:
                        for half in range(2):
                            keep_hi(half, xt_hi, 4 * (k - 10), 4, j, k - 6)
                    if not (k % 2 == 0 and 1 <= c <= 4):
                        split(j, k + AHEAD)

            for g in range(2):
                for half in range(2):
                    act.wait_ge(t_ready[half], g + 1)
                    act.copy(xt_hi[:, half, 4 * g:4 * g + 4, :], t_ps[:, half, :].rearrange("p (k m) -> p k m", m=P)
                             ).then_inc(t_hi[half], 1)
            for k in range(AHEAD):
                split(0, k)
            n = job_count(act)
            with act.Fori(0, n) as j:
                both = job_value(act, 2, j, 2)
                with act.If(both > 1):
                    body(j, (0, 1))
                with act.Else():
                    with act.If(both > 0):
                        body(j, (0, 1), few=True)
                    with act.Else():
                        body(j, (0,))

        @block.vector
        def _(dve):
            dve.sem_inc(lo_done, 2 * RAW)
            for half in range(2):
                dve.sem_inc(m_read[half], 2)
                dve.sem_inc(y_done[half], 2)

            def split(j, k):
                s = k % SPL
                dve.wait_ge(hi_done, j * NP + (2 * RAW + k + 1))
                dve.tensor_tensor(wlo[:, s, :, :], piece(k), whi[:, s, :, :].bitcast(F32), ALU.subtract).then_inc(lo_done, 1)

            def keep_lo(half, hi, lo, k0, n, j, g):
                dve.wait_ge(t_hi[half], j * 6 + (g + 3))
                dve.tensor_tensor(lo[:, half, k0:k0 + n, :], t_ps[:, half, 0:n * P].rearrange("p (k m) -> p k m", m=P),
                                  hi[:, half, k0:k0 + n, :].bitcast(F32), ALU.subtract).then_inc(t_lo[half], 1)

            def keep_lo_beside(k0, n, j, g):
                dve.wait_ge(t_hi[1], j * 6 + (g + 3))
                dve.tensor_tensor(ht_hi[:, 1, k0:k0 + n, FEW:P],
                                  t_ps[:, 1, 0:n * P].rearrange("p (k m) -> p k m", m=P)[:, :, 0:FEW],
                                  ht_hi[:, 1, k0:k0 + n, 0:FEW].bitcast(F32), ALU.subtract).then_inc(t_lo[1], 1)

            def products(j, k, half, halves):
                if half == halves[-1]:
                    dve.wait_ge(w_used, j * NP + (SPL + k + 1))
                else:
                    dve.wait_ge(a_ready, j * NC + {1: 1, 3: 2, 5: 3, 7: 4, 10: 5, 11: 6}[k])

            def sum_rows(j, n, out, src, b, done):
                dve.tensor_tensor(out, src[FEW:P], b, ALU.add).then_inc(summed, 1)
                dve.wait_ge(summed, j * 6 + (n + 1))
                dve.tensor_tensor(out, src[0:FEW], out, ALU.add).then_inc(done, 1)

            def swiglu(j, c, half, halves, at, few):
                r = FEW if few and half else P
                products(j, 2 * c + 1, half, halves)
                if c == 0:
                    dve.wait_ge(bias1, j + 1)
                if c >= 2:
                    dve.wait_ge(t_ready[half], j * 6 + (c + 1))
                if r == FEW:
                    sum_rows(j, c, gl[0:r, :], m_ps[:, M_BANK(c, 1), :], bias[0:r, 512 * c:512 * c + 512], m_read[1])
                else:
                    dve.tensor_tensor(gl[:, :], m_ps[:, M_BANK(c, half), :], bias[:, 512 * c:512 * c + 512], ALU.add
                                      ).then_inc(m_read[half], 1)
                dve.wait_ge(m_read[half], j * 4 + (c + 3))
                dve.tensor_scalar(gl[0:r, 256:512], gl[0:r, 256:512], LIMIT + 1.0, 1.0 - LIMIT, ALU.min, ALU.max).then_inc(dve_chain, 1)
                dve.wait_ge(dve_chain, at + 1)
                dve.wait_ge(sig_done[half], j * 4 + (c + 1))
                dve.scalar_tensor_tensor(out=hh[0:r, half, c % 2, :], in0=sg[0:r, :], scalar=GLU_LIMIT, in1=gl[0:r, 256:512],
                                         op0=ALU.min, op1=ALU.mult).then_inc(h_ready[half], 1)
                dve.wait_ge(h_ready[half], j * 4 + (c + 1))

            def finish(j, q, half, halves, few):
                products(j, 10 + q, half, halves)
                if q == 0:
                    dve.wait_ge(bias2, j + 1)
                    dve.wait_ge(idx_kept, j + 1)
                src = y_ps[:, q, :] if half == 0 else m_ps[:, 2 * q + 1, :]
                if few and half:
                    sum_rows(j, 4 + q, ys[0:FEW, 1, 512 * q:512 * q + 512], src,
                             bias[0:FEW, 2 * D + 512 * q:2 * D + 512 * q + 512], y_done[1])
                    return
                dve.tensor_tensor(ys[:, half, 512 * q:512 * q + 512], src, bias[:, 2 * D + 512 * q:2 * D + 512 * q + 512],
                                  ALU.add).then_inc(y_done[half], 1)

            def body(j, halves, few=False):
                if not few:
                    dve.sem_inc(packed, 1)
                    dve.sem_inc(summed, 6)
                for k in range(NP):
                    c = k // 2
                    if k == 2 and len(halves) == 1:
                        dve.wait_ge(t_lo[1], j * 6 + 2)
                        dve.wait_ge(y_done[1], j * 2 + 2)
                        for s, m in ((m_read, 4), (h_ready, 4), (t_lo, 4), (y_done, 2)):
                            dve.sem_inc(s[1], m)
                    if k % 2 == 0 and 1 <= c <= 4:
                        for half in halves:
                            swiglu(j, c - 1, half, halves, j * 8 + 2 * (c - 1) + half, few)
                        if len(halves) == 1:
                            dve.sem_inc(dve_chain, 1)
                    if k % 2 == 1 and 1 <= c <= 4:
                        for half in halves:
                            if few and half:
                                keep_lo_beside(2 * (c - 1), 2, j, c - 1)
                            else:
                                keep_lo(half, ht_hi, ht_lo, 2 * (c - 1), 2, j, c - 1)
                    if k >= 10:
                        for half in range(2):
                            keep_lo(half, xt_hi, xt_lo, 4 * (k - 10), 4, j, k - 6)
                    if k == 11:
                        for half in halves:
                            finish(j, 0, half, halves, few)
                    split(j, k + AHEAD)
                for half in halves:
                    finish(j, 1, half, halves, few)

            for g in range(2):
                for half in range(2):
                    dve.wait_ge(t_hi[half], g + 1)
                    dve.tensor_tensor(xt_lo[:, half, 4 * g:4 * g + 4, :], t_ps[:, half, :].rearrange("p (k m) -> p k m", m=P),
                                      xt_hi[:, half, 4 * g:4 * g + 4, :].bitcast(F32), ALU.subtract).then_inc(t_lo[half], 1)
            for k in range(AHEAD):
                split(0, k)
            n = job_count(dve)
            with dve.Fori(0, n) as j:
                both = job_value(dve, 2, j, 2)
                with dve.If(both > 1):
                    body(j, (0, 1))
                with dve.Else():
                    with dve.If(both > 0):
                        body(j, (0, 1), few=True)
                    with dve.Else():
                        body(j, (0,))

        @block.tensor
        def _(pe):
            pe.sem_inc(w_used, SPL)

            def transpose_x(half, g):
                for c in range(4):
                    k = 4 * g + c
                    ins = pe.transpose(t_ps[:, half, c * P:(c + 1) * P], xg[:, half, k * P:(k + 1) * P], ident[:, :])
                ins.then_inc(t_ready[half], 1)

            def transpose_h(j, c, half, few):
                r = FEW if few and half else P
                pe.wait_ge(h_ready[half], j * 4 + (c + 1))
                pe.wait_ge(t_lo[half], j * 6 + (c + 2))
                if r == FEW:
                    pe.sem_inc(passed, 1)
                for i in range(2):
                    ins = pe.transpose(t_ps[:, half, i * P:i * P + r], hh[0:r, half, c % 2, i * P:(i + 1) * P], ident[0:r, 0:r])
                ins.then_inc(t_ready[half], 1)

            def multiply(j, k, half, few):
                c, s = k // 2, k % SPL
                first = k < 8
                q = k % 2
                xh, xl = (xt_hi, xt_lo) if first else (ht_hi, ht_lo)
                if first:
                    bank = m_ps[:, M_BANK(c, half), :]
                else:
                    bank = y_ps[:, q, :] if half == 0 else m_ps[:, 2 * q + 1, :]
                if first and k % 2 == 0:
                    pe.wait_ge(m_read[half], j * 4 + (c + 1))
                    if half == 1 and k in (0, 2):
                        pe.wait_ge(y_done[1], j * 2 + 2)
                if k in (8, 9):
                    if half == 0:
                        pe.wait_ge(y_done[0], j * 2 + (q + 1))
                    else:
                        pe.wait_ge(m_read[1], j * 4 + (q + 5))
                need = {0: 1, 1: 2, 8: 4, 10: 6}.get(k)
                if need is not None:
                    pe.wait_ge(t_lo[half], j * 6 + need)
                if few and half and k == 0:
                    pe.wait_ge(packed, j + 1)
                n = 0
                for i in range(PK):
                    kc = PK * (k % 2 if first else (k - 8) // 2) + i
                    start = k % 2 == 0 if first else k in (8, 9)
                    stop = k % 2 == 1 if first else k in (10, 11)
                    if few and half:
                        parts = ((bank, xh[:, 1, kc, :], whi), (bank[0:FEW], xh[:, 1, kc, 0:FEW], wlo))
                        for o, x, w in (parts if i == 0 else parts[::-1]):
                            ins = pe.matmul(o, x, w[:, s, i, :], start=(start and i == 0 and w is whi),
                                            stop=(stop and i == PK - 1), skip_group_check=True)
                        continue
                    for x, w in ((xh, whi), (xh, wlo), (xl, whi)):
                        n += 1
                        ins = pe.matmul(bank, x[:, half, kc, :], w[:, s, i, :], start=(start and n == 1),
                                        stop=(stop and n == 3 * PK), skip_group_check=True)
                return ins

            def body(j, halves, few=False):
                for k in range(NP):
                    c = k // 2
                    pe.wait_ge(hi_done, j * NP + (2 * RAW + k + 1))
                    pe.wait_ge(lo_done, j * NP + (2 * RAW + k + 1))
                    if k == 2 and len(halves) == 1:
                        skip_b(j)
                    for half in halves:
                        ins = multiply(j, k, half, few)
                        if half != halves[-1] and k in (1, 3, 5, 7, 10, 11):
                            ins.then_inc(a_ready, 1)
                    ins.then_inc(w_used, 1)
                    if k % 2 == 0 and 1 <= c <= 4:
                        for half in halves:
                            transpose_h(j, c - 1, half, few)
                    if k in (9, 10):
                        for half in range(2):
                            if k == 9:
                                pe.wait_ge(x_landed[half], j * 16 + 32)
                                pe.wait_ge(t_lo[half], j * 6 + 6)
                            else:
                                pe.wait_ge(t_lo[half], j * 6 + 7)
                            transpose_x(half, k - 9)

            def skip_b(j):
                pe.wait_ge(t_lo[1], j * 6 + 2)
                pe.wait_ge(y_done[0], j * 2 + 2)
                pe.sem_inc(t_ready[1], 4)
                pe.sem_inc(a_ready, NC)

            pe.wait_ge(ident_landed, 16)
            for g in range(2):
                for half in range(2):
                    if g == 0:
                        pe.wait_ge(x_landed[half], 16)
                    else:
                        pe.wait_ge(t_lo[half], 1)
                    transpose_x(half, g)
            n = job_count(pe)
            with pe.Fori(0, n) as j:
                both = job_value(pe, 2, j, 2)
                with pe.If(both > 1):
                    body(j, (0, 1))
                with pe.Else():
                    with pe.If(both > 0):
                        body(j, (0, 1), few=True)
                    with pe.Else():
                        body(j, (0,))


def combine(nc, gates, h2_dram, y_dram, out):
    with ExitStack() as ctx:
        sb = lambda n, s, d=F32: ctx.enter_context(nc.sbuf_tensor(n, s, d))
        sem = lambda n: ctx.enter_context(nc.semaphore(n))
        yk = sb("yk", [P, 2, TOP_K * D])
        h2 = sb("h2_in", [P, 2, D])
        y_sem = [sem(f"yk_landed{i}") for i in range(2)]
        o_sem = [sem(f"out_stored{i}") for i in range(2)]
        added = sem("added")
        block = ctx.enter_context(nc.Block())

        @block.sync
        def _(sp):
            for t in range(NT):
                b = t % 2
                if t >= 2:
                    sp.wait_ge(added, TOP_K * (t - 1))
                    sp.wait_ge(o_sem[b], 16 * (t // 2))
                sp.dma_start(yk[:, b, :], y_dram[t * P * TOP_K:(t + 1) * P * TOP_K, :].rearrange("(p k) d -> p (k d)", k=TOP_K)
                             ).then_inc(y_sem[b], 16)
                sp.dma_start(h2[:, b, :], h2_dram[t * P:(t + 1) * P, :]).then_inc(y_sem[b], 16)

        @block.scalar
        def _(act):
            for t in range(NT):
                act.wait_ge(added, TOP_K * (t + 1))
                act.dma_start(out[0, t * P:(t + 1) * P, :], h2[:, t % 2, :]).then_inc(o_sem[t % 2], 16)
            for b in range(2):
                act.wait_ge(o_sem[b], 16 * (NT // 2))

        @block.vector
        def _(dve):
            for t in range(NT):
                b = t % 2
                dve.wait_ge(y_sem[b], 32 * (t // 2 + 1))
                for k in range(TOP_K):
                    if k:
                        dve.wait_ge(added, TOP_K * t + k)
                    dve.scalar_tensor_tensor(out=h2[:, b, :], in0=yk[:, b, k * D:(k + 1) * D], scalar=gates[:, t, k:k + 1],
                                             in1=h2[:, b, :], op0=ALU.mult, op1=ALU.add).then_inc(added, 1)


def build(nc, a, out):
    dram = lambda n, s, d=F32: nc.dram_tensor(n, s, d, kind="Internal").ap()
    qk_dram = dram("qk_dram", [2, R_W, KEYS])
    h2_dram, v_dram = dram("h2_dram", [SEQ, D]), dram("v_dram", [SEQ, D])
    y_dram = dram("y_dram", [SEQ * TOP_K, D])
    slot_dram = dram("slot_dram", [N_EXP * CAP, 2], U32)
    with nc.sbuf_tensor("gates", [P, NT, TOP_K], F32) as gates, nc.sbuf_tensor("jobs", [1, 4, NJ], I32) as jobs:
        with nc.sbuf_tensor("v_all", [P, NT + 1, 640], F32) as v_all:
            project(nc, a, v_all, qk_dram)
            with nc.sbuf_tensor("mixed", [P, NT, D], F32) as mixed, ExitStack() as ctx:
                stacks = DiffStacks(nc, ctx)
                attend_window(nc, a, v_all, mixed, qk_dram, stacks)
                weights = RouteWeights(nc, ctx)
                attend_diff(nc, a, v_all, mixed, qk_dram, stacks, weights)
                route(nc, a, mixed, gates, jobs, h2_dram, v_dram, slot_dram, weights)
        experts(nc, a, jobs, v_dram, slot_dram, y_dram)
        combine(nc, gates, h2_dram, y_dram, out)


def rope_table():
    pos = np.concatenate([np.arange(N_META, KEYS), np.arange(N_META)]).astype(np.float32)
    cols = []
    for d in (DH, DQ):
        inv = (np.float32(10000.0) ** (-np.arange(0, d, 2, dtype=np.float32) / np.float32(d))).astype(np.float32)
        ang = pos[:, None] * inv[None, :]
        cols += [np.cos(ang), np.sin(ang)]
    return np.concatenate(cols, 1).astype(np.float32)


def band_masks():
    q, k = np.arange(P)[:, None], np.arange(P)[None, :]
    prev, nxt = np.where(k >= q, 0.0, NEG), np.where(k <= q, 0.0, NEG)
    m = np.zeros((P, 3, 3 * P + N_META), np.float32)
    m[:, 0, P:2 * P] = nxt
    m[:, 1, 0:P], m[:, 1, 2 * P:3 * P] = prev, nxt
    m[:, 2, 0:P] = prev
    return m


def constants():
    c = np.zeros((P, C_W), np.float32)
    i = np.arange(P)
    c[:, C_ID:C_ID + P] = np.eye(P)
    c[:, C_TRI:C_TRI + P] = i[:, None] < i[None, :]
    c[:, C_EXP:C_EXP + N_EXP] = np.arange(N_EXP)
    c[:, C_BASE:C_BASE + N_EXP] = np.arange(N_EXP) * CAP
    c[:, C_JOB:C_JOB + NJ] = np.arange(NJ)
    c[:, C_STEP:C_STEP + 4] = np.arange(4) * JOB
    return c


_INS = ["x", "meta_tokens", "g_attn", "w_in", "g_q_swa", "g_k_swa", "g_q_diff", "g_k_diff", "sink_swa",
        "lambda_q1", "lambda_k1", "lambda_q2", "lambda_k2", "g_diff_head", "w_out", "g_ffn",
        "w_router", "b_router", "w_mlp1", "b_mlp1", "w_mlp2", "b_mlp2"]


def kernel(**inputs):
    import concourse.bacc as bacc
    from concourse.bass_utils import run_bass_kernel_spmd

    nc = bacc.Bacc("TRN2", target_bir_lowering=False, num_devices=1)
    arrays = {f"in_{n}": np.ascontiguousarray(inputs[n]) for n in _INS}
    arrays |= {"in_rope": rope_table(), "in_masks": band_masks(), "in_consts": constants(),
               "in_ones": np.ones((P, P), np.float32)}
    aps = {n[3:]: nc.dram_tensor(n, v.shape, mybir.dt.from_np(v.dtype), kind="ExternalInput").ap()
           for n, v in arrays.items()}
    out = nc.dram_tensor("out_h", (1, SEQ, D), F32, kind="ExternalOutput").ap()
    build(nc, aps, out)
    r = run_bass_kernel_spmd(nc, [arrays], core_ids=[0])
    return r.results[0]["out_h"]
```
